# Optimizing a Trainium2 kernel written in Bass

```python
import jax, jax.numpy as jnp
from jax import lax
import numpy as np

D_MODEL = 1024
BATCH = 1
SEQ = 512
DEPTH = 1
DEC_BATCH = 1
DEC_SEQ = 1024
PAST_LEN = 128

GRID_W = 64
D_FOURIER = D_MODEL // 2
N_FGROUPS = 4
FG_DIM = D_FOURIER // N_FGROUPS
D_NA = D_MODEL - D_FOURIER
N_HEADS = 8
HEAD_DIM = D_NA // N_HEADS
MAX_WIN_ROWS = 8
WIN_COLS = 16
RPB_ROWS = 2 * MAX_WIN_ROWS - 1
RPB_COLS = 2 * WIN_COLS - 1
D_IN = D_FOURIER + 3 * D_NA
D_FF = -(-8 * D_MODEL // (3 * 256)) * 256
N_MOD = 6
EPS = 1e-6

kernel_name = "hymba_fnet_natten_encoder"

def rmsnorm(x, g):
    xf = x.astype(jnp.float32)
    y = xf * lax.rsqrt(jnp.mean(xf * xf, axis=-1, keepdims=True) + EPS)
    return (y * g.astype(jnp.float32)).astype(x.dtype)

def fourier_mix(u, w_fmix):
    b, t, _ = u.shape
    ug = u.reshape(b, t, N_FGROUPS, FG_DIM).astype(jnp.float32)
    f = jnp.fft.fft2(ug, axes=(1, 3), norm="ortho").real.astype(u.dtype)
    out = jnp.einsum('btgc,gcd->btgd', f, w_fmix)
    return out.reshape(b, t, D_FOURIER)

def neighbourhood_attention(q, k, v, rpb):
    b, t, h, dh = q.shape
    rows = t // GRID_W
    kh = min(MAX_WIN_ROWS, rows)
    q5 = q.reshape(b, rows, GRID_W, h, dh)
    k5 = k.reshape(b, rows, GRID_W, h, dh)
    v5 = v.reshape(b, rows, GRID_W, h, dh)
    cols = np.arange(GRID_W)
    col_start = np.clip(cols - WIN_COLS // 2, 0, GRID_W - WIN_COLS)
    col_idx = col_start[:, None] + np.arange(WIN_COLS)[None, :]
    dc = col_idx - cols[:, None] + (WIN_COLS - 1)
    scale = HEAD_DIM ** -0.5

    def row_step(args):
        qi, i = args
        rs = jnp.clip(i - kh // 2, 0, rows - kh)
        kwin = lax.dynamic_slice_in_dim(k5, rs, kh, axis=1)
        vwin = lax.dynamic_slice_in_dim(v5, rs, kh, axis=1)
        kc = kwin[:, :, col_idx]
        vc = vwin[:, :, col_idx]
        dr = rs + jnp.arange(kh) - i + (MAX_WIN_ROWS - 1)
        bias = rpb[:, dr[None, :, None], dc[:, None, :]]
        bias = jnp.transpose(bias, (1, 0, 2, 3)).astype(jnp.float32)
        s = jnp.einsum('bqhd,brqkhd->bqhrk', qi, kc,
                       preferred_element_type=jnp.float32) * scale + bias[None]
        p = jax.nn.softmax(s.reshape(b, GRID_W, h, kh * WIN_COLS), axis=-1)
        p = p.reshape(b, GRID_W, h, kh, WIN_COLS).astype(v.dtype)
        return jnp.einsum('bqhrk,brqkhd->bqhd', p, vc)

    out = lax.map(row_step, (jnp.transpose(q5, (1, 0, 2, 3, 4)), jnp.arange(rows)))
    return jnp.transpose(out, (1, 0, 2, 3, 4)).reshape(b, t, h * dh)

def encoder_layer(x, c, w_ada, b_ada, g_attn, w_in, g_q, g_k, w_fmix, rpb,
                  g_fout, g_aout, w_o, g_ffn, w_gate, w_up, w_down):
    b, t, _ = x.shape
    mod = (jax.nn.silu(c) @ w_ada + b_ada)[:, None, :]
    shift1, scale1, gate1, shift2, scale2, gate2 = jnp.split(mod, N_MOD, axis=-1)

    h = rmsnorm(x, g_attn) * (1 + scale1) + shift1
    z = h @ w_in
    u, q, k, v = jnp.split(z, [D_FOURIER, D_FOURIER + D_NA, D_FOURIER + 2 * D_NA], axis=-1)
    q = rmsnorm(q.reshape(b, t, N_HEADS, HEAD_DIM), g_q)
    k = rmsnorm(k.reshape(b, t, N_HEADS, HEAD_DIM), g_k)
    v = v.reshape(b, t, N_HEADS, HEAD_DIM)
    f_out = fourier_mix(u, w_fmix)
    a_out = neighbourhood_attention(q, k, v, rpb)
    mix = jnp.concatenate([rmsnorm(f_out, g_fout), rmsnorm(a_out, g_aout)], axis=-1) @ w_o
    x = x + gate1 * mix

    h2 = rmsnorm(x, g_ffn) * (1 + scale2) + shift2
    ff = (jax.nn.silu(h2 @ w_gate) * (h2 @ w_up)) @ w_down
    return x + gate2 * ff

def setup_inputs(seed: int = 0) -> dict:
    key = jax.random.key(seed)
    ks = jax.random.split(key, 20)
    f32 = jnp.float32
    nrm = lambda k, shape, s: jax.random.normal(k, shape, f32) * s
    gain = lambda k, shape: 1.0 + 0.01 * jax.random.normal(k, shape, f32)
    L = DEPTH
    return {
        "x_prompt": nrm(ks[0], (BATCH, SEQ, D_MODEL), 1.0),
        "x_sample": nrm(ks[1], (DEC_BATCH, DEC_SEQ, D_MODEL), 1.0),
        "c_prompt": nrm(ks[2], (BATCH, D_MODEL), 1.0),
        "c_sample": nrm(ks[3], (DEC_BATCH, D_MODEL), 1.0),
        "w_ada": nrm(ks[4], (L, D_MODEL, N_MOD * D_MODEL), D_MODEL ** -0.5),
        "b_ada": nrm(ks[5], (L, N_MOD * D_MODEL), 0.01),
        "g_attn": gain(ks[6], (L, D_MODEL)),
        "w_in": nrm(ks[7], (L, D_MODEL, D_IN), D_MODEL ** -0.5),
        "g_q": gain(ks[8], (L, HEAD_DIM)),
        "g_k": gain(ks[9], (L, HEAD_DIM)),
        "w_fmix": nrm(ks[10], (L, N_FGROUPS, FG_DIM, FG_DIM), FG_DIM ** -0.5),
        "rpb": nrm(ks[11], (L, N_HEADS, RPB_ROWS, RPB_COLS), 0.02),
        "g_fout": gain(ks[12], (L, D_FOURIER)),
        "g_aout": gain(ks[13], (L, D_NA)),
        "w_o": nrm(ks[14], (L, D_MODEL, D_MODEL), D_MODEL ** -0.5),
        "g_ffn": gain(ks[15], (L, D_MODEL)),
        "w_gate": nrm(ks[16], (L, D_MODEL, D_FF), D_MODEL ** -0.5),
        "w_up": nrm(ks[17], (L, D_MODEL, D_FF), D_MODEL ** -0.5),
        "w_down": nrm(ks[18], (L, D_FF, D_MODEL), D_FF ** -0.5),
    }

def reference(x_prompt, x_sample, c_prompt, c_sample, w_ada, b_ada, g_attn, w_in, g_q, g_k,
              w_fmix, rpb, g_fout, g_aout, w_o, g_ffn, w_gate, w_up, w_down):
    def trunk(x, c):
        for l in range(DEPTH):
            x = encoder_layer(x, c, w_ada[l], b_ada[l], g_attn[l], w_in[l], g_q[l], g_k[l],
                              w_fmix[l], rpb[l], g_fout[l], g_aout[l], w_o[l], g_ffn[l],
                              w_gate[l], w_up[l], w_down[l])
        return x

    y_prompt = trunk(x_prompt, c_prompt)
    y_sample = trunk(x_sample, c_sample)
    return (y_prompt, y_sample)


_drawn_inputs = setup_inputs


def setup_inputs(seed=0):
    import zlib

    import numpy as np

    out = dict(_drawn_inputs(seed))
    spreads = {}
    factors = {'b_ada': 3.492,
     'g_attn': 8.0,
     'g_q': 8.0,
     'g_k': 8.0,
     'rpb': 23.711,
     'g_fout': 47.047,
     'g_aout': 46.607,
     'g_ffn': 32.998}
    for name, (base, spread) in spreads.items():
        noise = np.random.default_rng([zlib.crc32(name.encode()), seed]).standard_normal(out[name].shape)
        drawn = base * np.exp(spread * noise) if base else spread * noise
        out[name] = __import__('jax').numpy.asarray(drawn.astype(out[name].dtype))
    for name, factor in factors.items():
        out[name] = (out[name] * factor).astype(out[name].dtype)
    return out
```

```python
import numpy as np
from contextlib import ExitStack

import concourse.bass as bass
from concourse import mybir

F32, F32R = mybir.dt.float32, mybir.dt.float32r
ALU = mybir.AluOpType
ACT = mybir.ActivationFunctionType
AX = mybir.AxisListType

D = 1024
KT = D // 128
T_PROMPT, T_SAMPLE = 512, 1024
T = T_PROMPT + T_SAMPLE
CH = 512
NCH = T // CH
TT = T // 128
REQ = [0, 1, 1]
D_FOURIER = D // 2
FT = D_FOURIER // 128
HEAD = 64
N_HEADS = D_FOURIER // HEAD
D_FF = 2816
FF = D_FF // 128
GRID_W = 64
WIN_ROWS, WIN_COLS = 8, 16
N_MOD = 6
EPS = 1e-6

QROWS, QCOLS, KCOLS = 8, 16, 32
NB = GRID_W // QCOLS
KEY_COL = [min(max(QCOLS * b - WIN_COLS // 2, 0), GRID_W - KCOLS) for b in range(NB)]
KEY_ROWS = [8, 12, 12]
KEY_ROW0 = [0, 0, 4]
KEY_TOKEN0 = [0, T_PROMPT, T_PROMPT + 4 * GRID_W]
V_TILE0 = [0, 2, 3]
NVT = 6
BIAS_E, BIAS_X = 16, 48
RP_ROWS, RP_COLS = 23, 63
MASKED = 1e30
MASK_COLS = sum(KEY_ROWS) * KCOLS
UNITS = NB * NCH * 2

BASE = 16512
H_HI, H_LO = BASE, BASE + 49152
X_AT = BASE + 98304
GATE2_AT = BASE + 147456
REST = BASE + 155648
KEEP = BASE + 210176
END = BASE + 212832


def layer(nc, x_prompt, x_sample, c_rows, w_ada, vec_rows, w_in, w_fmix, rpb_pad, masks, dft_c, dft_t1,
          dft_t0, w_o, w_gate, w_up, w_down, u_scratch, y_prompt, y_sample):
    ctx = ExitStack()
    with ctx:
        def at(name, shape, dt, off):
            size = 4 * int(np.prod(shape[1:]))
            assert off % 32 == 0 and off >= BASE and off + size <= END, (name, off - BASE, size)
            made[name] = nc.alloc_sbuf_tensor_at(name, shape, dt, offset=off)
            return made[name]
        made = {}

        def sem(name):
            return ctx.enter_context(nc.semaphore(name))

        banks = ctx.enter_context(nc.psum_tensor("banks", [128, 8, 512], F32))

        ident = at("ident", [128, 128], F32, KEEP)
        ones_head = at("ones_head", [128, 128], F32R, KEEP + 512)
        ones_all = at("ones_all", [128, 128], F32R, KEEP + 1024)
        vec = at("vec", [128, 96], F32, KEEP + 1536)
        mod = at("mod", [128, N_MOD * KT, 2], F32, KEEP + 1920)
        coef = at("coef", [128, 2, KT, 2], F32, KEEP + 2304)
        stat = at("stat", [128, 2, TT], F32, KEEP + 2432)
        eps_t = at("eps_t", [128, 1], F32, KEEP + 2528)
        gq8 = at("gq8", [128, 1], F32, KEEP + 2560)
        V_C, V_GATTN, V_GFFN, V_GF, V_GA, V_GQ, V_GK, V_BADA = 0, 16, 24, 32, 36, 40, 41, 42

        h_hi = at("h_hi", [128, KT, T], F32R, H_HI)
        h_lo = at("h_lo", [128, KT, T], F32R, H_LO)

        def mm3(pe, out, lhs, rhs, start, stop):
            pe.matmul(out, lhs[0], rhs[0], start=start, stop=False)
            pe.matmul(out, lhs[0], rhs[1], start=False, stop=False)
            return pe.matmul(out, lhs[1], rhs[0], start=False, stop=stop)

        first_stage(nc, at, sem, banks, locals())
        projections(nc, at, sem, banks, locals())
        attention(nc, at, sem, banks, locals())
        fourier(nc, at, sem, banks, locals())
        mix_norm(nc, at, sem, banks, locals())
        out_projection(nc, at, sem, banks, locals())
        feed_forward(nc, at, sem, banks, locals())


def first_stage(nc, at, sem, banks, g):
    x_prompt, x_sample, c_rows, w_ada, vec_rows = (g[k] for k in ("x_prompt", "x_sample", "c_rows", "w_ada", "vec_rows"))
    ident, ones_head, ones_all, vec, mod, coef, stat, eps_t, gq8, h_hi, h_lo = (
        g[k] for k in ("ident", "ones_head", "ones_all", "vec", "mod", "coef", "stat", "eps_t", "gq8", "h_hi", "h_lo"))
    V_C, V_BADA, V_GQ = g["V_C"], g["V_BADA"], g["V_GQ"]
    NV = V_BADA + N_MOD * KT
    AC = 12
    x = at("x_first", [128, TT, D], F32, X_AT)
    ada = at("ada", [128, 3, KT, 512], F32, REST)
    mrow = at("mrow", [128, 2, 512], F32, GATE2_AT)
    junk = at("junk", [128, D], F32, GATE2_AT + 4096)
    t_ring = at("t_first", [128, 2, CH], F32, REST + 49152)
    vrow = at("vrow", [128, 128], F32, REST + 53248)
    silu_c = at("silu_c", [128, 16], F32, KEEP + 2592)

    x_in = [sem(f"x_in{c}") for c in range(NCH)]
    vec_in, ada_in = sem("vec_in"), [sem(f"ada_in{i}") for i in range(3)]
    ident_zero, ident_ready, ones_ready = sem("ident_zero"), sem("ident_ready"), sem("ones_ready")
    vec_turned, vec_ready, silu_ready = sem("vec_turned"), sem("vec_ready"), sem("silu_ready")
    mod_summed, mod_row, mod_turned = sem("mod_summed"), sem("mod_row"), sem("mod_turned")
    mod_ready, coef_ready = sem("mod_ready"), sem("coef_ready")
    squared, rooted, rstd_ready, x_normed = sem("squared"), sem("rooted"), sem("rstd_ready"), sem("x_normed")
    x_turned, t_ready, h_split = sem("x_turned"), sem("t_ready"), sem("h_split")
    h_hi_ready = sem("h_hi_ready")

    with nc.Block() as block:
        @block.sync
        def _(sp):
            sp.dma_start(vrow[0:NV, :], vec_rows).then_inc(vec_in, 16)
            for j in range(AC):
                if j >= 3:
                    sp.wait_ge(mod_summed, j - 2)
                sp.dma_start(ada[:, j % 3], w_ada[:, 512 * j:512 * j + 512].rearrange("(k p) n -> p k n", p=128)
                             ).then_inc(ada_in[j % 3], 16)

        @block.gpsimd
        def _(pool):
            pool.memset(ident[:], 0.0).then_inc(ident_zero, 1)
            pool.wait_ge(ident_zero, 1)
            pool.affine_select(out=ident[:], in_=ident[:], compare_op=ALU.not_equal, fill=1.0, base=0,
                               pattern=[[-1, 128]], channel_multiplier=1).then_inc(ident_ready, 1)

        @block.scalar
        def _(act):
            for c in range(NCH):
                src = x_prompt if c == 0 else x_sample[CH * (c - 1):CH * c]
                act.dma_start(x[:, 4 * c:4 * c + 4], src.rearrange("(t p) n -> p t n", p=128)).then_inc(x_in[c], 16)
            act.wait_ge(vec_turned, 1)
            act.activation(silu_c[:], banks[:, 2, V_C:V_C + 16], ACT.Silu).then_inc(silu_ready, 1)
            act.wait_ge(ones_ready, 1)
            for c in range(NCH):
                act.wait_ge(x_in[c], 16)
                for t in range(4 * c, 4 * c + 4):
                    if t:
                        act.wait_ge(squared, t)
                    act.activation(junk[:], x[:, t], ACT.Square, accum_out=stat[:, 0, t:t + 1]).then_inc(squared, 1)
                act.wait_ge(squared, 4 * c + 4)
                act.activation(stat[:, 0, 4 * c:4 * c + 4], stat[:, 0, 4 * c:4 * c + 4], ACT.Sqrt,
                               scale=1.0 / D, bias=eps_t[:]).then_inc(rooted, 1)
            act.wait_ge(coef_ready, 1)
            for n in range(NCH * KT):
                c, k = divmod(n, KT)
                act.wait_ge(x_turned, n + 1)
                if n >= 2:
                    act.wait_ge(h_split, n - 1)
                act.activation(t_ring[:, n % 2], banks[:, 4 + n % 4], ACT.Identity, scale=coef[:, 0, k, REQ[c]:REQ[c] + 1],
                               bias=mod[:, k, REQ[c]:REQ[c] + 1]).then_inc(t_ready, 1)

        @block.vector
        def _(dve):
            dve.memset(ones_head[:].bitcast(F32), 0.0).then_inc(mod_row, 1)
            dve.wait_ge(mod_row, 1)
            dve.memset(ones_head[0:64, 0:64].bitcast(F32), 1.0)
            dve.memset(ones_head[64:128, 64:128].bitcast(F32), 1.0)
            dve.memset(ones_all[:].bitcast(F32), 1.0)
            dve.memset(eps_t[:], EPS).then_inc(ones_ready, 1)
            dve.wait_ge(vec_turned, 1)
            dve.wait_ge(silu_ready, 1)
            dve.tensor_copy(vec[:, 0:NV], banks[:, 2, 0:NV]).then_inc(vec_ready, 1)
            dve.wait_ge(vec_ready, 1)
            dve.tensor_scalar(gq8[:], vec[:, V_GQ:V_GQ + 1], -float(HEAD) ** -0.5, None, ALU.mult).then_inc(vec_ready, 1)

            def norm_rows(c):
                dve.wait_ge(rooted, c + 1)
                dve.reciprocal(stat[:, 1, 4 * c:4 * c + 4], stat[:, 0, 4 * c:4 * c + 4]).then_inc(rstd_ready, 1)
                dve.wait_ge(rstd_ready, c + 1)
                for t in range(4 * c, 4 * c + 4):
                    dve.tensor_scalar(x[:, t], x[:, t], stat[:, 1, t:t + 1], None, ALU.mult).then_inc(x_normed, 1)

            def mod_part(a, b, n):
                dve.tensor_tensor(mod[:, a:b], banks[:, 3, 2 * a:2 * b].rearrange("p (j r) -> p j r", r=2),
                                  bass.AP(vec, V_BADA + a, [[96, 128], [1, b - a], [0, 2]]), ALU.add).then_inc(mod_ready, 1)
                dve.wait_ge(mod_ready, n)

            def gains(which, tile0, gain0, n):
                gain = bass.AP(vec, gain0, [[96, 128], [1, KT], [0, 2]])
                dve.scalar_tensor_tensor(coef[:, which], mod[:, tile0:tile0 + KT], 1.0, gain, ALU.add, ALU.mult
                                         ).then_inc(coef_ready, 1)

            for j in range(AC):
                dve.wait_ge(mod_summed, j + 1)
                if j >= 2:
                    dve.wait_ge(mod_turned, j - 1)
                dve.tensor_copy(mrow[0:2, j % 2], banks[0:2, j % 2]).then_inc(mod_row, 1)
                if j < NCH:
                    norm_rows(j)
                if j == 4:
                    dve.wait_ge(mod_turned, 4)
                    mod_part(0, 16, 1)
                    gains(0, 8, g["V_GATTN"], 1)
            dve.wait_ge(mod_turned, AC)
            mod_part(16, 48, 2)
            gains(1, 32, g["V_GFFN"], 2)
            for n in range(NCH * KT):
                c, k = divmod(n, KT)
                dve.wait_ge(t_ready, n + 1)
                hi, lo = (h[:, k, CH * c:CH * c + CH] for h in (h_hi, h_lo))
                dve.tensor_copy(hi, t_ring[:, n % 2]).then_inc(h_hi_ready, 1)
                dve.wait_ge(h_hi_ready, n + 1)
                dve.tensor_tensor(lo, t_ring[:, n % 2], hi.bitcast(F32), ALU.subtract).then_inc(h_split, 1)

        @block.tensor
        def _(pe):
            pe.wait_ge(ident_ready, 1)
            pe.wait_ge(vec_in, 16)
            pe.transpose(banks[:, 2, 0:NV], vrow[0:NV, :], ident[0:NV, 0:NV]).then_inc(vec_turned, 1)
            pe.wait_ge(silu_ready, 1)

            def turn_mod(j):
                pe.wait_ge(mod_row, j + 2)
                for i in range(4):
                    a = 8 * j + 2 * i
                    last = pe.transpose(banks[:, 3, a:a + 2], mrow[0:2, j % 2, 128 * i:128 * i + 128], ident[0:2, 0:2])
                last.then_inc(mod_turned, 1)

            for j in range(AC):
                pe.wait_ge(ada_in[j % 3], 16 * (j // 3 + 1))
                if j >= 2:
                    pe.wait_ge(mod_row, j)
                for k in range(KT):
                    last = pe.matmul(banks[0:2, j % 2], silu_c[:, V_C + k:V_C + k + 9:8], ada[:, j % 3, k],
                                     start=(k == 0), stop=(k == KT - 1))
                last.then_inc(mod_summed, 1)
                if j >= 1:
                    if j == 5:
                        pe.wait_ge(mod_ready, 1)
                    turn_mod(j - 1)
            turn_mod(AC - 1)
            for n in range(NCH * KT):
                c, k = divmod(n, KT)
                pe.wait_ge(x_normed, 4 * c + 4)
                if n >= 4:
                    pe.wait_ge(t_ready, n - 3)
                for i in range(4):
                    last = pe.transpose(banks[:, 4 + n % 4, 128 * i:128 * i + 128],
                                        x[:, 4 * c + i, 128 * k:128 * k + 128], ident[:])
                last.then_inc(x_turned, 1)


def projections(nc, at, sem, banks, g):
    w_in, u_scratch, h_hi, h_lo, vec, gq8, ones_head, eps_t, mm3 = (
        g[k] for k in ("w_in", "u_scratch", "h_hi", "h_lo", "vec", "gq8", "ones_head", "eps_t", "mm3"))
    V_GK = g["V_GK"]
    z = at("z", [128, 3 * FT * T], F32, X_AT)
    W = X_AT + 73728
    w_hi = at("win_hi", [128, 2, KT, 128], F32R, W)
    w_lo = at("win_lo", [128, 2, KT, 128], F32R, W + 8192)
    w_raw = at("win_raw", [128, 2, KT, 128], F32, W + 8192)
    u_stage = at("u_stage", [128, 2, CH], F32, W + 16384)
    sq = at("sq", [128, 2, CH], F32, W + 20480)
    sq_hi = at("sq_hi", [128, 2, CH], F32R, W + 24576)
    sq_lo = at("sq_lo", [128, 2, CH], F32R, W + 28672)
    rms = at("rms", [128, 2, CH], F32, W + 32768)

    w_in_s = [sem(f"win_in{s}") for s in range(2)]
    w_hi_s = [sem(f"win_hi_ready{s}") for s in range(2)]
    w_ready = [sem(f"win_ready{s}") for s in range(2)]
    z_summed = [sem(f"z_summed{b}") for b in range(6)]
    bank_free = [sem(f"z_bank_free{b}") for b in range(6)]
    u_stored = [sem(f"u_stored{s}") for s in range(2)]
    sq_hi_s, sq_lo_s = sem("sq_hi_s"), sem("sq_lo_s")
    ss_summed, rms_ready, rinv_ready, qk_normed = sem("ss_summed"), sem("rms_ready"), sem("rinv_ready"), sem("qk_normed")
    J_U, J_QK, J_V = FT // 2, 3 * FT // 2, 2 * FT

    with nc.Block() as block:
        @block.sync
        def _(sp):
            def load(j, s):
                sp.dma_start(w_raw[:, s], w_in[:, bass.ds((2 * j + s) * 128, 128)].rearrange("(k p) n -> p k n", p=128)
                             ).then_inc(w_in_s[s], 16)
            load(0, 0)
            load(0, 1)
            with sp.Fori(1, J_V) as j:
                for s in range(2):
                    sp.wait_ge(z_summed[3 * s + 2], j)
                    load(j, s)

        @block.gpsimd
        def _(pool):
            with pool.Fori(0, J_U) as j:
                for i in range(6):
                    s, c = divmod(i, NCH)
                    pool.wait_ge(bank_free[i], j + 1)
                    pool.dma_start(u_scratch[bass.ds((2 * j + s) * 128, 128), CH * c:CH * c + CH],
                                   u_stage[:, i % 2]).then_inc(u_stored[i % 2], 16)
            with pool.Fori(0, J_QK - J_U) as j:
                for i in range(6):
                    n = 6 * j + i
                    pool.wait_ge(sq_hi_s, n + 1)
                    if i >= 2:
                        pool.wait_ge(ss_summed, n - 1)
                    else:
                        pool.wait_ge(ss_summed, 6 * j)
                    pool.tensor_tensor(sq_lo[:, i % 2], sq[:, i % 2], sq_hi[:, i % 2].bitcast(F32), ALU.subtract
                                       ).then_inc(sq_lo_s, 1)
            for s in range(2):
                pool.wait_ge(u_stored[s], 16 * 3 * J_U)

        def split_hi(act, j, s):
            act.wait_ge(w_in_s[s], 16 * j + 16)
            act.activation(w_hi[:, s], w_raw[:, s], ACT.Copy).then_inc(w_hi_s[s], 1)

        def split_lo(dve, j, s):
            dve.wait_ge(w_hi_s[s], j + 1)
            dve.tensor_tensor(w_lo[:, s], w_raw[:, s], w_hi[:, s].bitcast(F32), ALU.subtract).then_inc(w_ready[s], 1)

        def z_at(j, s, c):
            return z[:, bass.ds(((2 * (j - J_U) + s) * NCH + c) * CH, CH)]

        @block.scalar
        def _(act):
            def evacuate(j, i, kind):
                s, c = divmod(i, NCH)
                act.wait_ge(z_summed[i], j + 1)
                if kind == "u":
                    act.wait_ge(u_stored[i % 2], 16 * (3 * j + i // 2))
                    act.activation(u_stage[:, i % 2], banks[:, i], ACT.Copy).then_inc(bank_free[i], 1)
                elif kind == "v":
                    act.activation(z_at(j, s, c), banks[:, i], ACT.Copy).then_inc(bank_free[i], 1)
                else:
                    n = 6 * (j - J_U) + i
                    act.activation(z_at(j, s, c), banks[:, i], ACT.Copy)
                    if i >= 2:
                        act.wait_ge(sq_lo_s, n - 1)
                    else:
                        act.wait_ge(sq_lo_s, 6 * (j - J_U))
                    act.activation(sq[:, i % 2], banks[:, i], ACT.Square).then_inc(bank_free[i], 1)

            def root(j, i):
                n = 6 * (j - J_U) + i
                act.wait_ge(ss_summed, n + 1)
                if i >= 2:
                    act.wait_ge(qk_normed, n - 1)
                else:
                    act.wait_ge(qk_normed, 6 * (j - J_U))
                act.activation(rms[:, i % 2], banks[:, 6 + i % 2], ACT.Sqrt, scale=1.0 / HEAD, bias=eps_t[:]
                               ).then_inc(rms_ready, 1)

            def pair(j, kind, more):
                for i in range(6):
                    evacuate(j, i, kind)
                    if kind == "qk" and i:
                        root(j, i - 1)
                    if i % 3 == 2 and more:
                        split_hi(act, j + 1, i // 3)
                if kind == "qk":
                    root(j, 5)
            split_hi(act, 0, 0)
            split_hi(act, 0, 1)
            with act.Fori(0, J_U) as j:
                pair(j, "u", True)
            with act.Fori(J_U, J_QK) as j:
                pair(j, "qk", True)
            with act.Fori(J_QK, J_V - 1) as j:
                pair(j, "v", True)
            pair(J_V - 1, "v", False)

        @block.vector
        def _(dve):
            def sq_split(j, i):
                n = 6 * (j - J_U) + i
                dve.wait_ge(bank_free[i], j + 1)
                dve.wait_ge(ss_summed, n - 1 if i >= 2 else 6 * (j - J_U))
                dve.tensor_copy(sq_hi[:, i % 2], sq[:, i % 2]).then_inc(sq_hi_s, 1)

            def qk_norm(j, i, gain):
                s, c = divmod(i, NCH)
                n = 6 * (j - J_U) + i
                dve.wait_ge(rms_ready, n + 1)
                dve.reciprocal(rms[:, i % 2], rms[:, i % 2]).then_inc(rinv_ready, 1)
                dve.wait_ge(rinv_ready, n + 1)
                zz = z_at(j, s, c)
                dve.scalar_tensor_tensor(zz, zz, gain, rms[:, i % 2], ALU.mult, ALU.mult).then_inc(qk_normed, 1)

            def splits(j, i):
                if i % 3 == 2:
                    split_lo(dve, j + 1, i // 3)
            split_lo(dve, 0, 0)
            split_lo(dve, 0, 1)
            with dve.Fori(0, J_U) as j:
                for i in range(6):
                    splits(j, i)
            for a, b, gain in ((J_U, J_U + FT // 2, gq8[:]), (J_U + FT // 2, J_QK, vec[:, V_GK:V_GK + 1])):
                with dve.Fori(a, b) as j:
                    for i in range(6):
                        sq_split(j, i)
                        if i:
                            qk_norm(j, i - 1, gain)
                        splits(j, i)
                    qk_norm(j, 5, gain)
            with dve.Fori(J_QK, J_V - 1) as j:
                for i in range(6):
                    splits(j, i)

        @block.tensor
        def _(pe):
            def tile(j, i):
                s, c = divmod(i, NCH)
                if c == 0:
                    pe.wait_ge(w_ready[s], j + 1)
                pe.wait_ge(bank_free[i], j)
                for k in range(KT):
                    last = mm3(pe, banks[:, i], (w_hi[:, s, k], w_lo[:, s, k]),
                               (h_hi[:, k, CH * c:CH * c + CH], h_lo[:, k, CH * c:CH * c + CH]), k == 0, k == KT - 1)
                last.then_inc(z_summed[i], 1)

            def head_sums(j, i):
                n = 6 * (j - J_U) + i
                pe.wait_ge(sq_lo_s, n + 1)
                pe.wait_ge(rms_ready, n - 1 if i >= 2 else 6 * (j - J_U))
                pe.matmul(banks[:, 6 + i % 2], ones_head[:], sq_hi[:, i % 2], start=True, stop=False)
                pe.matmul(banks[:, 6 + i % 2], ones_head[:], sq_lo[:, i % 2], start=False, stop=True
                          ).then_inc(ss_summed, 1)

            def tiles(j, i, qk):
                tile(j, i)
                if qk and i:
                    head_sums(j, i - 1)
            with pe.Fori(0, J_U) as j:
                for i in range(6):
                    tiles(j, i, False)
            with pe.Fori(J_U, J_QK) as j:
                for i in range(6):
                    tiles(j, i, True)
                head_sums(j, 5)
            with pe.Fori(J_QK, J_V) as j:
                for i in range(6):
                    tiles(j, i, False)


def attention(nc, at, sem, banks, g):
    z, rpb_pad, masks, ident = g["made"]["z"], g["rpb_pad"], g["masks"], g["ident"]
    bias = at("bias", [128, N_HEADS * BIAS_E * BIAS_X], F32, BASE)
    mask = at("mask", [128, NB * MASK_COLS], F32, BASE + 24576)
    v_tok = at("v_tok", [128, NB * NVT, 128], F32, BASE + 40960)
    v_pair = at("v_pair", [128, NB, T // 2], F32, BASE + 53248)
    q_pair = at("q_pair", [128, 2, NCH, NB, 128], F32, BASE + 65536)
    m_ring = at("m_ring", [128, 4, 384], F32, BASE + 77824)
    s_ring = at("s_ring", [128, 4, 384], F32, BASE + 83968)
    pt_ring = at("pt_ring", [128, 3, 384], F32, BASE + 90112)
    stats = at("stats", [128, 3, UNITS], F32, BASE + 94720)
    a_out = at("a_out", [128, FT * T], F32, X_AT + 73728)
    bias_pair = at("bias_pair", [128, BIAS_E, 2, BIAS_X], F32, BASE + 196608)

    bias_in, mask_in = sem("bias_in"), sem("mask_in")
    q_zeroed, q_staged, v_staged, v_turned, v_ready = (sem(n) for n in ("q_zeroed", "q_staged", "v_staged", "v_turned", "v_ready"))
    q_staged2, v_ready2, bias_staged = sem("q_staged2"), sem("v_ready2"), sem("bias_staged")
    masked_bias, qk_done, scored, exped, recip_done, normed = (
        sem(n) for n in ("masked_bias", "qk_done", "scored", "exped", "recip_done", "normed"))
    p_turned, pt_copied, pv_done, o_copied = (sem(n) for n in ("p_turned", "pt_copied", "pv_done", "o_copied"))

    def unit(u):
        b, c, hh = u // 6, u % 6 // 2, u % 2
        return b, c, hh, KEY_ROWS[c], KEY_ROWS[c] * KCOLS

    def since(p, u, back, per=UNITS):
        return per * p + max(u - back + 1, 0)

    with nc.Block() as block:
        @block.sync
        def _(sp):
            for i in range(QROWS):
                src = bass.AP(rpb_pad.tensor, (7 - i) * N_HEADS * RP_COLS,
                              [[1, QCOLS], [RP_COLS, BIAS_E * N_HEADS], [1, BIAS_X]])
                sp.dma_start(bias[QCOLS * i:QCOLS * i + QCOLS, :].rearrange("p (eh x) -> p eh x", x=BIAS_X),
                             src).then_inc(bias_in, 16)
            sp.dma_start(mask[:], masks).then_inc(mask_in, 16)

        @block.gpsimd
        def _(pool):
            pool.wait_ge(mask_in, 16)
            with pool.Fori(0, FT) as p:
                pool.wait_ge(bias_staged, p + 1)
                for u in range(UNITS):
                    b, c, hh, rows, n = unit(u)
                    pool.wait_ge(scored, since(p, u, 4))
                    e0 = 0 if c == 2 else 4
                    x0 = KEY_COL[b] - QCOLS * b + 16
                    tab = bias_pair[:, e0:e0 + rows, hh, x0:x0 + KCOLS]
                    k0 = b * MASK_COLS + sum(KEY_ROWS[:c]) * KCOLS
                    pool.tensor_tensor(m_ring[:, u % 4, 0:n].rearrange("p (e x) -> p e x", e=rows),
                                       mask[:, k0:k0 + n].rearrange("p (e x) -> p e x", e=rows), tab, ALU.subtract
                                       ).then_inc(masked_bias, 1)

        @block.scalar
        def _(act):
            act.wait_ge(q_zeroed, 2)
            with act.Fori(0, FT) as p:
                act.wait_ge(qk_done, UNITS * p)
                for c in range(NCH):
                    src = z[64:128, bass.ds(p * T + c * CH, CH)].rearrange("p (r b w) -> p b r w", b=NB, w=QCOLS)
                    act.activation(q_pair[64:128, 1, c].rearrange("p b (r w) -> p b r w", w=QCOLS)[:, :, :, ::-1], src, ACT.Copy
                                   ).then_inc(q_staged2, 1)
                for i in range(0, 6, 2):
                    act.wait_ge(v_turned, 6 * p + i + 1)
                    act.activation(v_tok[:, 4 * i:4 * i + 4], banks[:, 6].rearrange("p (t f) -> p t f", f=128), ACT.Copy
                                   ).then_inc(v_ready, 1)

                def exp(u):
                    n = unit(u)[4]
                    act.wait_ge(scored, since(p, u, 0))
                    act.activation(s_ring[:, u % 4, 0:n], s_ring[:, u % 4, 0:n], ACT.Exp, scale=-1.0,
                                   bias=stats[:, 0, u:u + 1], accum_out=stats[:, 1, u:u + 1]).then_inc(exped, 1)

                def copy_pt(u):
                    n = unit(u)[4]
                    act.wait_ge(p_turned, since(p, u, 0))
                    act.wait_ge(pv_done, since(p, u, 3))
                    act.activation(pt_ring[:, u % 3, 0:n], banks[:, 2 + u % 2, 0:n], ACT.Copy).then_inc(pt_copied, 1)

                def copy_o(v):
                    b, c = unit(2 * v)[:2]
                    act.wait_ge(pv_done, since(p, 2 * v + 1, 0))
                    dst = a_out[:, bass.ds(p * T + c * CH, CH)].rearrange("p (r b w) -> p b r w", b=NB, w=QCOLS)[:, b]
                    act.activation(dst, banks[:, 4 + v % 2, 0:128].rearrange("p (r w) -> p r w", w=QCOLS)[:, :, ::-1], ACT.Copy
                                   ).then_inc(o_copied, 1)

                for s in range(UNITS + 5):
                    if s < UNITS:
                        exp(s)
                    if 0 <= s - 3 < UNITS:
                        copy_pt(s - 3)
                    if s >= 6 and s % 2 == 0:
                        copy_o((s - 6) // 2)

        @block.vector
        def _(dve):
            dve.memset(q_pair[64:128, 0], 0.0).then_inc(q_zeroed, 1)
            dve.memset(q_pair[0:64, 1], 0.0).then_inc(q_zeroed, 1)
            dve.wait_ge(bias_in, 16 * QROWS)
            with dve.Fori(0, FT) as p:
                dve.wait_ge(masked_bias, UNITS * p)
                dve.tensor_copy(bias_pair[:].rearrange("p e h x -> p e (h x)"), bias[:].rearrange(
                    "p (e hx) -> p e hx", e=BIAS_E)[:, :, bass.ds(2 * BIAS_X * p, 2 * BIAS_X)]).then_inc(bias_staged, 1)
                dve.wait_ge(v_turned, 6 * p)
                for b in range(NB):
                    src = z[:, bass.ds((2 * FT + p) * T, T)].rearrange("p (r w) -> p r w", w=GRID_W)[
                        :, :, KEY_COL[b]:KEY_COL[b] + KCOLS]
                    dve.tensor_copy(v_pair[:, b].rearrange("p (r w) -> p r w", w=KCOLS), src).then_inc(v_staged, 1)
                dve.wait_ge(qk_done, UNITS * p)
                for c in range(NCH):
                    src = z[0:64, bass.ds(p * T + c * CH, CH)].rearrange("p (r b w) -> p b r w", b=NB, w=QCOLS)
                    dve.tensor_copy(q_pair[0:64, 0, c].rearrange("p b (r w) -> p b r w", w=QCOLS)[:, :, :, ::-1], src
                                    ).then_inc(q_staged, 1)
                def ready(u):
                    dve.wait_ge(qk_done, since(p, u, 0))
                    dve.wait_ge(masked_bias, since(p, u, 0))
                    dve.wait_ge(p_turned, since(p, u, 4))

                for i in range(1, 6, 2):
                    dve.wait_ge(v_turned, 6 * p + i + 1)
                    if i == 5:
                        ready(0)
                        ready(1)
                    dve.tensor_copy(v_tok[:, 4 * i:4 * i + 4], banks[:, 7].rearrange("p (t f) -> p t f", f=128)
                                    ).then_inc(v_ready2, 1)

                def score(u):
                    n = unit(u)[4]
                    dve.tensor_tensor_reduce(s_ring[:, u % 4, 0:n], banks[:, u % 2, 0:n], m_ring[:, u % 4, 0:n], 1.0,
                                             3e38, ALU.add, ALU.min, stats[:, 0, u:u + 1]).then_inc(scored, 1)

                def norm(u):
                    n = unit(u)[4]
                    dve.wait_ge(exped, since(p, u, 0))
                    dve.reciprocal(stats[:, 2, u:u + 1], stats[:, 1, u:u + 1]).then_inc(recip_done, 1)
                    dve.wait_ge(recip_done, since(p, u, 0))
                    if u + 2 < UNITS:
                        ready(u + 2)
                    dve.tensor_scalar(s_ring[:, u % 4, 0:n], s_ring[:, u % 4, 0:n], stats[:, 2, u:u + 1], None, ALU.mult
                                      ).then_inc(normed, 1)

                for s in range(UNITS + 2):
                    if s >= 2:
                        norm(s - 2)
                    if s < UNITS:
                        score(s)

        @block.tensor
        def _(pe):
            with pe.Fori(0, FT) as p:
                for i in range(6):
                    if i >= 2:
                        pe.wait_ge((v_ready, v_ready2)[i % 2], 3 * p + i // 2)
                    pe.wait_ge(v_staged, NB * p + (4 * i + 3) // NVT + 1)
                    for t in range(4 * i, 4 * i + 4):
                        b, vt = divmod(t, NVT)
                        last = pe.transpose(banks[:, 6 + i % 2, 128 * (t % 4):128 * (t % 4) + 128],
                                            v_pair[:, b, 128 * vt:128 * vt + 128], ident[:])
                    last.then_inc(v_turned, 1)
                pe.wait_ge(q_staged, NCH * p + NCH)
                pe.wait_ge(q_staged2, NCH * p + NCH)

                def scores(u):
                    b, c, hh, rows, n = unit(u)
                    pe.wait_ge(scored, since(p, u, 2))
                    keys = z[:, bass.ds((FT + p) * T + KEY_TOKEN0[c], rows * GRID_W)].rearrange(
                        "p (r w) -> p r w", w=GRID_W)[:, :, KEY_COL[b]:KEY_COL[b] + KCOLS]
                    pe.matmul(banks[:, u % 2, 0:n], q_pair[:, hh, c, b], keys, start=True, stop=True).then_inc(qk_done, 1)

                def turn(u):
                    rows = unit(u)[3]
                    pe.wait_ge(normed, since(p, u, 0))
                    pe.wait_ge(pt_copied, since(p, u, 2))
                    for j in range(rows // 4):
                        last = pe.transpose(banks[:, 2 + u % 2, 128 * j:128 * j + 128],
                                            s_ring[:, u % 4, 128 * j:128 * j + 128], ident[:])
                    last.then_inc(p_turned, 1)

                def values(u):
                    b, c, hh, rows, n = unit(u)
                    v = u // 2
                    if u == 0:
                        pe.wait_ge(v_ready, 3 * p + 3)
                        pe.wait_ge(v_ready2, 3 * p + 3)
                    pe.wait_ge(pt_copied, since(p, u, 0))
                    pe.wait_ge(o_copied, since(p, v, 2, UNITS // 2))
                    for j in range(rows // 4):
                        last = pe.matmul(banks[64 * hh:64 * hh + 64, 4 + v % 2, 0:128],
                                         v_tok[:, b * NVT + V_TILE0[c] + j, 64 * hh:64 * hh + 64],
                                         pt_ring[:, u % 3, 128 * j:128 * j + 128], start=(j == 0), stop=(j == rows // 4 - 1))
                    last.then_inc(pv_done, 1)

                for s in range(UNITS + 4):
                    if s < UNITS:
                        scores(s)
                    if 0 <= s - 3 < UNITS:
                        turn(s - 3)
                    if s >= 4:
                        values(s - 4)


def fourier(nc, at, sem, banks, g):
    u_scratch, w_fmix, dft_c, dft_t1, dft_t0 = (g[k] for k in ("u_scratch", "w_fmix", "dft_c", "dft_t1", "dft_t0"))
    u = at("u", [128, FT, T], F32, BASE)
    pq = at("pq", [128, TT, FT, 256], F32, BASE + 24576)
    tab0 = at("tab0", [128, 2, T_PROMPT // 128, T_PROMPT // 2], F32, BASE + 73728)
    tab1 = at("tab1", [128, 2, T_SAMPLE // 128, T_SAMPLE // 2], F32, X_AT + 24576)
    maps = at("maps", [128, FT, 256], F32, BASE + 81920)
    wf = at("wf", [128, FT, 128], F32, BASE + 86016)
    cs = at("cs", [128, 256], F32, BASE + 88064)
    alt = at("alt", [128, 3, FT, 2], F32, BASE + 89088)
    b_ring = at("b_ring", [128, 2, CH], F32, BASE + 90112)
    f_out = at("f_out", [128, FT, T], F32, X_AT)
    REQS = [(0, T_PROMPT, tab0), (T_PROMPT, T_SAMPLE, tab1)]

    u_in, wf_in, cs_in, tab0_in, tab1_in = (sem(n) for n in ("u_in", "wf_in", "cs_in", "tab0_in", "tab1_in"))
    maps_summed, maps_ready, alt_sums, alt_ready = (sem(n) for n in ("maps_summed", "maps_ready", "alt_sums", "alt_ready"))
    pq_summed, pq_act, pq_dve, half_summed, half_ready = (
        sem(n) for n in ("pq_summed", "pq_act", "pq_dve", "half_summed", "half_ready"))
    ab_summed, b_ready, f_ready = sem("ab_summed"), sem("b_ready"), sem("f_ready")

    with nc.Block() as block:
        @block.sync
        def _(sp):
            sp.dma_start(cs[:], dft_c).then_inc(cs_in, 16)
            sp.dma_start(wf[:], w_fmix.rearrange("g c d -> c g d")).then_inc(wf_in, 16)
            sp.dma_start(u[:], u_scratch.rearrange("(g p) t -> p g t", p=128)).then_inc(u_in, 16)
            for half in range(2):
                sp.dma_start(tab0[:, half], dft_t0[half].rearrange("(t p) k -> p t k", p=128)).then_inc(tab0_in, 16)
            for half in range(2):
                sp.dma_start(tab1[:, half], dft_t1[half].rearrange("(t p) k -> p t k", p=128)).then_inc(tab1_in, 16)

        @block.scalar
        def _(act):
            act.wait_ge(maps_summed, 1)
            act.activation(maps[:, 0:2], banks[:, 0].rearrange("p (g n) -> p g n", g=2), ACT.Copy).then_inc(maps_ready, 1)
            act.activation(maps[:, 2:4], banks[:, 1].rearrange("p (g n) -> p g n", g=2), ACT.Copy).then_inc(maps_ready, 1)
            for t in range(TT):
                act.wait_ge(pq_summed, t + 1)
                act.activation(pq[:, t, 0:2], banks[:, 2 * (t % 2)].rearrange("p (g n) -> p g n", g=2), ACT.Copy
                               ).then_inc(pq_act, 1)
            for n in range(2 * FT):
                r, c = divmod(n, FT)
                k = REQS[r][1] // 2
                act.wait_ge(ab_summed, n + 1)
                if n >= 2:
                    act.wait_ge(f_ready, n - 1)
                act.activation(b_ring[:, n % 2, 0:k], banks[:, 5 + 2 * (n % 2), 0:k], ACT.Copy).then_inc(b_ready, 1)

        @block.vector
        def _(dve):
            dve.wait_ge(u_in, 16)
            for r, (t0, t, _) in enumerate(REQS):
                parts = u[:, :, t0:t0 + t].rearrange("p g (t two) -> p g two t", two=2)
                for odd in range(2):
                    dve.tensor_reduce(alt[:, odd, :, r:r + 1], parts[:, :, odd:odd + 1], AX.X, ALU.add).then_inc(alt_sums, 1)
            dve.wait_ge(alt_sums, 4)
            dve.tensor_tensor(alt[:, 2], alt[:, 0], alt[:, 1], ALU.subtract).then_inc(alt_ready, 1)
            for t in range(TT):
                dve.wait_ge(pq_summed, t + 1)
                dve.tensor_copy(pq[:, t, 2:4], banks[:, 2 * (t % 2) + 1].rearrange("p (g n) -> p g n", g=2)
                                ).then_inc(pq_dve, 1)
            dve.wait_ge(half_summed, 1)
            for r, (t0, t, _) in enumerate(REQS):
                dve.tensor_scalar(f_out[:, :, t0 + t // 2:t0 + t // 2 + 1],
                                  banks[:, 0, 0:2 * FT].rearrange("p (g r) -> p g r", r=2)[:, :, r:r + 1],
                                  t ** -0.5, None, ALU.mult).then_inc(half_ready, 1)
            for n in range(2 * FT):
                r, c = divmod(n, FT)
                t0, t, _ = REQS[r]
                k = t // 2
                dve.wait_ge(b_ready, n + 1)
                dve.tensor_tensor(f_out[:, c, t0:t0 + k], banks[:, 4 + 2 * (n % 2), 0:k], b_ring[:, n % 2, 0:k], ALU.subtract)
                dve.tensor_tensor(f_out[:, c, t0 + k + 1:t0 + t][:, ::-1], banks[:, 4 + 2 * (n % 2), 1:k],
                                  b_ring[:, n % 2, 1:k], ALU.add).then_inc(f_ready, 1)

        @block.tensor
        def _(pe):
            pe.wait_ge(cs_in, 16)
            pe.wait_ge(wf_in, 16)
            for c in range(FT):
                for half in range(2):
                    at_ = 256 * (c % 2) + 128 * half
                    last = pe.matmul(banks[:, c // 2, at_:at_ + 128], cs[:, 128 * half:128 * half + 128], wf[:, c],
                                     start=True, stop=True)
            last.then_inc(maps_summed, 1)
            pe.wait_ge(maps_ready, 2)
            pe.wait_ge(u_in, 16)
            for t in range(TT):
                if t >= 2:
                    pe.wait_ge(pq_act, t - 1)
                    pe.wait_ge(pq_dve, t - 1)
                for c in range(FT):
                    last = pe.matmul(banks[:, 2 * (t % 2) + c // 2, 256 * (c % 2):256 * (c % 2) + 256],
                                     u[:, c, 128 * t:128 * t + 128], maps[:, c], start=True, stop=True)
                last.then_inc(pq_summed, 1)
            pe.wait_ge(alt_ready, 1)
            pe.wait_ge(pq_act, TT - 1)
            for c in range(FT):
                last = pe.matmul(banks[:, 0, 2 * c:2 * c + 2], maps[:, c, 0:128], alt[:, 2, c], start=True, stop=True)
            last.then_inc(half_summed, 1)
            pe.wait_ge(pq_act, TT)
            pe.wait_ge(pq_dve, TT)
            for n in range(2 * FT):
                r, c = divmod(n, FT)
                t0, t, tab = REQS[r]
                if c == 0:
                    pe.wait_ge((tab0_in, tab1_in)[r], 32)
                if n >= 2:
                    pe.wait_ge(f_ready, n - 1)
                for half in range(2):
                    for i in range(t // 128):
                        last = pe.matmul(banks[:, 4 + 2 * (n % 2) + half, 0:t // 2],
                                         pq[:, t0 // 128 + i, c, 128 * half:128 * half + 128], tab[:, half, i],
                                         start=(i == 0), stop=(i == t // 128 - 1))
                last.then_inc(ab_summed, 1)


def mix_norm(nc, at, sem, banks, g):
    f_out, a_out, ones_all, vec, eps_t, h_hi, h_lo = (
        g["made"]["f_out"], g["made"]["a_out"], g["ones_all"], g["vec"], g["eps_t"], g["h_hi"], g["h_lo"])
    V_GF, V_GA = g["V_GF"], g["V_GA"]
    W = X_AT + 24576
    sq = at("mix_sq", [128, 2, FT, CH], F32, W)
    rms = at("mix_rms", [128, 2, CH], F32, W + 16384)
    t_ring = at("mix_t", [128, 4, CH], F32, W + 20480)
    squared, summed, rooted, recips, t_ready, hi_ready, split = (
        sem("mix_" + n) for n in ("squared", "summed", "rooted", "recips", "t_ready", "hi_ready", "split"))
    a3 = a_out[:].rearrange("p (g t) -> p g t", t=T)
    groups = [(half, c) for c in range(NCH) for half in range(2)]

    with nc.Block() as block:
        @block.scalar
        def _(act):
            for n, (half, c) in enumerate(groups):
                src = (f_out, a3)[half][:, :, CH * c:CH * c + CH]
                if n >= 2:
                    act.wait_ge(summed, n - 1)
                for i in range(FT):
                    act.activation(sq[:, n % 2, i], src[:, i], ACT.Square).then_inc(squared, 1)
                act.wait_ge(summed, n + 1)
                if n >= 2:
                    act.wait_ge(t_ready, 4 * (n - 1))
                act.activation(rms[:, n % 2], banks[:, n % 2], ACT.Sqrt, scale=1.0 / D_FOURIER, bias=eps_t[:]
                               ).then_inc(rooted, 1)

        @block.vector
        def _(dve):
            for n, (half, c) in enumerate(groups):
                src = (f_out, a3)[half][:, :, CH * c:CH * c + CH]
                dve.wait_ge(rooted, n + 1)
                dve.reciprocal(rms[:, n % 2], rms[:, n % 2]).then_inc(recips, 1)
                dve.wait_ge(recips, n + 1)
                for i in range(FT):
                    m = 4 * n + i
                    gain = (V_GF, V_GA)[half] + i
                    dve.scalar_tensor_tensor(t_ring[:, m % 4], src[:, i], vec[:, gain:gain + 1], rms[:, n % 2],
                                             ALU.mult, ALU.mult).then_inc(t_ready, 1)
                    hi, lo = (h[:, FT * half + i, CH * c:CH * c + CH] for h in (h_hi, h_lo))
                    dve.wait_ge(t_ready, m + 1)
                    dve.tensor_copy(hi, t_ring[:, m % 4]).then_inc(hi_ready, 1)
                    dve.wait_ge(hi_ready, m + 1)
                    dve.tensor_tensor(lo, t_ring[:, m % 4], hi.bitcast(F32), ALU.subtract).then_inc(split, 1)

        @block.tensor
        def _(pe):
            for n in range(len(groups)):
                pe.wait_ge(squared, FT * (n + 1))
                if n >= 2:
                    pe.wait_ge(rooted, n - 1)
                for i in range(FT):
                    last = pe.matmul(banks[:, n % 2], ones_all[:].bitcast(F32), sq[:, n % 2, i],
                                     start=(i == 0), stop=(i == FT - 1))
                last.then_inc(summed, 1)


def out_projection(nc, at, sem, banks, g):
    x_prompt, x_sample, w_o, mod, coef, ident, ones_all, eps_t, stat, h_hi, h_lo, mm3 = (
        g[k] for k in ("x_prompt", "x_sample", "w_o", "mod", "coef", "ident", "ones_all", "eps_t", "stat", "h_hi",
                       "h_lo", "mm3"))
    NO = 256
    x1 = at("x1", [128, TT, D], F32, X_AT)
    gate2 = at("gate2", [128, 2, D], F32, GATE2_AT)
    wo_hi = at("wo_hi", [128, 2, KT, NO], F32R, REST)
    wo_lo = at("wo_lo", [128, 2, KT, NO], F32R, REST + 16384)
    wo_raw = at("wo_raw", [128, 2, KT, NO], F32, REST + 16384)
    gate1 = at("gate1", [128, 2, D], F32, REST + 32768)
    diag = at("diag", [128, 4, 128], F32, REST + 40960)
    tmp = at("gated", [128, 4, NO], F32, REST + 43008)
    t_ring = at("t_second", [128, 2, CH], F32, REST + 47104)
    xn = at("xn", [128, 4, D], F32, REST)
    junk = at("junk2", [128, D], F32, REST + 16384)

    x_in, wo_in = [sem(f"x1_in{c}") for c in range(NCH)], [sem(f"wo_in{s}") for s in range(2)]
    wo_hi_s, wo_ready = sem("wo_hi_s"), sem("wo_ready")
    diag_ready, gate_summed, gates = sem("diag_ready"), sem("gate_summed"), sem("gates")
    o_summed, gated, x1_added = sem("o_summed"), sem("gated_s"), sem("x1_added")
    squared, rooted, rstd, xn_ready, turned, t_ready, hi_ready, split = (
        sem("h2_" + n) for n in ("squared", "rooted", "rstd", "xn_ready", "turned", "t_ready", "hi_ready", "split"))
    OS, NG = D // NO, 6

    with nc.Block() as block:
        @block.sync
        def _(sp):
            for n in range(OS):
                if n >= 2:
                    sp.wait_ge(o_summed, TT * (n - 1))
                sp.dma_start(wo_raw[:, n % 2], w_o[:, NO * n:NO * n + NO].rearrange("(k p) n -> p k n", p=128)
                             ).then_inc(wo_in[n % 2], 16)
                if n == 1:
                    for c in range(NCH):
                        src = x_prompt if c == 0 else x_sample[CH * (c - 1):CH * c]
                        sp.dma_start(x1[:, 4 * c:4 * c + 4], src.rearrange("(t p) n -> p t n", p=128)
                                     ).then_inc(x_in[c], 16)

        @block.scalar
        def _(act):
            def split_hi(n):
                act.wait_ge(wo_in[n % 2], 16 * (n // 2) + 16)
                act.activation(wo_hi[:, n % 2], wo_raw[:, n % 2], ACT.Copy).then_inc(wo_hi_s, 1)
            split_hi(0)
            split_hi(1)
            for m in range(8):
                act.wait_ge(gate_summed, m + 1)
                gate, r, half = (gate1, gate2)[m // 4], m // 2 % 2, m % 2
                act.activation(gate[:, r, 512 * half:512 * half + 512], banks[:, 6 + m % 2], ACT.Copy).then_inc(gates, 1)
            split_hi(2)
            split_hi(3)
            act.wait_ge(o_summed, TT * OS)
            for c in range(NCH):
                act.wait_ge(x1_added, TT * (OS - 1) + 4 * c + 4)
                for t in range(4 * c, 4 * c + 4):
                    if t:
                        act.wait_ge(squared, t)
                    act.activation(junk[:], x1[:, t], ACT.Square, accum_out=stat[:, 0, t:t + 1]).then_inc(squared, 1)
                act.wait_ge(squared, 4 * c + 4)
                act.activation(stat[:, 0, 4 * c:4 * c + 4], stat[:, 0, 4 * c:4 * c + 4], ACT.Sqrt,
                               scale=1.0 / D, bias=eps_t[:]).then_inc(rooted, 1)
            for n in range(NCH * KT):
                c, k = divmod(n, KT)
                r = REQ[c]
                act.wait_ge(turned, n + 1)
                if n >= 2:
                    act.wait_ge(split, n - 1)
                act.activation(t_ring[:, n % 2], banks[:, n % 4], ACT.Identity, scale=coef[:, 1, k, r:r + 1],
                               bias=mod[:, 3 * KT + k, r:r + 1]).then_inc(t_ready, 1)

        @block.gpsimd
        def _(pool):
            for n in range(OS):
                for t in range(TT):
                    if n == 0 and t % 4 == 0:
                        pool.wait_ge(x_in[t // 4], 16)
                    pool.wait_ge(gated, TT * n + t + 1)
                    part = x1[:, t, NO * n:NO * n + NO]
                    pool.tensor_tensor(part, part, tmp[:, (TT * n + t) % 4], ALU.add).then_inc(x1_added, 1)

        @block.vector
        def _(dve):
            def split_lo(n):
                dve.wait_ge(wo_hi_s, n + 1)
                dve.tensor_tensor(wo_lo[:, n % 2], wo_raw[:, n % 2], wo_hi[:, n % 2].bitcast(F32), ALU.subtract
                                  ).then_inc(wo_ready, 1)
            split_lo(0)
            for m in range(32):
                gate, r, k = m // 16, m // 8 % 2, m % 8
                if m >= 4:
                    dve.wait_ge(gate_summed, m // 4)
                tile = (2 + 3 * gate) * KT + k
                dve.tensor_scalar(diag[:, m % 4], ident[:], mod[:, tile, r:r + 1], None, ALU.mult).then_inc(diag_ready, 1)
            split_lo(1)
            dve.wait_ge(gates, 8)
            for n in range(OS):
                for t in range(TT):
                    m = TT * n + t
                    dve.wait_ge(o_summed, m + 1)
                    if m >= 4:
                        dve.wait_ge(x1_added, m - 3)
                    dve.tensor_tensor(tmp[:, m % 4], banks[:, m % NG, 0:NO], gate1[:, REQ[t // 4], NO * n:NO * n + NO],
                                      ALU.mult).then_inc(gated, 1)
                    if t == 3 and 1 <= n < OS - 1:
                        split_lo(n + 1)
            for c in range(NCH):
                dve.wait_ge(rooted, c + 1)
                dve.reciprocal(stat[:, 1, 4 * c:4 * c + 4], stat[:, 0, 4 * c:4 * c + 4]).then_inc(rstd, 1)
                dve.wait_ge(rstd, c + 1)
                if c:
                    dve.wait_ge(turned, KT * c)
                for i in range(4):
                    dve.tensor_scalar(xn[:, i], x1[:, 4 * c + i], stat[:, 1, 4 * c + i:4 * c + i + 1], None, ALU.mult
                                      ).then_inc(xn_ready, 1)
                for k in range(KT):
                    n = KT * c + k
                    dve.wait_ge(t_ready, n + 1)
                    hi, lo = (h[:, k, CH * c:CH * c + CH] for h in (h_hi, h_lo))
                    dve.tensor_copy(hi, t_ring[:, n % 2]).then_inc(hi_ready, 1)
                    dve.wait_ge(hi_ready, n + 1)
                    dve.tensor_tensor(lo, t_ring[:, n % 2], hi.bitcast(F32), ALU.subtract).then_inc(split, 1)

        @block.tensor
        def _(pe):
            for m in range(8):
                pe.wait_ge(diag_ready, 4 * m + 4)
                if m >= 2:
                    pe.wait_ge(gates, m - 1)
                for i in range(4):
                    last = pe.matmul(banks[:, 6 + m % 2, 128 * i:128 * i + 128], ones_all[:].bitcast(F32), diag[:, i],
                                     start=True, stop=True)
                last.then_inc(gate_summed, 1)
            for n in range(OS):
                pe.wait_ge(wo_ready, n + 1)
                for t in range(TT):
                    m = TT * n + t
                    if m >= NG:
                        pe.wait_ge(gated, m - NG + 1)
                    for k in range(KT):
                        last = mm3(pe, banks[:, m % NG, 0:NO],
                                   (h_hi[:, k, 128 * t:128 * t + 128], h_lo[:, k, 128 * t:128 * t + 128]),
                                   (wo_hi[:, n % 2, k], wo_lo[:, n % 2, k]), k == 0, k == KT - 1)
                    last.then_inc(o_summed, 1)
            pe.wait_ge(gated, TT * OS)
            for n in range(NCH * KT):
                c, k = divmod(n, KT)
                pe.wait_ge(xn_ready, 4 * c + 4)
                if n >= 4:
                    pe.wait_ge(t_ready, n - 3)
                for i in range(4):
                    last = pe.transpose(banks[:, n % 4, 128 * i:128 * i + 128], xn[:, i, 128 * k:128 * k + 128], ident[:])
                last.then_inc(turned, 1)


def feed_forward(nc, at, sem, banks, g):
    w_gate, w_up, w_down, y_prompt, y_sample, h_hi, h_lo, mm3 = (
        g[k] for k in ("w_gate", "w_up", "w_down", "y_prompt", "y_sample", "h_hi", "h_lo", "mm3"))
    x1, gate2 = g["made"]["x1"], g["made"]["gate2"]
    ff_hi = at("ff_hi", [128, 2, T], F32R, REST)
    ff_lo = at("ff_lo", [128, 2, T], F32R, REST + 12288)
    ff_raw = at("ff_raw", [128, 2, T], F32, REST + 12288)
    w_hi = at("wff_hi", [128, 3, D], F32R, REST + 24576)
    w_lo = at("wff_lo", [128, 3, D], F32R, REST + 36864)
    w_raw = at("wff_raw", [128, 3, D], F32, REST + 36864)
    scratch = at("ff_scratch", [128, 3, CH], F32, REST + 49152)
    PAIRS = FF // 2
    GATE, UP, DOWN = 0, 1, 2
    TILES = [(GATE, 0), (UP, 0), (GATE, 1), (UP, 1), (DOWN, 0), (DOWN, 1)]

    w_in = [sem(f"wff_in{s}") for s in range(3)]
    w_split_hi, w_ready = sem("wff_split_hi"), sem("wff_ready")
    g_summed, u_summed, silu_ready, product, ff_hi_s, ff_ready = (
        sem("ff_" + n) for n in ("g_summed", "u_summed", "silu_ready", "product", "hi_s", "ready"))
    d_summed, d_gated, d_added = sem("d_summed"), sem("d_gated"), sem("d_added")
    y_stored = sem("y_stored")
    DG = 2 * TT

    with nc.Block() as block:
        @block.sync
        def _(sp):
            def load(j, i):
                kind, f = TILES[i]
                if kind == DOWN:
                    src, dst = w_down[bass.ds((2 * j + f) * 128, 128), :], w_raw[:, i % 3]
                else:
                    src = (w_gate, w_up)[kind][:, bass.ds((2 * j + f) * 128, 128)].rearrange("(k p) n -> p k n", p=128)
                    dst = w_raw[:, i % 3].rearrange("p (k n) -> p k n", n=128)
                sp.dma_start(dst, src).then_inc(w_in[i % 3], 16)

            def used(j, i):
                kind, f = TILES[i]
                if kind == DOWN:
                    sp.wait_ge(d_summed, DG * j + DG)
                else:
                    sp.wait_ge((g_summed, u_summed)[kind], 6 * j + 3 * f + 3)

            def later(j):
                for i in range(6):
                    used(j, i)
                    load(j + (i + 3) // 6, (i + 3) % 6)
            for i in range(3):
                load(0, i)
            with sp.Fori(0, PAIRS - 1) as j:
                later(j)
            for i in range(3):
                used(PAIRS - 1, i)
                load(PAIRS - 1, i + 3)
            for t in range(TT):
                sp.wait_ge(d_added, DG * (PAIRS - 1) + 2 * t + 2)
                dst = y_prompt[0, 128 * t:128 * t + 128] if t < 4 else y_sample[0, 128 * (t - 4):128 * (t - 3)]
                sp.dma_start(dst, x1[:, t]).then_inc(y_stored, 16)
            sp.wait_ge(y_stored, 16 * TT)

        def split_hi(act, j, i):
            act.wait_ge(w_in[i % 3], 16 * (2 * j + i // 3) + 16)
            act.activation(w_hi[:, i % 3], w_raw[:, i % 3], ACT.Copy).then_inc(w_split_hi, 1)

        def split_lo(dve, j, i):
            dve.wait_ge(w_split_hi, 6 * j + i + 1)
            dve.tensor_tensor(w_lo[:, i % 3], w_raw[:, i % 3], w_hi[:, i % 3].bitcast(F32), ALU.subtract
                              ).then_inc(w_ready, 1)

        @block.scalar
        def _(act):
            def pair(j, last):
                for i, (kind, f) in enumerate(TILES):
                    if not (last and i >= 4):
                        split_hi(act, j + (i + 2) // 6, (i + 2) % 6)
                    for c in range(NCH):
                        n = 3 * f + c
                        if kind == GATE:
                            act.wait_ge(g_summed, 6 * j + n + 1)
                            if n == 0:
                                act.wait_ge(d_added, DG * j)
                            act.wait_ge(product, 6 * j + max(n - 2, 0))
                            act.activation(scratch[:, c], banks[:, c], ACT.Silu).then_inc(silu_ready, 1)
                        if kind == UP:
                            act.wait_ge(product, 6 * j + n + 1)
                            act.activation(ff_hi[:, f, CH * c:CH * c + CH], ff_raw[:, f, CH * c:CH * c + CH], ACT.Copy
                                           ).then_inc(ff_hi_s, 1)
            split_hi(act, 0, 0)
            split_hi(act, 0, 1)
            with act.Fori(0, PAIRS - 1) as j:
                pair(j, False)
            pair(PAIRS - 1, True)

        @block.vector
        def _(dve):
            def pair(j, last):
                for i, (kind, f) in enumerate(TILES):
                    if i < 5 and not (last and i == 4):
                        split_lo(dve, j + (i + 2) // 6, (i + 2) % 6)
                    if kind == UP:
                        for c in range(NCH):
                            n = 3 * f + c
                            part = ff_raw[:, f, CH * c:CH * c + CH]
                            dve.wait_ge(u_summed, 6 * j + n + 1)
                            dve.wait_ge(silu_ready, 6 * j + n + 1)
                            dve.tensor_tensor(part, banks[:, 3 + c], scratch[:, c], ALU.mult).then_inc(product, 1)
                            dve.wait_ge(ff_hi_s, 6 * j + n + 1)
                            dve.tensor_tensor(ff_lo[:, f, CH * c:CH * c + CH], part,
                                              ff_hi[:, f, CH * c:CH * c + CH].bitcast(F32), ALU.subtract
                                              ).then_inc(ff_ready, 1)
                    if i == 5:
                        for n in range(DG):
                            t, half = divmod(n, 2)
                            dve.wait_ge(d_summed, DG * j + n + 1)
                            dve.wait_ge(d_added, DG * j + max(n - 2, 0))
                            dve.tensor_tensor(scratch[:, n % 3], banks[:, (6 + n) % 8], gate2[:, REQ[t // 4], 512 * half:512 * half + 512],
                                              ALU.mult).then_inc(d_gated, 1)
                        if not last:
                            split_lo(dve, j + 1, 1)
            split_lo(dve, 0, 0)
            split_lo(dve, 0, 1)
            with dve.Fori(0, PAIRS - 1) as j:
                pair(j, False)
            pair(PAIRS - 1, True)

        @block.gpsimd
        def _(pool):
            with pool.Fori(0, PAIRS) as j:
                for n in range(DG):
                    t, half = divmod(n, 2)
                    pool.wait_ge(d_gated, DG * j + n + 1)
                    part = x1[:, t, 512 * half:512 * half + 512]
                    pool.tensor_tensor(part, part, scratch[:, n % 3], ALU.add).then_inc(d_added, 1)

        @block.tensor
        def _(pe):
            with pe.Fori(0, PAIRS) as j:
                for i, (kind, f) in enumerate(TILES[:4]):
                    w = [part[:, i % 3].rearrange("p (k n) -> p k n", n=128) for part in (w_hi, w_lo)]
                    pe.wait_ge(w_ready, 6 * j + i + 1)
                    for c in range(NCH):
                        if f == 0:
                            pe.wait_ge(d_gated, DG * j)
                        elif kind == GATE:
                            pe.wait_ge(silu_ready, 6 * j + c + 1)
                        else:
                            pe.wait_ge(product, 6 * j + c + 1)
                        for k in range(KT):
                            last = mm3(pe, banks[:, 3 * kind + c], (w[0][:, k], w[1][:, k]),
                                       (h_hi[:, k, CH * c:CH * c + CH], h_lo[:, k, CH * c:CH * c + CH]), k == 0, k == KT - 1)
                        last.then_inc((g_summed, u_summed)[kind], 1)
                pe.wait_ge(w_ready, 6 * j + 6)
                for n in range(DG):
                    t, half = divmod(n, 2)
                    if t % 4 == 0 and half == 0:
                        pe.wait_ge(ff_ready, 6 * j + 3 + t // 4 + 1)
                    if n >= 8:
                        pe.wait_ge(d_gated, DG * j + n - 7)
                    elif n >= 2:
                        pe.wait_ge(product, 6 * j + 6)
                    for f in range(2):
                        last = mm3(pe, banks[:, (6 + n) % 8],
                                   (ff_hi[:, f, 128 * t:128 * t + 128], ff_lo[:, f, 128 * t:128 * t + 128]),
                                   [part[:, 1 + f, 512 * half:512 * half + 512] for part in (w_hi, w_lo)], f == 0, f == 1)
                    last.then_inc(d_summed, 1)


def _inputs(inputs):
    f = lambda n: np.ascontiguousarray(inputs[n])
    g_q, g_k = f("g_q")[0], f("g_k")[0]
    c = np.concatenate([f("c_prompt"), f("c_sample")]).reshape(16, 128)
    rows = [c, f("g_attn").reshape(8, 128), f("g_ffn").reshape(8, 128), f("g_fout").reshape(4, 128),
            f("g_aout").reshape(4, 128), np.concatenate([g_q, g_q])[None], np.concatenate([g_k, g_k])[None],
            f("b_ada").reshape(48, 128)]
    rp = f("rpb")[0]
    pad = np.zeros((RP_ROWS, N_HEADS, RP_COLS), np.float32)
    pad[4:4 + 2 * WIN_ROWS - 1, :, 16:16 + 2 * WIN_COLS - 1] = rp.transpose(1, 0, 2)
    return {
        "x_prompt": f("x_prompt")[0], "x_sample": f("x_sample")[0], "c_rows": c, "w_ada": f("w_ada")[0],
        "vec_rows": np.concatenate(rows), "w_in": f("w_in")[0], "w_fmix": f("w_fmix")[0], "rpb_pad": pad.reshape(-1),
        "masks": _masks(), "dft_c": _dft_channels(), "dft_t1": _dft_tokens(T_SAMPLE), "dft_t0": _dft_tokens(T_PROMPT),
        "w_o": f("w_o")[0], "w_gate": f("w_gate")[0], "w_up": f("w_up")[0], "w_down": f("w_down")[0],
    }


def _masks():
    out = np.full((128, NB, MASK_COLS), MASKED, np.float32)
    for b in range(NB):
        at = 0
        for c in range(NCH):
            rows = 8 if c == 0 else 16
            for qi in range(QROWS):
                i = qi + (QROWS if c == 2 else 0)
                r0 = min(max(i - WIN_ROWS // 2, 0), rows - WIN_ROWS)
                for qc in range(QCOLS):
                    col = QCOLS * b + qc
                    c0 = min(max(col - WIN_COLS // 2, 0), GRID_W - WIN_COLS)
                    for r in range(r0, r0 + WIN_ROWS):
                        k = at + (r - KEY_ROW0[c]) * KCOLS + c0 - KEY_COL[b]
                        out[qi * QCOLS + QCOLS - 1 - qc, b, k:k + WIN_COLS] = 0.0
            at += KEY_ROWS[c] * KCOLS
    return out.reshape(128, NB * MASK_COLS)


def _dft_channels():
    n = np.arange(128)
    a = 2 * np.pi * ((n[:, None] * n) % 128) / 128
    return np.concatenate([np.cos(a), np.sin(a)], 1).astype(np.float32) / np.float32(128 ** 0.5)


def _dft_tokens(t):
    n, k = np.arange(t), np.arange(t // 2)
    a = 2 * np.pi * ((n[:, None] * k) % t) / t
    return (np.stack([np.cos(a), np.sin(a)]) / t ** 0.5).astype(np.float32)


def kernel(**inputs):
    import concourse.bacc as bacc
    from concourse.bass_utils import run_bass_kernel_spmd

    nc = bacc.Bacc("TRN2", target_bir_lowering=False, num_devices=1)
    arrays, args = {}, {}
    for name, a in _inputs(inputs).items():
        arrays[f"in_{name}"] = a
        args[name] = nc.dram_tensor(f"in_{name}", a.shape, mybir.dt.from_np(a.dtype), kind="ExternalInput").ap()
    args["u_scratch"] = nc.dram_tensor("u_scratch", (D_FOURIER, T), F32).ap()
    for name, t in (("y_prompt", T_PROMPT), ("y_sample", T_SAMPLE)):
        args[name] = nc.dram_tensor(name, (1, t, D), F32, kind="ExternalOutput").ap()
    layer(nc, **args)
    r = run_bass_kernel_spmd(nc, [arrays], core_ids=[0])
    return r.results[0]["y_prompt"], r.results[0]["y_sample"]
```

```python
import numpy as np
from contextlib import ExitStack

import concourse.bass as bass
from concourse import mybir

F32, F32R = mybir.dt.float32, mybir.dt.float32r
ALU = mybir.AluOpType
ACT = mybir.ActivationFunctionType
AX = mybir.AxisListType

D = 1024
KT = D // 128
T_PROMPT, T_SAMPLE = 512, 1024
T = T_PROMPT + T_SAMPLE
CH = 512
NCH = T // CH
TT = T // 128
REQ = [0, 1, 1]
D_FOURIER = D // 2
FT = D_FOURIER // 128
HEAD = 64
N_HEADS = D_FOURIER // HEAD
D_FF = 2816
FF = D_FF // 128
GRID_W = 64
WIN_ROWS, WIN_COLS = 8, 16
N_MOD = 6
EPS = 1e-6

QROWS, QCOLS, KCOLS = 8, 16, 32
NB = GRID_W // QCOLS
KEY_COL = [min(max(QCOLS * b - WIN_COLS // 2, 0), GRID_W - KCOLS) for b in range(NB)]
KEY_ROWS = [8, 12, 12]
KEY_ROW0 = [0, 0, 4]
KEY_TOKEN0 = [0, T_PROMPT, T_PROMPT + 4 * GRID_W]
V_TILE0 = [0, 2, 3]
NVT = 6
BIAS_E, BIAS_X = 16, 48
RP_ROWS, RP_COLS = 23, 63
MASKED = 1e30
MASK_COLS = sum(KEY_ROWS) * KCOLS
UNITS = NB * NCH * 2

BASE = 16512
H_LO, H_HI = BASE, BASE + 49152
X_AT = BASE + 98304
GATE2_AT = BASE + 147456
REST = BASE + 155648
SQ_SUM_AT = BASE + 197888
KEEP = BASE + 210176
END = BASE + 212832


def after(eng, s, count):
    if not (isinstance(count, int) and count <= 0):
        eng.wait_ge(s, count)


def rounds(eng, first, end, body):
    body(first)
    if end - first > 1:
        with eng.Fori(first + 1, end) as j:
            body(j)


def layer(nc, x_prompt, x_sample, c_rows, w_ada, vec_rows, w_in, w_fmix, rpb_pad, masks, dft_c, dft_t1,
          dft_t0, w_o, w_gate, w_up, w_down, u_scratch, y_prompt, y_sample):
    ctx = ExitStack()
    with ctx:
        def at(name, shape, dt, off):
            size = 4 * int(np.prod(shape[1:]))
            assert off % 32 == 0 and off >= BASE and off + size <= END, (name, off - BASE, size)
            made[name] = nc.alloc_sbuf_tensor_at(name, shape, dt, offset=off)
            return made[name]
        made = {}

        def sem(name):
            return ctx.enter_context(nc.semaphore(name))

        banks = ctx.enter_context(nc.psum_tensor("banks", [128, 8, 512], F32))

        ident = at("ident", [128, 128], F32, KEEP)
        ones_head = at("ones_head", [128, 128], F32R, KEEP + 512)
        ones_all = at("ones_all", [128, 128], F32R, KEEP + 1024)
        vec = at("vec", [128, 96], F32, KEEP + 1536)
        mod = at("mod", [128, N_MOD * KT, 2], F32, KEEP + 1920)
        coef = at("coef", [128, 2, KT, 2], F32, KEEP + 2304)
        stat = at("stat", [128, 2, TT], F32, KEEP + 2432)
        eps_t = at("eps_t", [128, 1], F32, KEEP + 2528)
        gq8 = at("gq8", [128, 1], F32, KEEP + 2560)
        V_C, V_GATTN, V_GFFN, V_GF, V_GA, V_GQ, V_GK, V_BADA = 0, 16, 24, 32, 36, 40, 41, 42

        h_hi = at("h_hi", [128, KT, T], F32R, H_HI)
        h_lo = at("h_lo", [128, KT, T], F32R, H_LO)

        def mm3(pe, out, lhs, rhs, start, stop):
            pe.matmul(out, lhs[0], rhs[0], start=start, stop=False)
            pe.matmul(out, lhs[0], rhs[1], start=False, stop=False)
            return pe.matmul(out, lhs[1], rhs[0], start=False, stop=stop)

        first_stage(nc, at, sem, banks, locals())
        projections(nc, at, sem, banks, locals())
        attention(nc, at, sem, banks, locals())
        fourier(nc, at, sem, banks, locals())
        second_half(nc, at, sem, banks, locals())


def first_stage(nc, at, sem, banks, g):
    x_prompt, x_sample, c_rows, w_ada, vec_rows = (g[k] for k in ("x_prompt", "x_sample", "c_rows", "w_ada", "vec_rows"))
    ident, ones_head, ones_all, vec, mod, coef, stat, eps_t, gq8, h_hi, h_lo = (
        g[k] for k in ("ident", "ones_head", "ones_all", "vec", "mod", "coef", "stat", "eps_t", "gq8", "h_hi", "h_lo"))
    V_C, V_BADA, V_GQ = g["V_C"], g["V_BADA"], g["V_GQ"]
    NV = V_BADA + N_MOD * KT
    AC = 12

    def groups(j):
        return range(3 * (j - 4), 3 * (j - 3)) if j >= 4 else ()
    x = at("x_first", [128, TT, D], F32, X_AT)
    ada = at("ada", [128, 3, KT, 512], F32, REST)
    mrow = at("mrow", [128, 2, 512], F32, GATE2_AT)
    junk = at("junk", [128, D], F32, GATE2_AT + 4096)
    t_ring = at("t_first", [128, 2, CH], F32, REST + 49152)
    vrow = at("vrow", [128, 128], F32, REST + 53248)
    silu_c = at("silu_c", [128, 16], F32, KEEP + 2592)

    x_in = [sem(f"x_in{c}") for c in range(NCH)]
    vec_in, ada_in = sem("vec_in"), [sem(f"ada_in{i}") for i in range(3)]
    ident_zero, ident_ready, ones_ready = sem("ident_zero"), sem("ident_ready"), sem("ones_ready")
    vec_turned, vec_ready, silu_ready = sem("vec_turned"), sem("vec_ready"), sem("silu_ready")
    mod_summed, mod_row, mod_turned = sem("mod_summed"), sem("mod_row"), sem("mod_turned")
    mod_ready, coef_ready = sem("mod_ready"), sem("coef_ready")
    squared, rooted, rstd_ready, x_normed = sem("squared"), sem("rooted"), sem("rstd_ready"), sem("x_normed")
    x_turned, t_ready, h_split = sem("x_turned"), sem("t_ready"), sem("h_split")
    h_hi_ready = sem("h_hi_ready")

    with nc.Block() as block:
        @block.sync
        def _(sp):
            sp.dma_start(vrow[0:NV, :], vec_rows).then_inc(vec_in, 16)
            for j in range(AC):
                if j >= 3:
                    sp.wait_ge(mod_summed, j - 2)
                sp.dma_start(ada[:, j % 3], w_ada[:, 512 * j:512 * j + 512].rearrange("(k p) n -> p k n", p=128)
                             ).then_inc(ada_in[j % 3], 16)

        @block.gpsimd
        def _(pool):
            pool.memset(ident[:], 0.0).then_inc(ident_zero, 1)
            pool.wait_ge(ident_zero, 1)
            pool.affine_select(out=ident[:], in_=ident[:], compare_op=ALU.not_equal, fill=1.0, base=0,
                               pattern=[[-1, 128]], channel_multiplier=1).then_inc(ident_ready, 1)

        @block.scalar
        def _(act):
            for c in range(NCH):
                src = x_prompt if c == 0 else x_sample[CH * (c - 1):CH * c]
                act.dma_start(x[:, 4 * c:4 * c + 4], src.rearrange("(t p) n -> p t n", p=128)).then_inc(x_in[c], 16)
            act.wait_ge(vec_turned, 1)
            act.activation(silu_c[:], banks[:, 2, V_C:V_C + 16], ACT.Silu).then_inc(silu_ready, 1)
            act.wait_ge(ones_ready, 1)
            for c in range(NCH):
                act.wait_ge(x_in[c], 16)
                for t in range(4 * c, 4 * c + 4):
                    if t:
                        act.wait_ge(squared, t)
                    act.activation(junk[:], x[:, t], ACT.Square, accum_out=stat[:, 0, t:t + 1]).then_inc(squared, 1)
                act.wait_ge(squared, 4 * c + 4)
                act.activation(stat[:, 0, 4 * c:4 * c + 4], stat[:, 0, 4 * c:4 * c + 4], ACT.Sqrt,
                               scale=1.0 / D, bias=eps_t[:]).then_inc(rooted, 1)
            act.wait_ge(coef_ready, 1)
            for n in range(NCH * KT):
                c, k = divmod(n, KT)
                act.wait_ge(x_turned, n + 1)
                if n >= 2:
                    act.wait_ge(h_split, n - 1)
                act.activation(t_ring[:, n % 2], banks[:, 4 + n % 4], ACT.Identity, scale=coef[:, 0, k, REQ[c]:REQ[c] + 1],
                               bias=mod[:, k, REQ[c]:REQ[c] + 1]).then_inc(t_ready, 1)

        @block.vector
        def _(dve):
            dve.memset(ones_head[:].bitcast(F32), 0.0).then_inc(mod_row, 1)
            dve.wait_ge(mod_row, 1)
            dve.memset(ones_head[0:64, 0:64].bitcast(F32), 1.0)
            dve.memset(ones_head[64:128, 64:128].bitcast(F32), 1.0)
            dve.memset(ones_all[:].bitcast(F32), 1.0)
            dve.memset(eps_t[:], EPS).then_inc(ones_ready, 1)
            dve.wait_ge(vec_turned, 1)
            dve.wait_ge(silu_ready, 1)
            dve.tensor_copy(vec[:, 0:NV], banks[:, 2, 0:NV]).then_inc(vec_ready, 1)
            dve.wait_ge(vec_ready, 1)
            dve.tensor_scalar(gq8[:], vec[:, V_GQ:V_GQ + 1], -float(HEAD) ** -0.5, None, ALU.mult).then_inc(vec_ready, 1)

            def norm_rows(c):
                dve.wait_ge(rooted, c + 1)
                dve.reciprocal(stat[:, 1, 4 * c:4 * c + 4], stat[:, 0, 4 * c:4 * c + 4]).then_inc(rstd_ready, 1)
                dve.wait_ge(rstd_ready, c + 1)
                for t in range(4 * c, 4 * c + 4):
                    dve.tensor_scalar(x[:, t], x[:, t], stat[:, 1, t:t + 1], None, ALU.mult).then_inc(x_normed, 1)

            def mod_part(a, b, n):
                dve.tensor_tensor(mod[:, a:b], banks[:, 3, 2 * a:2 * b].rearrange("p (j r) -> p j r", r=2),
                                  bass.AP(vec, V_BADA + a, [[96, 128], [1, b - a], [0, 2]]), ALU.add).then_inc(mod_ready, 1)
                dve.wait_ge(mod_ready, n)

            def gains(which, tile0, gain0, n):
                gain = bass.AP(vec, gain0, [[96, 128], [1, KT], [0, 2]])
                dve.scalar_tensor_tensor(coef[:, which], mod[:, tile0:tile0 + KT], 1.0, gain, ALU.add, ALU.mult
                                         ).then_inc(coef_ready, 1)

            def split(n):
                c, k = divmod(n, KT)
                dve.wait_ge(t_ready, n + 1)
                hi, lo = (h[:, k, CH * c:CH * c + CH] for h in (h_hi, h_lo))
                dve.tensor_copy(hi, t_ring[:, n % 2]).then_inc(h_hi_ready, 1)
                dve.wait_ge(h_hi_ready, n + 1)
                dve.tensor_tensor(lo, t_ring[:, n % 2], hi.bitcast(F32), ALU.subtract).then_inc(h_split, 1)

            for j in range(AC):
                dve.wait_ge(mod_summed, j + 1)
                if j >= 2:
                    dve.wait_ge(mod_turned, j - 1)
                dve.tensor_copy(mrow[0:2, j % 2], banks[0:2, j % 2]).then_inc(mod_row, 1)
                if j < NCH:
                    norm_rows(j)
                if j == 3:
                    dve.wait_ge(mod_turned, 4)
                    mod_part(0, 16, 1)
                    gains(0, 8, g["V_GATTN"], 1)
                for n in groups(j):
                    split(n)
            dve.wait_ge(mod_turned, AC)
            mod_part(16, 48, 2)
            gains(1, 32, g["V_GFFN"], 2)

        @block.tensor
        def _(pe):
            pe.wait_ge(ident_ready, 1)
            pe.wait_ge(vec_in, 16)
            pe.transpose(banks[:, 2, 0:NV], vrow[0:NV, :], ident[0:NV, 0:NV]).then_inc(vec_turned, 1)
            pe.wait_ge(silu_ready, 1)

            def turn_mod(j):
                pe.wait_ge(mod_row, j + 2)
                for i in range(4):
                    a = 8 * j + 2 * i
                    last = pe.transpose(banks[:, 3, a:a + 2], mrow[0:2, j % 2, 128 * i:128 * i + 128], ident[0:2, 0:2])
                last.then_inc(mod_turned, 1)

            def turn_x(n):
                c, k = divmod(n, KT)
                pe.wait_ge(x_normed, 4 * c + 4)
                if n >= 4:
                    pe.wait_ge(t_ready, n - 3)
                for i in range(4):
                    last = pe.transpose(banks[:, 4 + n % 4, 128 * i:128 * i + 128],
                                        x[:, 4 * c + i, 128 * k:128 * k + 128], ident[:])
                last.then_inc(x_turned, 1)

            for j in range(AC):
                pe.wait_ge(ada_in[j % 3], 16 * (j // 3 + 1))
                if j >= 2:
                    pe.wait_ge(mod_row, j)
                for k in range(KT):
                    last = pe.matmul(banks[0:2, j % 2], silu_c[:, V_C + k:V_C + k + 9:8], ada[:, j % 3, k],
                                     start=(k == 0), stop=(k == KT - 1))
                last.then_inc(mod_summed, 1)
                if j >= 1 and j != 4:
                    if j == 5:
                        pe.wait_ge(mod_ready, 1)
                    turn_mod(j - 1)
                if j == 3:
                    turn_mod(3)
                for n in groups(j):
                    turn_x(n)
            turn_mod(AC - 1)


def projections(nc, at, sem, banks, g):
    w_in, u_scratch, h_hi, h_lo, vec, gq8, ones_head, eps_t, mm3 = (
        g[k] for k in ("w_in", "u_scratch", "h_hi", "h_lo", "vec", "gq8", "ones_head", "eps_t", "mm3"))
    V_GK = g["V_GK"]
    z = at("z", [128, 3 * FT * T], F32, X_AT)
    W = X_AT + 73728
    w_hi = at("win_hi", [128, 2, KT, 128], F32R, W)
    w_lo = at("win_lo", [128, 2, KT, 128], F32R, W + 8192)
    w_raw = at("win_raw", [128, 2, KT, 128], F32, W + 8192)
    u_stage = at("u_stage", [128, 2, CH], F32, W + 16384)
    sq = at("sq", [128, 2, CH], F32, W + 20480)
    sq_hi = at("sq_hi", [128, 2, CH], F32R, W + 24576)
    sq_lo = at("sq_lo", [128, 2, CH], F32R, W + 28672)
    rms = at("rms", [128, 2, CH], F32, W + 32768)

    w_in_s = [sem(f"win_in{s}") for s in range(2)]
    w_hi_s = [sem(f"win_hi_ready{s}") for s in range(2)]
    w_ready = [sem(f"win_ready{s}") for s in range(2)]
    z_summed = [sem(f"z_summed{b}") for b in range(6)]
    bank_free = [sem(f"z_bank_free{b}") for b in range(6)]
    u_stored = [sem(f"u_stored{s}") for s in range(2)]
    sq_hi_s, sq_lo_s = sem("sq_hi_s"), sem("sq_lo_s")
    ss_summed, rms_ready, rinv_ready, qk_normed = sem("ss_summed"), sem("rms_ready"), sem("rinv_ready"), sem("qk_normed")
    J_U, J_QK, J_V = FT // 2, 3 * FT // 2, 2 * FT

    with nc.Block() as block:
        @block.sync
        def _(sp):
            def load(j, s):
                sp.dma_start(w_raw[:, s], w_in[:, bass.ds((2 * j + s) * 128, 128)].rearrange("(k p) n -> p k n", p=128)
                             ).then_inc(w_in_s[s], 16)
            load(0, 0)
            load(0, 1)
            with sp.Fori(1, J_V) as j:
                for s in range(2):
                    sp.wait_ge(z_summed[3 * s + 2], j)
                    load(j, s)

        @block.gpsimd
        def _(pool):
            def store(j):
                for i in range(6):
                    s, c = divmod(i, NCH)
                    pool.wait_ge(bank_free[i], j + 1)
                    pool.dma_start(u_scratch[bass.ds((2 * j + s) * 128, 128), CH * c:CH * c + CH],
                                   u_stage[:, i % 2]).then_inc(u_stored[i % 2], 16)

            def sq_lows(j):
                for i in range(6):
                    n = 6 * j + i
                    pool.wait_ge(sq_hi_s, n + 1)
                    after(pool, ss_summed, n - 1 if i >= 2 else 6 * j)
                    pool.tensor_tensor(sq_lo[:, i % 2], sq[:, i % 2], sq_hi[:, i % 2].bitcast(F32), ALU.subtract
                                       ).then_inc(sq_lo_s, 1)
            rounds(pool, 0, J_U, store)
            rounds(pool, 0, J_QK - J_U, sq_lows)
            for s in range(2):
                pool.wait_ge(u_stored[s], 16 * 3 * J_U)

        def split_hi(act, j, s):
            act.wait_ge(w_in_s[s], 16 * j + 16)
            act.activation(w_hi[:, s], w_raw[:, s], ACT.Copy).then_inc(w_hi_s[s], 1)

        def split_lo(dve, j, s):
            dve.wait_ge(w_hi_s[s], j + 1)
            dve.tensor_tensor(w_lo[:, s], w_raw[:, s], w_hi[:, s].bitcast(F32), ALU.subtract).then_inc(w_ready[s], 1)

        def z_at(j, s, c):
            return z[:, bass.ds(((2 * (j - J_U) + s) * NCH + c) * CH, CH)]

        @block.scalar
        def _(act):
            def evacuate(j, i, kind):
                s, c = divmod(i, NCH)
                act.wait_ge(z_summed[i], j + 1)
                if kind == "u":
                    after(act, u_stored[i % 2], 16 * (3 * j + i // 2))
                    act.activation(u_stage[:, i % 2], banks[:, i], ACT.Copy).then_inc(bank_free[i], 1)
                elif kind == "v":
                    act.activation(z_at(j, s, c), banks[:, i], ACT.Copy).then_inc(bank_free[i], 1)
                else:
                    n = 6 * (j - J_U) + i
                    act.activation(z_at(j, s, c), banks[:, i], ACT.Copy)
                    after(act, sq_lo_s, n - 1 if i >= 2 else 6 * (j - J_U))
                    act.activation(sq[:, i % 2], banks[:, i], ACT.Square).then_inc(bank_free[i], 1)

            def root(j, i):
                n = 6 * (j - J_U) + i
                act.wait_ge(ss_summed, n + 1)
                after(act, qk_normed, n - 1 if i >= 2 else 6 * (j - J_U))
                act.activation(rms[:, i % 2], banks[:, 6 + i % 2], ACT.Sqrt, scale=1.0 / HEAD, bias=eps_t[:]
                               ).then_inc(rms_ready, 1)

            def pair(j, kind, more):
                for i in range(6):
                    evacuate(j, i, kind)
                    if kind == "qk" and i:
                        root(j, i - 1)
                    if i % 3 == 2 and more:
                        split_hi(act, j + 1, i // 3)
                if kind == "qk":
                    root(j, 5)
            split_hi(act, 0, 0)
            split_hi(act, 0, 1)
            rounds(act, 0, J_U, lambda j: pair(j, "u", True))
            rounds(act, J_U, J_QK, lambda j: pair(j, "qk", True))
            with act.Fori(J_QK, J_V - 1) as j:
                pair(j, "v", True)
            pair(J_V - 1, "v", False)

        @block.vector
        def _(dve):
            def sq_split(j, i):
                n = 6 * (j - J_U) + i
                dve.wait_ge(bank_free[i], j + 1)
                after(dve, ss_summed, n - 1 if i >= 2 else 6 * (j - J_U))
                dve.tensor_copy(sq_hi[:, i % 2], sq[:, i % 2]).then_inc(sq_hi_s, 1)

            def qk_norm(j, i, gain):
                s, c = divmod(i, NCH)
                n = 6 * (j - J_U) + i
                dve.wait_ge(rms_ready, n + 1)
                dve.reciprocal(rms[:, i % 2], rms[:, i % 2]).then_inc(rinv_ready, 1)
                dve.wait_ge(rinv_ready, n + 1)
                zz = z_at(j, s, c)
                dve.scalar_tensor_tensor(zz, zz, gain, rms[:, i % 2], ALU.mult, ALU.mult).then_inc(qk_normed, 1)

            def splits(j, i):
                if i % 3 == 2:
                    split_lo(dve, j + 1, i // 3)
            split_lo(dve, 0, 0)
            split_lo(dve, 0, 1)
            with dve.Fori(0, J_U) as j:
                for i in range(6):
                    splits(j, i)
            for a, b, gain in ((J_U, J_U + FT // 2, gq8[:]), (J_U + FT // 2, J_QK, vec[:, V_GK:V_GK + 1])):
                def normed(j):
                    for i in range(6):
                        sq_split(j, i)
                        if i:
                            qk_norm(j, i - 1, gain)
                        splits(j, i)
                    qk_norm(j, 5, gain)
                rounds(dve, a, b, normed)
            with dve.Fori(J_QK, J_V - 1) as j:
                for i in range(6):
                    splits(j, i)

        @block.tensor
        def _(pe):
            def tile(j, i):
                s, c = divmod(i, NCH)
                if c == 0:
                    pe.wait_ge(w_ready[s], j + 1)
                after(pe, bank_free[i], j)
                for k in range(KT):
                    last = mm3(pe, banks[:, i], (w_hi[:, s, k], w_lo[:, s, k]),
                               (h_hi[:, k, CH * c:CH * c + CH], h_lo[:, k, CH * c:CH * c + CH]), k == 0, k == KT - 1)
                last.then_inc(z_summed[i], 1)

            def head_sums(j, i):
                n = 6 * (j - J_U) + i
                pe.wait_ge(sq_lo_s, n + 1)
                after(pe, rms_ready, n - 1 if i >= 2 else 6 * (j - J_U))
                pe.matmul(banks[:, 6 + i % 2], ones_head[:], sq_hi[:, i % 2], start=True, stop=False)
                pe.matmul(banks[:, 6 + i % 2], ones_head[:], sq_lo[:, i % 2], start=False, stop=True
                          ).then_inc(ss_summed, 1)

            def tiles(j, i, qk):
                tile(j, i)
                if qk and i:
                    head_sums(j, i - 1)
            def plain(j):
                for i in range(6):
                    tiles(j, i, False)

            def normed(j):
                for i in range(6):
                    tiles(j, i, True)
                head_sums(j, 5)
            rounds(pe, 0, J_U, plain)
            rounds(pe, J_U, J_QK, normed)
            with pe.Fori(J_QK, J_V) as j:
                for i in range(6):
                    tiles(j, i, False)


def attention(nc, at, sem, banks, g):
    z, rpb_pad, masks, ident = g["made"]["z"], g["rpb_pad"], g["masks"], g["ident"]
    bias = at("bias", [128, N_HEADS * BIAS_E * BIAS_X], F32, BASE + 172032)
    mask = at("mask", [128, NB * MASK_COLS], F32, BASE + 24576)
    v_tok = at("v_tok", [128, NB * NVT, 128], F32, BASE + 40960)
    v_pair = at("v_pair", [128, NB, T // 2], F32, BASE + 53248)
    q_pair = at("q_pair", [128, 2, NCH, NB, 128], F32, BASE + 65536)
    m_ring = at("m_ring", [128, 4, 384], F32, BASE + 77824)
    s_ring = at("s_ring", [128, 4, 384], F32, BASE + 83968)
    pt_ring = at("pt_ring", [128, 3, 384], F32, BASE + 90112)
    stats = at("stats", [128, 3, UNITS], F32, BASE + 94720)
    a_out = at("a_out", [128, FT * T], F32, H_LO)
    bias_pair = at("bias_pair", [128, BIAS_E, 2, BIAS_X], F32, BASE + 196608)

    bias_in, mask_in = sem("bias_in"), sem("mask_in")
    q_zeroed, q_staged, v_staged, v_turned, v_ready = (sem(n) for n in ("q_zeroed", "q_staged", "v_staged", "v_turned", "v_ready"))
    q_staged2, v_ready2, bias_staged = sem("q_staged2"), sem("v_ready2"), sem("bias_staged")
    masked_bias, qk_done, scored, exped, recip_done, normed = (
        sem(n) for n in ("masked_bias", "qk_done", "scored", "exped", "recip_done", "normed"))
    p_turned, pt_copied, pv_done, o_copied = (sem(n) for n in ("p_turned", "pt_copied", "pv_done", "o_copied"))

    def unit(u):
        b, c, hh = u // 6, u % 6 // 2, u % 2
        return b, c, hh, KEY_ROWS[c], KEY_ROWS[c] * KCOLS

    def since(p, u, back, per=UNITS):
        return per * p + max(u - back + 1, 0)

    with nc.Block() as block:
        @block.sync
        def _(sp):
            for i in range(QROWS):
                src = bass.AP(rpb_pad.tensor, (7 - i) * N_HEADS * RP_COLS,
                              [[1, QCOLS], [RP_COLS, BIAS_E * N_HEADS], [1, BIAS_X]])
                sp.dma_start(bias[QCOLS * i:QCOLS * i + QCOLS, :].rearrange("p (eh x) -> p eh x", x=BIAS_X),
                             src).then_inc(bias_in, 16)
            sp.dma_start(mask[:], masks).then_inc(mask_in, 16)

        @block.gpsimd
        def _(pool):
            pool.wait_ge(mask_in, 16)
            def head_pair(p):
                pool.wait_ge(bias_staged, p + 1)
                for u in range(UNITS):
                    b, c, hh, rows, n = unit(u)
                    after(pool, scored, since(p, u, 4))
                    e0 = 0 if c == 2 else 4
                    x0 = KEY_COL[b] - QCOLS * b + 16
                    tab = bias_pair[:, e0:e0 + rows, hh, x0:x0 + KCOLS]
                    k0 = b * MASK_COLS + sum(KEY_ROWS[:c]) * KCOLS
                    pool.tensor_tensor(m_ring[:, u % 4, 0:n].rearrange("p (e x) -> p e x", e=rows),
                                       mask[:, k0:k0 + n].rearrange("p (e x) -> p e x", e=rows), tab, ALU.subtract
                                       ).then_inc(masked_bias, 1)
            rounds(pool, 0, FT, head_pair)

        @block.scalar
        def _(act):
            act.wait_ge(q_zeroed, 2)
            def head_pair(p):
                after(act, qk_done, UNITS * p)
                for c in range(NCH):
                    src = z[64:128, bass.ds(p * T + c * CH, CH)].rearrange("p (r b w) -> p b r w", b=NB, w=QCOLS)
                    act.activation(q_pair[64:128, 1, c].rearrange("p b (r w) -> p b r w", w=QCOLS)[:, :, :, ::-1], src, ACT.Copy
                                   ).then_inc(q_staged2, 1)
                for i in range(0, 6, 2):
                    act.wait_ge(v_turned, 6 * p + i + 1)
                    act.activation(v_tok[:, 4 * i:4 * i + 4], banks[:, 6].rearrange("p (t f) -> p t f", f=128), ACT.Copy
                                   ).then_inc(v_ready, 1)

                def exp(u):
                    n = unit(u)[4]
                    after(act, scored, since(p, u, 0))
                    act.activation(s_ring[:, u % 4, 0:n], s_ring[:, u % 4, 0:n], ACT.Exp, scale=-1.0,
                                   bias=stats[:, 0, u:u + 1], accum_out=stats[:, 1, u:u + 1]).then_inc(exped, 1)

                def copy_pt(u):
                    n = unit(u)[4]
                    after(act, p_turned, since(p, u, 0))
                    after(act, pv_done, since(p, u, 3))
                    act.activation(pt_ring[:, u % 3, 0:n], banks[:, 2 + u % 2, 0:n], ACT.Copy).then_inc(pt_copied, 1)

                def copy_o(v):
                    b, c = unit(2 * v)[:2]
                    after(act, pv_done, since(p, 2 * v + 1, 0))
                    dst = a_out[:, bass.ds(p * T + c * CH, CH)].rearrange("p (r b w) -> p b r w", b=NB, w=QCOLS)[:, b]
                    act.activation(dst, banks[:, 4 + v % 2, 0:128].rearrange("p (r w) -> p r w", w=QCOLS)[:, :, ::-1], ACT.Copy
                                   ).then_inc(o_copied, 1)

                for s in range(UNITS + 5):
                    if s < UNITS:
                        exp(s)
                    if 0 <= s - 3 < UNITS:
                        copy_pt(s - 3)
                    if s >= 6 and s % 2 == 0:
                        copy_o((s - 6) // 2)
            rounds(act, 0, FT, head_pair)

        @block.vector
        def _(dve):
            dve.memset(q_pair[64:128, 0], 0.0).then_inc(q_zeroed, 1)
            dve.memset(q_pair[0:64, 1], 0.0).then_inc(q_zeroed, 1)
            dve.wait_ge(bias_in, 16 * QROWS)
            def head_pair(p):
                after(dve, masked_bias, UNITS * p)
                dve.tensor_copy(bias_pair[:].rearrange("p e h x -> p e (h x)"), bias[:].rearrange(
                    "p (e hx) -> p e hx", e=BIAS_E)[:, :, bass.ds(2 * BIAS_X * p, 2 * BIAS_X)]).then_inc(bias_staged, 1)
                after(dve, v_turned, 6 * p)
                for b in range(NB):
                    src = z[:, bass.ds((2 * FT + p) * T, T)].rearrange("p (r w) -> p r w", w=GRID_W)[
                        :, :, KEY_COL[b]:KEY_COL[b] + KCOLS]
                    dve.tensor_copy(v_pair[:, b].rearrange("p (r w) -> p r w", w=KCOLS), src).then_inc(v_staged, 1)
                after(dve, qk_done, UNITS * p)
                for c in range(NCH):
                    src = z[0:64, bass.ds(p * T + c * CH, CH)].rearrange("p (r b w) -> p b r w", b=NB, w=QCOLS)
                    dve.tensor_copy(q_pair[0:64, 0, c].rearrange("p b (r w) -> p b r w", w=QCOLS)[:, :, :, ::-1], src
                                    ).then_inc(q_staged, 1)
                def ready(u):
                    after(dve, qk_done, since(p, u, 0))
                    after(dve, masked_bias, since(p, u, 0))
                    after(dve, p_turned, since(p, u, 4))

                for i in range(1, 6, 2):
                    dve.wait_ge(v_turned, 6 * p + i + 1)
                    if i == 5:
                        ready(0)
                        ready(1)
                    dve.tensor_copy(v_tok[:, 4 * i:4 * i + 4], banks[:, 7].rearrange("p (t f) -> p t f", f=128)
                                    ).then_inc(v_ready2, 1)

                def score(u):
                    n = unit(u)[4]
                    dve.tensor_tensor_reduce(s_ring[:, u % 4, 0:n], banks[:, u % 2, 0:n], m_ring[:, u % 4, 0:n], 1.0,
                                             3e38, ALU.add, ALU.min, stats[:, 0, u:u + 1]).then_inc(scored, 1)

                def norm(u):
                    n = unit(u)[4]
                    after(dve, exped, since(p, u, 0))
                    dve.reciprocal(stats[:, 2, u:u + 1], stats[:, 1, u:u + 1]).then_inc(recip_done, 1)
                    after(dve, recip_done, since(p, u, 0))
                    if u + 2 < UNITS:
                        ready(u + 2)
                    dve.tensor_scalar(s_ring[:, u % 4, 0:n], s_ring[:, u % 4, 0:n], stats[:, 2, u:u + 1], None, ALU.mult
                                      ).then_inc(normed, 1)

                for s in range(UNITS + 2):
                    if s >= 2:
                        norm(s - 2)
                    if s < UNITS:
                        score(s)
            rounds(dve, 0, FT, head_pair)

        @block.tensor
        def _(pe):
            def head_pair(p):
                for i in range(6):
                    if i >= 2:
                        pe.wait_ge((v_ready, v_ready2)[i % 2], 3 * p + i // 2)
                    pe.wait_ge(v_staged, NB * p + (4 * i + 3) // NVT + 1)
                    for t in range(4 * i, 4 * i + 4):
                        b, vt = divmod(t, NVT)
                        last = pe.transpose(banks[:, 6 + i % 2, 128 * (t % 4):128 * (t % 4) + 128],
                                            v_pair[:, b, 128 * vt:128 * vt + 128], ident[:])
                    last.then_inc(v_turned, 1)
                pe.wait_ge(q_staged, NCH * p + NCH)
                pe.wait_ge(q_staged2, NCH * p + NCH)

                def scores(u):
                    b, c, hh, rows, n = unit(u)
                    after(pe, scored, since(p, u, 2))
                    keys = z[:, bass.ds((FT + p) * T + KEY_TOKEN0[c], rows * GRID_W)].rearrange(
                        "p (r w) -> p r w", w=GRID_W)[:, :, KEY_COL[b]:KEY_COL[b] + KCOLS]
                    pe.matmul(banks[:, u % 2, 0:n], q_pair[:, hh, c, b], keys, start=True, stop=True).then_inc(qk_done, 1)

                def turn(u):
                    rows = unit(u)[3]
                    after(pe, normed, since(p, u, 0))
                    after(pe, pt_copied, since(p, u, 2))
                    for j in range(rows // 4):
                        last = pe.transpose(banks[:, 2 + u % 2, 128 * j:128 * j + 128],
                                            s_ring[:, u % 4, 128 * j:128 * j + 128], ident[:])
                    last.then_inc(p_turned, 1)

                def values(u):
                    b, c, hh, rows, n = unit(u)
                    v = u // 2
                    if u == 0:
                        pe.wait_ge(v_ready, 3 * p + 3)
                        pe.wait_ge(v_ready2, 3 * p + 3)
                    after(pe, pt_copied, since(p, u, 0))
                    after(pe, o_copied, since(p, v, 2, UNITS // 2))
                    for j in range(rows // 4):
                        last = pe.matmul(banks[64 * hh:64 * hh + 64, 4 + v % 2, 0:128],
                                         v_tok[:, b * NVT + V_TILE0[c] + j, 64 * hh:64 * hh + 64],
                                         pt_ring[:, u % 3, 128 * j:128 * j + 128], start=(j == 0), stop=(j == rows // 4 - 1))
                    last.then_inc(pv_done, 1)

                scores(0)
                for s in range(UNITS + 4):
                    if s + 1 < UNITS:
                        scores(s + 1)
                    if 0 <= s - 3 < UNITS:
                        turn(s - 3)
                    if s >= 4:
                        values(s - 4)
            rounds(pe, 0, FT, head_pair)


def fourier(nc, at, sem, banks, g):
    u_scratch, w_fmix, dft_c, dft_t1, dft_t0 = (g[k] for k in ("u_scratch", "w_fmix", "dft_c", "dft_t1", "dft_t0"))
    a_out, vec, h_hi, h_lo = g["made"]["a_out"], g["vec"], g["h_hi"], g["h_lo"]
    V_GF, V_GA = g["V_GF"], g["V_GA"]
    f_out = at("f_out", [128, FT, T], F32, H_LO + 24576)
    u = at("u", [128, FT, T], F32, H_HI + 24576)
    pq = at("pq", [128, TT, FT, 256], F32, BASE + 98304)
    tab1 = at("tab1", [128, 2, T_SAMPLE // 128, T_SAMPLE // 2], F32, BASE + 147456)
    tab0 = at("tab0", [128, 2, T_PROMPT // 128, T_PROMPT // 2], F32, BASE + 180224)
    maps = at("maps", [128, FT, 256], F32, BASE + 188416)
    f_sq = at("f_sq", [128, T_SAMPLE], F32, BASE + 188416)
    b_ring = at("b_ring", [128, 2, CH], F32, BASE + 192512)
    wf = at("wf", [128, FT, 128], F32, BASE + 192512)
    cs = at("cs", [128, 256], F32, BASE + 194560)
    alt = at("alt", [128, 3, FT, 2], F32, BASE + 196608)
    sq_sum = at("sq_sum", [128, 2, T], F32, SQ_SUM_AT)
    REQS = [(0, T_PROMPT, tab0), (T_PROMPT, T_SAMPLE, tab1)]

    u_in = [sem(f"u_in{c}") for c in range(NCH)]
    wf_in, cs_in, tab0_in, tab1_in = (sem(n) for n in ("wf_in", "cs_in", "tab0_in", "tab1_in"))
    maps_summed, maps_ready, alt_sums, alt_ready = (sem(n) for n in ("maps_summed", "maps_ready", "alt_sums", "alt_ready"))
    pq_summed, pq_act, pq_dve, half_summed, half_ready = (
        sem(n) for n in ("pq_summed", "pq_act", "pq_dve", "half_summed", "half_ready"))
    ab_summed, b_ready, f_ready = sem("ab_summed"), sem("b_ready"), sem("f_ready")
    a_squared, a_sq_added, a_hi_s, a_split = (sem(n) for n in ("a_squared", "a_sq_added", "a_hi_s", "a_split"))
    f_squared, f_sq_added, f_hi_s, f_split = (sem(n) for n in ("f_squared", "f_sq_added", "f_hi_s", "f_split"))

    def a_part(n):
        i, c = divmod(n, NCH)
        return i, slice(CH * c, CH * c + CH), a_out[:, T * i + CH * c:T * i + CH * c + CH]

    with nc.Block() as block:
        @block.sync
        def _(sp):
            sp.dma_start(cs[:], dft_c).then_inc(cs_in, 16)
            sp.dma_start(wf[:], w_fmix.rearrange("g c d -> c g d")).then_inc(wf_in, 16)
            for c in range(NCH):
                cols = slice(CH * c, CH * c + CH)
                sp.dma_start(u[:, :, cols], u_scratch[:, cols].rearrange("(g p) t -> p g t", p=128)).then_inc(u_in[c], 16)
            for half in range(2):
                sp.dma_start(tab0[:, half], dft_t0[half].rearrange("(t p) k -> p t k", p=128)).then_inc(tab0_in, 16)
            for half in range(2):
                sp.dma_start(tab1[:, half], dft_t1[half].rearrange("(t p) k -> p t k", p=128)).then_inc(tab1_in, 16)

        @block.scalar
        def _(act):
            act.wait_ge(maps_summed, 1)
            act.activation(maps[:, 0:2], banks[:, 0].rearrange("p (g n) -> p g n", g=2), ACT.Copy).then_inc(maps_ready, 1)
            act.activation(maps[:, 2:4], banks[:, 1].rearrange("p (g n) -> p g n", g=2), ACT.Copy).then_inc(maps_ready, 1)
            for t in range(TT):
                act.wait_ge(pq_summed, t + 1)
                act.activation(pq[:, t, 0:2], banks[:, 2 * (t % 2)].rearrange("p (g n) -> p g n", g=2), ACT.Copy
                               ).then_inc(pq_act, 1)
                i, cols, part = a_part(t)
                if i and t >= NCH + 2:
                    act.wait_ge(a_sq_added, t - NCH - 1)
                act.activation(sq_sum[:, 0, cols] if i == 0 else b_ring[:, t % 2], part, ACT.Square).then_inc(a_squared, 1)
                act.activation(h_hi[:, i, cols], part, ACT.Copy, scale=vec[:, V_GA + i:V_GA + i + 1]).then_inc(a_hi_s, 1)
            act.wait_ge(a_sq_added, TT - NCH)
            act.wait_ge(half_summed, 1)
            for n in range(2 * FT):
                r, c = divmod(n, FT)
                t0, t, _ = REQS[r]
                k = t // 2
                act.wait_ge(ab_summed, n + 1)
                act.activation(b_ring[:, n % 2, 0:k], banks[:, 5 + 2 * (n % 2), 0:k], ACT.Copy).then_inc(b_ready, 1)
                act.wait_ge(half_ready, 2)
                act.wait_ge(f_ready, n + 1)
                act.activation(h_hi[:, FT + c, t0:t0 + t], f_out[:, c, t0:t0 + t], ACT.Copy,
                               scale=vec[:, V_GF + c:V_GF + c + 1]).then_inc(f_hi_s, 1)
                if n >= 2:
                    act.wait_ge(f_sq_added, (FT - 1) * r + max(c - 1, 0))
                act.activation(sq_sum[:, 1, t0:t0 + t] if c == 0 else f_sq[:, 0:t], f_out[:, c, t0:t0 + t], ACT.Square
                               ).then_inc(f_squared, 1)

        @block.gpsimd
        def _(pool):
            for n in range(NCH, TT):
                cols = a_part(n)[1]
                pool.wait_ge(a_squared, n + 1)
                if n >= 2 * NCH:
                    pool.wait_ge(a_sq_added, n - 2 * NCH + 1)
                pool.tensor_tensor(sq_sum[:, 0, cols], sq_sum[:, 0, cols], b_ring[:, n % 2], ALU.add).then_inc(a_sq_added, 1)
            for n in range(2 * FT):
                r, c = divmod(n, FT)
                t0, t, _ = REQS[r]
                if c:
                    pool.wait_ge(f_squared, n + 1)
                    if c > 1:
                        pool.wait_ge(f_sq_added, (FT - 1) * r + c - 1)
                    pool.tensor_tensor(sq_sum[:, 1, t0:t0 + t], sq_sum[:, 1, t0:t0 + t], f_sq[:, 0:t], ALU.add
                                       ).then_inc(f_sq_added, 1)

        @block.vector
        def _(dve):
            for t in range(TT):
                dve.wait_ge(pq_summed, t + 1)
                dve.tensor_copy(pq[:, t, 2:4], banks[:, 2 * (t % 2) + 1].rearrange("p (g n) -> p g n", g=2)
                                ).then_inc(pq_dve, 1)
                i, cols, part = a_part(t)
                dve.wait_ge(a_squared, t + 1)
                dve.wait_ge(a_hi_s, t + 1)
                dve.scalar_tensor_tensor(h_lo[:, i, cols], part, vec[:, V_GA + i:V_GA + i + 1],
                                         h_hi[:, i, cols].bitcast(F32), ALU.mult, ALU.subtract).then_inc(a_split, 1)
            for c in range(NCH):
                dve.wait_ge(u_in[c], 16)
            for r, (t0, t, _) in enumerate(REQS):
                parts = u[:, :, t0:t0 + t].rearrange("p g (t two) -> p g two t", two=2)
                for odd in range(2):
                    dve.tensor_reduce(alt[:, odd, :, r:r + 1], parts[:, :, odd:odd + 1], AX.X, ALU.add).then_inc(alt_sums, 1)
            dve.wait_ge(alt_sums, 4)
            dve.tensor_tensor(alt[:, 2], alt[:, 0], alt[:, 1], ALU.subtract).then_inc(alt_ready, 1)
            dve.wait_ge(half_summed, 1)
            for r, (t0, t, _) in enumerate(REQS):
                dve.tensor_scalar(f_out[:, :, t0 + t // 2:t0 + t // 2 + 1],
                                  banks[:, 0, 0:2 * FT].rearrange("p (g r) -> p g r", r=2)[:, :, r:r + 1],
                                  t ** -0.5, None, ALU.mult).then_inc(half_ready, 1)

            def f_lo(n):
                r, c = divmod(n, FT)
                t0, t, _ = REQS[r]
                if n == 0:
                    dve.wait_ge(half_ready, 2)
                dve.wait_ge(f_hi_s, n + 1)
                dve.wait_ge(f_squared, n + 1)
                dve.scalar_tensor_tensor(h_lo[:, FT + c, t0:t0 + t], f_out[:, c, t0:t0 + t], vec[:, V_GF + c:V_GF + c + 1],
                                         h_hi[:, FT + c, t0:t0 + t].bitcast(F32), ALU.mult, ALU.subtract).then_inc(f_split, 1)
            for n in range(2 * FT):
                r, c = divmod(n, FT)
                t0, t, _ = REQS[r]
                k = t // 2
                dve.wait_ge(b_ready, n + 1)
                dve.tensor_tensor(f_out[:, c, t0:t0 + k], banks[:, 4 + 2 * (n % 2), 0:k], b_ring[:, n % 2, 0:k], ALU.subtract)
                dve.tensor_tensor(f_out[:, c, t0 + k + 1:t0 + t][:, ::-1], banks[:, 4 + 2 * (n % 2), 1:k],
                                  b_ring[:, n % 2, 1:k], ALU.add).then_inc(f_ready, 1)
                f_lo(n)

        @block.tensor
        def _(pe):
            pe.wait_ge(cs_in, 16)
            pe.wait_ge(wf_in, 16)
            for c in range(FT):
                for half in range(2):
                    at_ = 256 * (c % 2) + 128 * half
                    last = pe.matmul(banks[:, c // 2, at_:at_ + 128], cs[:, 128 * half:128 * half + 128], wf[:, c],
                                     start=True, stop=True)
            last.then_inc(maps_summed, 1)
            pe.wait_ge(maps_ready, 2)
            for t in range(TT):
                if t % 4 == 0:
                    pe.wait_ge(u_in[t // 4], 16)
                if t >= 2:
                    pe.wait_ge(pq_act, t - 1)
                    pe.wait_ge(pq_dve, t - 1)
                for c in range(FT):
                    last = pe.matmul(banks[:, 2 * (t % 2) + c // 2, 256 * (c % 2):256 * (c % 2) + 256],
                                     u[:, c, 128 * t:128 * t + 128], maps[:, c], start=True, stop=True)
                last.then_inc(pq_summed, 1)
            pe.wait_ge(alt_ready, 1)
            pe.wait_ge(pq_act, TT - 1)
            for c in range(FT):
                last = pe.matmul(banks[:, 0, 2 * c:2 * c + 2], maps[:, c, 0:128], alt[:, 2, c], start=True, stop=True)
            last.then_inc(half_summed, 1)
            pe.wait_ge(pq_act, TT)
            pe.wait_ge(pq_dve, TT)
            for n in range(2 * FT):
                r, c = divmod(n, FT)
                t0, t, tab = REQS[r]
                if c == 0:
                    pe.wait_ge((tab0_in, tab1_in)[r], 32)
                if n >= 2:
                    pe.wait_ge(f_ready, n - 1)
                for half in range(2):
                    for i in range(t // 128):
                        last = pe.matmul(banks[:, 4 + 2 * (n % 2) + half, 0:t // 2],
                                         pq[:, t0 // 128 + i, c, 128 * half:128 * half + 128], tab[:, half, i],
                                         start=(i == 0), stop=(i == t // 128 - 1))
                last.then_inc(ab_summed, 1)


def second_half(nc, at, sem, banks, g):
    (x_prompt, x_sample, w_o, w_gate, w_up, w_down, y_prompt, y_sample, mod, coef, ident, ones_all, eps_t, h_hi, h_lo,
     mm3) = (g[k] for k in ("x_prompt", "x_sample", "w_o", "w_gate", "w_up", "w_down", "y_prompt", "y_sample", "mod", "coef",
                            "ident", "ones_all", "eps_t", "h_hi", "h_lo", "mm3"))
    sq_sum = g["made"]["sq_sum"]
    stat = g["stat"]
    NO, OS = 256, D // 256
    x1 = at("x1", [128, TT, D], F32, X_AT)
    gate2 = at("gate2", [128, 2, D], F32, GATE2_AT)
    WO_AT = [(REST, REST + 8192), (REST + 28672, REST + 40960)]
    wo_hi = [at(f"wo_hi{s}", [128, KT, NO], F32R, WO_AT[s][0]) for s in range(2)]
    wo_lo = [at(f"wo_lo{s}", [128, KT, NO], F32R, WO_AT[s][1]) for s in range(2)]
    wo_raw = [at(f"wo_raw{s}", [128, KT, NO], F32, WO_AT[s][1]) for s in range(2)]
    w_hi = at("wff_hi", [128, 3, D], F32R, REST + 24576)
    w_lo = at("wff_lo", [128, 3, D], F32R, REST + 36864)
    w_raw = at("wff_raw", [128, 3, D], F32, REST + 36864)
    xn = at("xn", [128, 4, D], F32, REST)
    gate1 = at("gate1", [128, OS, 2, NO], F32, REST + 16384)
    t_ring = at("t_second", [128, 2, CH], F32, REST + 16384)
    diag = at("diag", [128, 4, 128], F32, REST + 24576)
    mix_ring = at("mix_ring", [128, 4, NO], F32, REST + 49152)
    ff_hi = at("ff_hi", [128, 2, T], F32R, REST)
    ff_lo = at("ff_lo", [128, 2, T], F32R, REST + 12288)
    ff_raw = at("ff_raw", [128, 2, T], F32, REST + 12288)
    scratch = at("ff_scratch", [128, 3, CH], F32, REST + 49152)
    mix_rstd = at("mix_rstd", [128, 2, 2 * TT], F32, KEEP + 1536)

    x_in, wo_in = [sem(f"x1_in{c}") for c in range(NCH)], [sem(f"wo_in{s}") for s in range(2)]
    wo_hi_s, wo_ready = sem("wo_hi_s"), sem("wo_ready")
    sq_summed, mix_rooted, mix_rstd_ready = sem("sq_summed"), sem("mix_rooted"), sem("mix_rstd_ready")
    diag_ready, gate_summed, gates = sem("diag_ready"), sem("gate_summed"), sem("gates")
    o_summed, f_scaled, a_scaled, gated, x1_added = (
        sem(n) for n in ("o_summed", "f_scaled", "a_scaled", "o_gated", "x1_added"))
    squared, rooted, rstd, xn_dve, xn_act, turned, t_ready, hi_ready, split_even, split_odd = (
        sem("h2_" + n) for n in ("squared", "rooted", "rstd", "xn_dve", "xn_act", "turned", "t_ready", "hi_ready",
                                 "split_even", "split_odd"))
    PAIRS = FF // 2
    GATE, UP, DOWN = 0, 1, 2
    TILES = [(GATE, 0), (UP, 0), (GATE, 1), (UP, 1), (DOWN, 0), (DOWN, 1)]
    w_in = [sem(f"wff_in{s}") for s in range(3)]
    w_split_hi, w_ready = sem("wff_split_hi"), sem("wff_ready")
    g_summed, u_summed, silu_ready, product, ff_hi_s, ff_ready = (
        sem("ff_" + n) for n in ("g_summed", "u_summed", "silu_ready", "product", "hi_s", "ready"))
    d_summed, d_gated, d_added, d_added_dve = (sem(n) for n in ("d_summed", "d_gated", "d_added", "d_added_dve"))
    y_stored = sem("y_stored")
    DG = 2 * TT
    NG, TB = 4, 4

    DV, DP = DG // 4, DG - DG // 4

    def on_dve(n):
        return n % 4 == 3

    def waits_added(eng, j, n):
        if n < 0:
            j, n = j - 1, n + DG
        if not (isinstance(j, int) and j < 0):
            if on_dve(n):
                eng.wait_ge(d_added_dve, DV * j + n // 4 + 1)
            else:
                eng.wait_ge(d_added, DP * j + n + 1 - (n + 1) // 4)

    def waits_split(eng, n):
        if n >= 0:
            eng.wait_ge(split_even, n // 2 + 1)
        if n >= 1:
            eng.wait_ge(split_odd, (n + 1) // 2)

    with nc.Block() as block:
        @block.sync
        def _(sp):
            def load_o(n):
                sp.dma_start(wo_raw[n % 2][:], w_o[:, NO * n:NO * n + NO].rearrange("(k p) n -> p k n", p=128)
                             ).then_inc(wo_in[n % 2], 16)

            def load(j, i):
                kind, f = TILES[i]
                if kind == DOWN:
                    src, dst = w_down[bass.ds((2 * j + f) * 128, 128), :], w_raw[:, i % 3]
                else:
                    src = (w_gate, w_up)[kind][:, bass.ds((2 * j + f) * 128, 128)].rearrange("(k p) n -> p k n", p=128)
                    dst = w_raw[:, i % 3].rearrange("p (k n) -> p k n", n=128)
                sp.dma_start(dst, src).then_inc(w_in[i % 3], 16)

            def used(j, i):
                kind, f = TILES[i]
                if kind == DOWN:
                    sp.wait_ge(d_summed, DG * j + DG)
                else:
                    sp.wait_ge((g_summed, u_summed)[kind], 6 * j + 3 * f + 3)

            def later(j):
                for i in range(6):
                    used(j, i)
                    load(j + (i + 3) // 6, (i + 3) % 6)
            def load_x(c):
                src = x_prompt if c == 0 else x_sample[CH * (c - 1):CH * c]
                sp.dma_start(x1[:, 4 * c:4 * c + 4], src.rearrange("(t p) n -> p t n", p=128)).then_inc(x_in[c], 16)
            load_o(0)
            load_x(0)
            sp.wait_ge(sq_summed, 1)
            load_x(1)
            load_x(2)
            load_o(1)
            for n in range(2, OS):
                sp.wait_ge(o_summed, TT * (n - 1))
                load_o(n)
            load(0, 0)
            sp.wait_ge(o_summed, TT * OS)
            load(0, 1)
            sp.wait_ge(gated, TT * OS)
            load(0, 2)
            later(0)
            with sp.Fori(1, PAIRS - 1) as j:
                later(j)
            for i in range(3):
                used(PAIRS - 1, i)
                load(PAIRS - 1, i + 3)
            for t in range(TT):
                waits_added(sp, PAIRS - 1, 2 * t)
                waits_added(sp, PAIRS - 1, 2 * t + 1)
                dst = y_prompt[0, 128 * t:128 * t + 128] if t < 4 else y_sample[0, 128 * (t - 4):128 * (t - 3)]
                sp.dma_start(dst, x1[:, t]).then_inc(y_stored, 16)
            sp.wait_ge(y_stored, 16 * TT)

        def split_hi(act, j, i):
            act.wait_ge(w_in[i % 3], 16 * (2 * j + i // 3) + 16)
            act.activation(w_hi[:, i % 3], w_raw[:, i % 3], ACT.Copy).then_inc(w_split_hi, 1)

        def split_lo(dve, j, i):
            dve.wait_ge(w_split_hi, 6 * j + i + 1)
            dve.tensor_tensor(w_lo[:, i % 3], w_raw[:, i % 3], w_hi[:, i % 3].bitcast(F32), ALU.subtract
                              ).then_inc(w_ready, 1)

        def silu(act, j, n):
            c = n % NCH
            act.wait_ge(g_summed, 6 * j + n + 1)
            if n == 0:
                if isinstance(j, int) and j == 0:
                    act.wait_ge(x1_added, TT * OS)
                waits_added(act, j, -2)
                waits_added(act, j, -1)
            if n >= 3:
                act.wait_ge(product, 6 * j + n - 2)
            act.activation(scratch[:, c], banks[:, c], ACT.Silu).then_inc(silu_ready, 1)

        def pair_act(act, j, last):
            first = isinstance(j, int) and j == 0
            for i, (kind, f) in enumerate(TILES):
                if not (last and i >= 4) and not (first and i == 0):
                    split_hi(act, j + (i + 2) // 6, (i + 2) % 6)
                for c in range(NCH):
                    n = 3 * f + c
                    if kind == GATE and not (first and n < 2):
                        silu(act, j, n)
                    if kind == UP:
                        act.wait_ge(product, 6 * j + n + 1)
                        act.activation(ff_hi[:, f, CH * c:CH * c + CH], ff_raw[:, f, CH * c:CH * c + CH], ACT.Copy
                                       ).then_inc(ff_hi_s, 1)

        @block.scalar
        def _(act):
            def split_o(n):
                act.wait_ge(wo_in[n % 2], 16 * (n // 2) + 16)
                act.activation(wo_hi[n % 2][:], wo_raw[n % 2][:], ACT.Copy).then_inc(wo_hi_s, 1)

            def scale_f(m):
                act.wait_ge(o_summed, m + 1)
                if m >= 4:
                    act.wait_ge(x1_added, m - 3)
                act.activation(mix_ring[:, m % 4], banks[:, m % NG, NO:2 * NO], ACT.Copy,
                               scale=mix_rstd[:, 1, TT + m % TT:TT + m % TT + 1]).then_inc(f_scaled, 1)

            def square(t):
                act.wait_ge(x1_added, TT * (OS - 1) + t + 1)
                if t:
                    act.wait_ge(squared, t)
                act.activation(banks[:, 6:8], x1[:, t].rearrange("p (b n) -> p b n", b=2), ACT.Square,
                               accum_out=stat[:, 0, t:t + 1]).then_inc(squared, 1)

            def root(c):
                act.wait_ge(squared, 4 * c + 4)
                act.activation(stat[:, 0, 4 * c:4 * c + 4], stat[:, 0, 4 * c:4 * c + 4], ACT.Sqrt,
                               scale=1.0 / D, bias=eps_t[:]).then_inc(rooted, 1)

            def norm(c):
                act.wait_ge(rstd, c + 1)
                if c:
                    act.wait_ge(turned, KT * c)
                t = 4 * c + 3
                act.activation(xn[:, 3], x1[:, t], ACT.Copy, scale=stat[:, 1, t:t + 1]).then_inc(xn_act, 1)

            def modulate(n):
                c, k = divmod(n, KT)
                r = REQ[c]
                act.wait_ge(turned, n + 1)
                if n >= 2:
                    act.wait_ge((split_even, split_odd)[n % 2], n // 2)
                act.activation(t_ring[:, n % 2], banks[:, TB + n % 2], ACT.Identity, scale=coef[:, 1, k, r:r + 1],
                               bias=mod[:, 3 * KT + k, r:r + 1]).then_inc(t_ready, 1)
            split_o(0)
            for m in range(8):
                act.wait_ge(gate_summed, m + 1)
                r, half = m // 2 % 2, m % 2
                if m < 4:
                    dst, src = gate1[:, 2 * half:2 * half + 2, r], banks[:, 6 + m % 2].rearrange("p (n x) -> p n x", n=2)
                else:
                    dst, src = gate2[:, r, 512 * half:512 * half + 512], banks[:, 6 + m % 2]
                act.activation(dst, src, ACT.Copy).then_inc(gates, 1)
            act.wait_ge(sq_summed, 1)
            act.activation(mix_rstd[:, 0], banks[:, TB, 0:4 * TT:2], ACT.Sqrt, scale=1.0 / D_FOURIER, bias=eps_t[:]
                           ).then_inc(mix_rooted, 1)
            act.wait_ge(mix_rstd_ready, 1)
            for m in range(TT * OS - 4):
                scale_f(m)
                if m == 7:
                    split_o(1)
                if m % TT == 0 and m and m // TT + 1 < OS:
                    split_o(m // TT + 1)
                if m >= TT * OS - 8:
                    square(m - (TT * OS - 8))
            root(0)
            norm(0)
            for i in range(4):
                scale_f(TT * OS - 4 + i)
                if i == 1:
                    split_hi(act, 0, 0)
                modulate(2 * i)
                modulate(2 * i + 1)
                square(4 + i)
            root(1)
            norm(1)
            for k in range(KT):
                modulate(KT + k)
                if k % 2:
                    square(8 + k // 2)
            root(2)
            norm(2)
            split_hi(act, 0, 1)
            for c in range(NCH):
                if c < 2:
                    silu(act, 0, c)
                if c == 0:
                    for k in range(KT):
                        modulate(2 * KT + k)
                    split_hi(act, 0, 2)
            pair_act(act, 0, False)
            with act.Fori(1, PAIRS - 1) as j:
                pair_act(act, j, False)
            pair_act(act, PAIRS - 1, True)

        def pair_dve(dve, j, last):
            first = isinstance(j, int) and j == 0
            for i, (kind, f) in enumerate(TILES):
                if i < 5 and not (last and i == 4) and not (first and i == 0):
                    split_lo(dve, j + (i + 2) // 6, (i + 2) % 6)
                if kind == UP:
                    for c in range(NCH):
                        n = 3 * f + c
                        part = ff_raw[:, f, CH * c:CH * c + CH]
                        dve.wait_ge(u_summed, 6 * j + n + 1)
                        dve.wait_ge(silu_ready, 6 * j + n + 1)
                        dve.tensor_tensor(part, banks[:, 3 + c], scratch[:, c], ALU.mult).then_inc(product, 1)
                        dve.wait_ge(ff_hi_s, 6 * j + n + 1)
                        dve.tensor_tensor(ff_lo[:, f, CH * c:CH * c + CH], part,
                                          ff_hi[:, f, CH * c:CH * c + CH].bitcast(F32), ALU.subtract
                                          ).then_inc(ff_ready, 1)
                if i == 5:
                    for n in range(DG):
                        t, half = divmod(n, 2)
                        dve.wait_ge(d_summed, DG * j + n + 1)
                        if n >= 3:
                            waits_added(dve, j, n - 3)
                        dve.tensor_tensor(scratch[:, n % 3], banks[:, (6 + n) % 8],
                                          gate2[:, REQ[t // 4], 512 * half:512 * half + 512], ALU.mult
                                          ).then_inc(d_gated, 1)
                        if on_dve(n):
                            part = x1[:, t, 512 * half:512 * half + 512]
                            dve.wait_ge(d_gated, DG * j + n + 1)
                            dve.tensor_tensor(part, part, scratch[:, n % 3], ALU.add).then_inc(d_added_dve, 1)
                    if not last:
                        split_lo(dve, j + 1, 1)

        @block.vector
        def _(dve):
            def split_o(n):
                dve.wait_ge(wo_hi_s, n + 1)
                dve.tensor_tensor(wo_lo[n % 2][:], wo_raw[n % 2][:], wo_hi[n % 2][:].bitcast(F32), ALU.subtract
                                  ).then_inc(wo_ready, 1)

            def gate_mix(m):
                n, t = divmod(m, TT)
                part = mix_ring[:, m % 4]
                dve.wait_ge(f_scaled, m + 1)
                dve.scalar_tensor_tensor(part, banks[:, m % NG, 0:NO], mix_rstd[:, 1, t:t + 1], part, ALU.mult, ALU.add
                                         ).then_inc(a_scaled, 1)
                dve.wait_ge(a_scaled, m + 1)
                dve.tensor_tensor(part, part, gate1[:, n, REQ[t // 4]], ALU.mult).then_inc(gated, 1)

            def norm(c):
                dve.wait_ge(rooted, c + 1)
                dve.reciprocal(stat[:, 1, 4 * c:4 * c + 4], stat[:, 0, 4 * c:4 * c + 4]).then_inc(rstd, 1)
                dve.wait_ge(rstd, c + 1)
                if c:
                    dve.wait_ge(turned, KT * c)
                for i in range(3):
                    dve.tensor_scalar(xn[:, i], x1[:, 4 * c + i], stat[:, 1, 4 * c + i:4 * c + i + 1], None, ALU.mult
                                      ).then_inc(xn_dve, 1)

            def split(n):
                c, k = divmod(n, KT)
                dve.wait_ge(t_ready, n + 1)
                hi, lo = (h[:, k, CH * c:CH * c + CH] for h in (h_hi, h_lo))
                dve.tensor_copy(hi, t_ring[:, n % 2]).then_inc(hi_ready, 1)
                if n % 2 == 0:
                    dve.wait_ge(hi_ready, n + 1)
                    dve.tensor_tensor(lo, t_ring[:, n % 2], hi.bitcast(F32), ALU.subtract).then_inc(split_even, 1)
            for m in range(32):
                if m == 16:
                    split_o(0)
                gate, r, k = m // 16, m // 8 % 2, m % 8
                if m >= 4:
                    dve.wait_ge(gate_summed, m // 4)
                tile = (2 + 3 * gate) * KT + k
                dve.tensor_scalar(diag[:, m % 4], ident[:], mod[:, tile, r:r + 1], None, ALU.mult).then_inc(diag_ready, 1)
            dve.wait_ge(mix_rooted, 1)
            dve.reciprocal(mix_rstd[:, 1], mix_rstd[:, 0]).then_inc(mix_rstd_ready, 1)
            dve.wait_ge(mix_rstd_ready, 1)
            dve.wait_ge(gates, 8)
            for m in range(TT * OS - 4):
                gate_mix(m)
                if m == 7:
                    split_o(1)
                if m % TT == 1 and m > TT and m // TT + 1 < OS:
                    split_o(m // TT + 1)
            norm(0)
            for i in range(4):
                gate_mix(TT * OS - 4 + i)
                if i == 2:
                    split_lo(dve, 0, 0)
                split(2 * i)
                split(2 * i + 1)
            norm(1)
            for k in range(KT):
                split(KT + k)
            norm(2)
            split_lo(dve, 0, 1)
            for k in range(KT):
                split(2 * KT + k)
            split_lo(dve, 0, 2)
            pair_dve(dve, 0, False)
            with dve.Fori(1, PAIRS - 1) as j:
                pair_dve(dve, j, False)
            pair_dve(dve, PAIRS - 1, True)

        @block.gpsimd
        def _(pool):
            def add_mix(m):
                n, t = divmod(m, TT)
                if n == 0 and t % 4 == 0:
                    pool.wait_ge(x_in[t // 4], 16)
                pool.wait_ge(gated, m + 1)
                part = x1[:, t, NO * n:NO * n + NO]
                pool.tensor_tensor(part, part, mix_ring[:, m % 4], ALU.add).then_inc(x1_added, 1)

            def split(n):
                c, k = divmod(n, KT)
                hi, lo = (h[:, k, CH * c:CH * c + CH] for h in (h_hi, h_lo))
                pool.wait_ge(hi_ready, n + 1)
                pool.tensor_tensor(lo, t_ring[:, n % 2], hi.bitcast(F32), ALU.subtract).then_inc(split_odd, 1)
            for m in range(TT * OS - 4):
                add_mix(m)
            for i in range(4):
                add_mix(TT * OS - 4 + i)
                split(2 * i + 1)
            for c in range(1, NCH):
                for k in range(1, KT, 2):
                    split(KT * c + k)
            with pool.Fori(0, PAIRS) as j:
                for n in range(DG):
                    if on_dve(n):
                        continue
                    t, half = divmod(n, 2)
                    pool.wait_ge(d_gated, DG * j + n + 1)
                    part = x1[:, t, 512 * half:512 * half + 512]
                    pool.tensor_tensor(part, part, scratch[:, n % 3], ALU.add).then_inc(d_added, 1)

        @block.tensor
        def _(pe):
            for n in range(2 * TT):
                half, t = divmod(n, TT)
                last = pe.matmul(banks[:, TB, 2 * n:2 * n + 2], sq_sum[:, half, 128 * t:128 * t + 128],
                                 ones_all[:, 0:2].bitcast(F32), start=True, stop=True)
            last.then_inc(sq_summed, 1)
            for m in range(8):
                pe.wait_ge(diag_ready, 4 * m + 4)
                if m >= 2:
                    pe.wait_ge(gates, m - 1)
                for i in range(4):
                    last = pe.matmul(banks[:, 6 + m % 2, 128 * i:128 * i + 128], ones_all[:].bitcast(F32), diag[:, i],
                                     start=True, stop=True)
                last.then_inc(gate_summed, 1)

            def mix_out(m):
                n, t = divmod(m, TT)
                if t == 0:
                    pe.wait_ge(wo_ready, n + 1)
                if m >= NG:
                    pe.wait_ge(gated, m - NG + 1)
                for half in range(2):
                    for i in range(FT):
                        k, row = FT * half + i, FT * (1 - half) + i
                        last = mm3(pe, banks[:, m % NG, NO * half:NO * half + NO],
                                   (h_hi[:, k, 128 * t:128 * t + 128], h_lo[:, k, 128 * t:128 * t + 128]),
                                   (wo_hi[n % 2][:, row], wo_lo[n % 2][:, row]), i == 0, i == FT - 1)
                last.then_inc(o_summed, 1)

            def turn(n):
                c, k = divmod(n, KT)
                pe.wait_ge(xn_dve, 3 * c + 3)
                pe.wait_ge(xn_act, c + 1)
                if n >= 2:
                    pe.wait_ge(t_ready, n - 1)
                elif n == 0:
                    pe.wait_ge(mix_rooted, 1)
                for i in range(4):
                    last = pe.transpose(banks[:, TB + n % 2, 128 * i:128 * i + 128], xn[:, i, 128 * k:128 * k + 128], ident[:])
                last.then_inc(turned, 1)

            def gate_step(k, c):
                if k == 0:
                    pe.wait_ge(w_ready, 1)
                    waits_split(pe, KT * c + KT - 1)
                    pe.wait_ge(gated, TT * OS)
                w = [part[:, 0].rearrange("p (k n) -> p k n", n=128) for part in (w_hi, w_lo)]
                last = mm3(pe, banks[:, c], (w[0][:, k], w[1][:, k]),
                           (h_hi[:, k, CH * c:CH * c + CH], h_lo[:, k, CH * c:CH * c + CH]), k == 0, k == KT - 1)
                if k == KT - 1:
                    last.then_inc(g_summed, 1)
            for m in range(TT * OS - 4):
                mix_out(m)
            for i in range(4):
                mix_out(TT * OS - 4 + i)
                turn(2 * i)
                turn(2 * i + 1)
            for c in range(1, NCH):
                for k in range(KT):
                    turn(KT * c + k)
                    gate_step(k, c - 1)
            waits_split(pe, KT * NCH - 1)

            def pair(j):
                first = isinstance(j, int) and j == 0
                for i, (kind, f) in enumerate(TILES[:4]):
                    w = [part[:, i % 3].rearrange("p (k n) -> p k n", n=128) for part in (w_hi, w_lo)]
                    pe.wait_ge(w_ready, 6 * j + i + 1)
                    for c in range(2 if first and i == 0 else 0, NCH):
                        if f == 0 and first:
                            if kind == UP:
                                pe.wait_ge(t_ready, NCH * KT)
                        elif f == 0:
                            pe.wait_ge(d_gated, DG * j - 5 + 3 * kind + c)
                        elif kind == GATE:
                            pe.wait_ge(silu_ready, 6 * j + c + 1)
                        else:
                            pe.wait_ge(product, 6 * j + c + 1)
                        for k in range(KT):
                            last = mm3(pe, banks[:, 3 * kind + c], (w[0][:, k], w[1][:, k]),
                                       (h_hi[:, k, CH * c:CH * c + CH], h_lo[:, k, CH * c:CH * c + CH]), k == 0, k == KT - 1)
                        last.then_inc((g_summed, u_summed)[kind], 1)
                pe.wait_ge(w_ready, 6 * j + 6)
                for n in range(DG):
                    t, half = divmod(n, 2)
                    if t % 4 == 0 and half == 0:
                        pe.wait_ge(ff_ready, 6 * j + 3 + t // 4 + 1)
                    if n >= 8:
                        pe.wait_ge(d_gated, DG * j + n - 7)
                    elif n >= 5:
                        pe.wait_ge(product, 6 * j + 6)
                    elif n >= 2:
                        pe.wait_ge(silu_ready, 6 * j + 6)
                    elif first:
                        pe.wait_ge(squared, TT)
                    for f in range(2):
                        last = mm3(pe, banks[:, (6 + n) % 8],
                                   (ff_hi[:, f, 128 * t:128 * t + 128], ff_lo[:, f, 128 * t:128 * t + 128]),
                                   [part[:, 1 + f, 512 * half:512 * half + 512] for part in (w_hi, w_lo)], f == 0, f == 1)
                    last.then_inc(d_summed, 1)
            pair(0)
            with pe.Fori(1, PAIRS) as j:
                pair(j)


def _inputs(inputs):
    f = lambda n: np.ascontiguousarray(inputs[n])
    g_q, g_k = f("g_q")[0], f("g_k")[0]
    c = np.concatenate([f("c_prompt"), f("c_sample")]).reshape(16, 128)
    rows = [c, f("g_attn").reshape(8, 128), f("g_ffn").reshape(8, 128), f("g_fout").reshape(4, 128),
            f("g_aout").reshape(4, 128), np.concatenate([g_q, g_q])[None], np.concatenate([g_k, g_k])[None],
            f("b_ada").reshape(48, 128)]
    rp = f("rpb")[0]
    pad = np.zeros((RP_ROWS, N_HEADS, RP_COLS), np.float32)
    pad[4:4 + 2 * WIN_ROWS - 1, :, 16:16 + 2 * WIN_COLS - 1] = rp.transpose(1, 0, 2)
    return {
        "x_prompt": f("x_prompt")[0], "x_sample": f("x_sample")[0], "c_rows": c, "w_ada": f("w_ada")[0],
        "vec_rows": np.concatenate(rows), "w_in": f("w_in")[0], "w_fmix": f("w_fmix")[0], "rpb_pad": pad.reshape(-1),
        "masks": _masks(), "dft_c": _dft_channels(), "dft_t1": _dft_tokens(T_SAMPLE), "dft_t0": _dft_tokens(T_PROMPT),
        "w_o": f("w_o")[0], "w_gate": f("w_gate")[0], "w_up": f("w_up")[0], "w_down": f("w_down")[0],
    }


def _masks():
    out = np.full((128, NB, MASK_COLS), MASKED, np.float32)
    for b in range(NB):
        at = 0
        for c in range(NCH):
            rows = 8 if c == 0 else 16
            for qi in range(QROWS):
                i = qi + (QROWS if c == 2 else 0)
                r0 = min(max(i - WIN_ROWS // 2, 0), rows - WIN_ROWS)
                for qc in range(QCOLS):
                    col = QCOLS * b + qc
                    c0 = min(max(col - WIN_COLS // 2, 0), GRID_W - WIN_COLS)
                    for r in range(r0, r0 + WIN_ROWS):
                        k = at + (r - KEY_ROW0[c]) * KCOLS + c0 - KEY_COL[b]
                        out[qi * QCOLS + QCOLS - 1 - qc, b, k:k + WIN_COLS] = 0.0
            at += KEY_ROWS[c] * KCOLS
    return out.reshape(128, NB * MASK_COLS)


def _dft_channels():
    n = np.arange(128)
    a = 2 * np.pi * ((n[:, None] * n) % 128) / 128
    return np.concatenate([np.cos(a), np.sin(a)], 1).astype(np.float32) / np.float32(128 ** 0.5)


def _dft_tokens(t):
    n, k = np.arange(t), np.arange(t // 2)
    a = 2 * np.pi * ((n[:, None] * k) % t) / t
    return (np.stack([np.cos(a), np.sin(a)]) / t ** 0.5).astype(np.float32)


def kernel(**inputs):
    import concourse.bacc as bacc
    from concourse.bass_utils import run_bass_kernel_spmd

    nc = bacc.Bacc("TRN2", target_bir_lowering=False, num_devices=1)
    arrays, args = {}, {}
    for name, a in _inputs(inputs).items():
        arrays[f"in_{name}"] = a
        args[name] = nc.dram_tensor(f"in_{name}", a.shape, mybir.dt.from_np(a.dtype), kind="ExternalInput").ap()
    args["u_scratch"] = nc.dram_tensor("u_scratch", (D_FOURIER, T), F32).ap()
    for name, t in (("y_prompt", T_PROMPT), ("y_sample", T_SAMPLE)):
        args[name] = nc.dram_tensor(name, (1, t, D), F32, kind="ExternalOutput").ap()
    layer(nc, **args)
    r = run_bass_kernel_spmd(nc, [arrays], core_ids=[0])
    return r.results[0]["y_prompt"], r.results[0]["y_sample"]
```

```python
import numpy as np
from contextlib import ExitStack

import concourse.bass as bass
from concourse import mybir

F32, F32R = mybir.dt.float32, mybir.dt.float32r
ALU = mybir.AluOpType
ACT = mybir.ActivationFunctionType
AX = mybir.AxisListType

D = 1024
KT = D // 128
T_PROMPT, T_SAMPLE = 512, 1024
T = T_PROMPT + T_SAMPLE
CH = 512
NCH = T // CH
TT = T // 128
REQ = [0, 1, 1]
D_FOURIER = D // 2
FT = D_FOURIER // 128
HEAD = 64
N_HEADS = D_FOURIER // HEAD
D_FF = 2816
FF = D_FF // 128
GRID_W = 64
WIN_ROWS, WIN_COLS = 8, 16
N_MOD = 6
EPS = 1e-6

QROWS, QCOLS, KCOLS = 8, 16, 32
NB = GRID_W // QCOLS
KEY_COL = [min(max(QCOLS * b - WIN_COLS // 2, 0), GRID_W - KCOLS) for b in range(NB)]
KEY_ROWS = [8, 12, 12]
KEY_ROW0 = [0, 0, 4]
KEY_TOKEN0 = [0, T_PROMPT, T_PROMPT + 4 * GRID_W]
V_TILE0 = [0, 2, 3]
NVT = 6
BIAS_E, BIAS_X = 16, 48
RP_ROWS, RP_COLS = 23, 63
MASKED = 1e30
MASK_COLS = sum(KEY_ROWS) * KCOLS
UNITS = NB * NCH * 2

ADA_FIRST = 4

V_C, V_GATTN, V_GFFN, V_GF, V_GA, V_GQ, V_GK, V_BADA = 0, 16, 24, 32, 36, 40, 41, 42

BASE = 16512
H_LO, H_HI = BASE, BASE + 49152
X_AT = BASE + 98304
WIN_RAW_AT = X_AT + 98304
GATE2_AT = BASE + 147456
REST = BASE + 155648
SQ_SUM_AT = BASE + 197888
NO, OS = 256, D // 256
WO_AT = [(REST, REST + 8192), (REST + 28672, REST + 40960)]
KEEP = BASE + 210176
END = BASE + 212832


def after(eng, s, count):
    if not (isinstance(count, int) and count <= 0):
        eng.wait_ge(s, count)


def rounds(eng, first, end, body):
    body(first)
    if end - first > 1:
        with eng.Fori(first + 1, end) as j:
            body(j)


class Kept:
    pass


def mm3(pe, out, lhs, rhs, start, stop):
    pe.matmul(out, lhs[0], rhs[0], start=start, stop=False)
    pe.matmul(out, lhs[0], rhs[1], start=False, stop=False)
    return pe.matmul(out, lhs[1], rhs[0], start=False, stop=stop)


def layer(nc, x_prompt, x_sample, w_ada, b_ada, vec_rows, w_in, w_fmix, rpb_pad, masks, dft_c, dft_t1,
          dft_t0, w_o, w_gate, w_up, w_down, u_scratch, gate_rows, y_prompt, y_sample):
    ctx = ExitStack()
    with ctx:
        def at(name, shape, dt, off):
            size = 4 * int(np.prod(shape[1:]))
            assert off % 32 == 0 and off >= BASE and off + size <= END, (name, off - BASE, size)
            return nc.alloc_sbuf_tensor_at(name, shape, dt, offset=off)

        def sem(name):
            return ctx.enter_context(nc.semaphore(name))

        kept = Kept()
        kept.x_prompt, kept.x_sample, kept.w_ada, kept.b_ada, kept.vec_rows = x_prompt, x_sample, w_ada, b_ada, vec_rows
        kept.w_in, kept.w_fmix, kept.rpb_pad, kept.masks, kept.dft_c = w_in, w_fmix, rpb_pad, masks, dft_c
        kept.dft_t1, kept.dft_t0, kept.w_o, kept.w_gate, kept.w_up = dft_t1, dft_t0, w_o, w_gate, w_up
        kept.w_down, kept.u_scratch, kept.gate_rows, kept.y_prompt, kept.y_sample = w_down, u_scratch, gate_rows, y_prompt, y_sample
        banks = ctx.enter_context(nc.psum_tensor("banks", [128, 8, 512], F32))

        kept.ident = at("ident", [128, 128], F32, KEEP)
        kept.ones_head = at("ones_head", [128, 128], F32R, KEEP + 512)
        kept.ones_all = at("ones_all", [128, 128], F32R, KEEP + 1024)
        kept.vec = at("vec", [128, 96], F32, KEEP + 1536)
        kept.mod = at("mod", [128, N_MOD * KT, 2], F32, KEEP + 1920)
        kept.coef = at("coef", [128, 2, KT, 2], F32, KEEP + 2304)
        kept.stat = at("stat", [128, 2, TT], F32, KEEP + 2432)
        kept.eps_t = at("eps_t", [128, 1], F32, KEEP + 2528)
        kept.gq8 = at("gq8", [128, 1], F32, KEEP + 2560)
        kept.h_hi = at("h_hi", [128, KT, T], F32R, H_HI)
        kept.h_lo = at("h_lo", [128, KT, T], F32R, H_LO)

        kept.w_raw = at("win_raw", [128, 2, KT, 128], F32, WIN_RAW_AT)
        kept.w_in_s = [sem(f"win_in{s}") for s in range(2)]
        kept.c_split = at("c_split", [128, KT, 4], F32R, X_AT + 111104)
        kept.pick = at("pick", [128, 2], F32, X_AT + 111232)
        kept.gate_stored = sem("gate_stored")

        first_stage(nc, at, sem, banks, kept)
        projections(nc, at, sem, banks, kept)
        attention(nc, at, sem, banks, kept)
        fourier(nc, at, sem, banks, kept)
        second_half(nc, at, sem, banks, kept)


def first_stage(nc, at, sem, banks, kept):
    x_prompt, x_sample, w_ada, w_in, vec_rows = kept.x_prompt, kept.x_sample, kept.w_ada, kept.w_in, kept.vec_rows
    w_raw, w_in_s, c_split, pick = kept.w_raw, kept.w_in_s, kept.c_split, kept.pick
    ident, ones_head, ones_all, vec, mod, coef = kept.ident, kept.ones_head, kept.ones_all, kept.vec, kept.mod, kept.coef
    stat, eps_t, gq8, h_hi, h_lo = kept.stat, kept.eps_t, kept.gq8, kept.h_hi, kept.h_lo
    NV = V_BADA + N_MOD * KT
    X_BANKS = (4, 5, 0, 1)
    AC = ADA_FIRST
    x = at("x_first", [128, TT, D], F32, X_AT)
    ada = at("ada", [128, 3, KT, 512], F32, X_AT + 49152)
    mrow = at("mrow", [128, 2, 512], F32, H_HI + 45056)
    t_ring = at("t_first", [128, 4, CH], F32, X_AT + 81920)
    vrow = at("vrow", [128, 128], F32, X_AT + 110592)
    silu_c = at("silu_c", [128, 2, KT], F32, KEEP + 2592)

    x_in = [sem(f"x_in{c}") for c in range(NCH)]
    vec_in, ada_in = sem("vec_in"), [sem(f"ada_in{i}") for i in range(3)]
    ident_zero, ident_ready, ones_ready = sem("ident_zero"), sem("ident_ready"), sem("ones_ready")
    vec_turned, vec_ready, silu_ready, c_ready = sem("vec_turned"), sem("vec_ready"), sem("silu_ready"), sem("c_ready")
    mod_summed, mod_row, mod_turned = sem("mod_summed"), sem("mod_row"), sem("mod_turned")
    mod_ready, coef_ready = sem("mod_ready"), sem("coef_ready")
    squared, rooted, rstd_ready, x_normed = sem("squared"), sem("rooted"), sem("rstd_ready"), sem("x_normed")
    x_turned, t_ready, h_hi_ready, split_even, split_odd = (
        sem(n) for n in ("x_turned", "t_ready", "h_hi_ready", "h_split_even", "h_split_odd"))

    with nc.Block() as block:
        @block.sync
        def _(sp):
            sp.dma_start(vrow[0:NV, :], vec_rows).then_inc(vec_in, 16)
            def load_ada(j):
                sp.dma_start(ada[:, j % 3], w_ada[:, 512 * j:512 * j + 512].rearrange("(k p) n -> p k n", p=128)
                             ).then_inc(ada_in[j % 3], 16)

            def load_x(c):
                src = x_prompt if c == 0 else x_sample[CH * (c - 1):CH * c]
                sp.dma_start(x[:, 4 * c:4 * c + 4], src.rearrange("(t p) n -> p t n", p=128)).then_inc(x_in[c], 16)
            load_ada(0)
            load_ada(1)
            load_ada(2)
            load_x(0)
            sp.wait_ge(mod_summed, 1)
            load_ada(3)
            load_x(1)
            load_x(2)
            for s in range(2):
                sp.dma_start(w_raw[:, s], w_in[:, 128 * s:128 * s + 128].rearrange("(k p) n -> p k n", p=128)
                             ).then_inc(w_in_s[s], 16)

        @block.gpsimd
        def _(pool):
            pool.memset(ident[:], 0.0).then_inc(ident_zero, 1)
            pool.wait_ge(ident_zero, 1)
            pool.affine_select(out=ident[:], in_=ident[:], compare_op=ALU.not_equal, fill=1.0, base=0,
                               pattern=[[-1, 128]], channel_multiplier=1).then_inc(ident_ready, 1)
            for n in range(1, NCH * KT, 2):
                c, k = divmod(n, KT)
                hi, lo = (h[:, k, CH * c:CH * c + CH] for h in (h_hi, h_lo))
                pool.wait_ge(h_hi_ready, n + 1)
                pool.tensor_tensor(lo, t_ring[:, n % 4], hi.bitcast(F32), ALU.subtract).then_inc(split_odd, 1)

        @block.scalar
        def _(act):
            act.wait_ge(vec_turned, 1)
            act.activation(silu_c[:].rearrange("p r k -> p (r k)"), banks[:, 2, V_C:V_C + 16], ACT.Silu).then_inc(silu_ready, 1)
            act.wait_ge(ones_ready, 1)

            def square(t):
                if t % 4 == 0:
                    act.wait_ge(x_in[t // 4], 16)
                if t:
                    act.wait_ge(squared, t)
                act.activation(banks[:, 6:8], x[:, t].rearrange("p (b n) -> p b n", b=2), ACT.Square,
                               accum_out=stat[:, 0, t:t + 1]).then_inc(squared, 1)

            def root(c):
                act.wait_ge(squared, 4 * c + 4)
                act.activation(stat[:, 0, 4 * c:4 * c + 4], stat[:, 0, 4 * c:4 * c + 4], ACT.Sqrt,
                               scale=1.0 / D, bias=eps_t[:]).then_inc(rooted, 1)

            def modulate(n):
                c, k = divmod(n, KT)
                act.wait_ge(x_turned, n + 1)
                if n >= 4:
                    act.wait_ge((split_even, split_odd)[n % 2], n // 2 - 1)
                act.activation(t_ring[:, n % 4], banks[:, X_BANKS[n % 4]], ACT.Identity, scale=coef[:, 0, k, REQ[c]:REQ[c] + 1],
                               bias=mod[:, k, REQ[c]:REQ[c] + 1]).then_inc(t_ready, 1)
            for t in range(8):
                square(t)
                if t % 4 == 3:
                    root(t // 4)
            act.wait_ge(coef_ready, 1)
            for n in range(NCH * KT):
                modulate(n)
                if 4 <= n < 8:
                    square(4 + n)
                    if n == 7:
                        root(2)

        @block.vector
        def _(dve):
            dve.memset(ones_head[:].bitcast(F32), 0.0).then_inc(mod_row, 1)
            dve.wait_ge(mod_row, 1)
            dve.memset(ones_head[0:64, 0:64].bitcast(F32), 1.0)
            dve.memset(ones_head[64:128, 64:128].bitcast(F32), 1.0)
            dve.memset(ones_all[:].bitcast(F32), 1.0)
            dve.memset(eps_t[:], EPS).then_inc(ones_ready, 1)
            dve.wait_ge(vec_turned, 1)
            dve.wait_ge(silu_ready, 1)
            dve.tensor_copy(vec[:, 0:NV], banks[:, 2, 0:NV]).then_inc(vec_ready, 1)
            silu = silu_c[:].rearrange("p r k -> p k r")
            dve.tensor_copy(c_split[:, :, 0:2], silu).then_inc(c_ready, 1)
            dve.wait_ge(ident_ready, 1)
            dve.tensor_tensor(pick[0:4, :], ident[0:4, 0:2], ident[0:4, 2:4], ALU.add).then_inc(c_ready, 1)
            dve.wait_ge(c_ready, 2)
            dve.tensor_tensor(c_split[:, :, 2:4], silu, c_split[:, :, 0:2].bitcast(F32), ALU.subtract).then_inc(c_ready, 1)
            dve.wait_ge(vec_ready, 1)
            dve.tensor_scalar(gq8[:], vec[:, V_GQ:V_GQ + 1], -float(HEAD) ** -0.5, None, ALU.mult).then_inc(vec_ready, 1)

            def norm_row(t):
                c = t // 4
                if t % 4 == 0:
                    dve.wait_ge(rooted, c + 1)
                    dve.reciprocal(stat[:, 1, 4 * c:4 * c + 4], stat[:, 0, 4 * c:4 * c + 4]).then_inc(rstd_ready, 1)
                    dve.wait_ge(rstd_ready, c + 1)
                dve.tensor_scalar(x[:, t], x[:, t], stat[:, 1, t:t + 1], None, ALU.mult).then_inc(x_normed, 1)

            def mod_part(a, b, n):
                dve.tensor_tensor(mod[:, a:b], banks[:, 3, 2 * a:2 * b].rearrange("p (j r) -> p j r", r=2),
                                  bass.AP(vec, V_BADA + a, [[96, 128], [1, b - a], [0, 2]]), ALU.add).then_inc(mod_ready, 1)
                dve.wait_ge(mod_ready, n)

            def gains(which, tile0, gain0, n):
                gain = bass.AP(vec, gain0, [[96, 128], [1, KT], [0, 2]])
                dve.scalar_tensor_tensor(coef[:, which], mod[:, tile0:tile0 + KT], 1.0, gain, ALU.add, ALU.mult
                                         ).then_inc(coef_ready, 1)

            def split(n):
                c, k = divmod(n, KT)
                dve.wait_ge(t_ready, n + 1)
                hi, lo = (h[:, k, CH * c:CH * c + CH] for h in (h_hi, h_lo))
                dve.tensor_copy(hi, t_ring[:, n % 4]).then_inc(h_hi_ready, 1)
                if n % 2 == 0:
                    dve.wait_ge(h_hi_ready, n + 1)
                    dve.tensor_tensor(lo, t_ring[:, n % 4], hi.bitcast(F32), ALU.subtract).then_inc(split_even, 1)
            for j in range(AC):
                dve.wait_ge(mod_summed, j + 1)
                if j >= 2:
                    dve.wait_ge(mod_turned, j - 1)
                dve.tensor_copy(mrow[0:2, j % 2], banks[0:2, j % 2]).then_inc(mod_row, 1)
                if j == 2:
                    for t in range(4):
                        norm_row(t)
            dve.wait_ge(mod_turned, AC)
            mod_part(0, 2 * KT, 1)
            gains(0, KT, V_GATTN, 1)
            for n in range(NCH * KT):
                c, k = divmod(n, KT)
                split(n)
                if c + 1 < NCH and k < 4:
                    norm_row(4 * (c + 1) + k)

        @block.tensor
        def _(pe):
            pe.wait_ge(ident_ready, 1)
            pe.wait_ge(vec_in, 16)
            pe.transpose(banks[:, 2, 0:NV], vrow[0:NV, :], ident[0:NV, 0:NV]).then_inc(vec_turned, 1)
            pe.wait_ge(silu_ready, 1)

            def turn_mod(j):
                pe.wait_ge(mod_row, j + 2)
                for i in range(4):
                    a = 8 * j + 2 * i
                    last = pe.transpose(banks[:, 3, a:a + 2], mrow[0:2, j % 2, 128 * i:128 * i + 128], ident[0:2, 0:2])
                last.then_inc(mod_turned, 1)

            def turn_x(n):
                c, k = divmod(n, KT)
                pe.wait_ge(x_normed, 4 * c + 4)
                if n >= 4:
                    pe.wait_ge(t_ready, n - 3)
                for i in range(4):
                    last = pe.transpose(banks[:, X_BANKS[n % 4], 128 * i:128 * i + 128],
                                        x[:, 4 * c + i, 128 * k:128 * k + 128], ident[:])
                last.then_inc(x_turned, 1)

            for j in range(AC):
                pe.wait_ge(ada_in[j % 3], 16 * (j // 3 + 1))
                if j >= 2:
                    pe.wait_ge(mod_row, j)
                for k in range(KT):
                    last = pe.matmul(banks[0:2, j % 2], silu_c[:, :, k], ada[:, j % 3, k],
                                     start=(k == 0), stop=(k == KT - 1))
                last.then_inc(mod_summed, 1)
                if j:
                    turn_mod(j - 1)
            turn_mod(AC - 1)
            for n in range(NCH * KT):
                turn_x(n)


def projections(nc, at, sem, banks, kept):
    w_in, u_scratch, h_hi, h_lo, vec, gq8 = kept.w_in, kept.u_scratch, kept.h_hi, kept.h_lo, kept.vec, kept.gq8
    ones_head, eps_t = kept.ones_head, kept.eps_t
    w_ada, b_ada, gate_rows, gate_stored, mod, coef = kept.w_ada, kept.b_ada, kept.gate_rows, kept.gate_stored, kept.mod, kept.coef
    w_raw, w_in_s, c_split, pick = kept.w_raw, kept.w_in_s, kept.c_split, kept.pick
    kept.z = z = at("z", [128, 3 * FT * T], F32, X_AT)
    W = X_AT + 73728
    w_hi = at("win_hi", [128, 2, KT, 128], F32R, W)
    sq_hi = at("sq_hi", [128, 2, CH], F32R, W + 8192)
    sq_lo = at("sq_lo", [128, 2, CH], F32R, W + 12288)
    u_stage = at("u_stage", [128, 2, CH], F32, W + 16384)
    sq = at("sq", [128, 2, CH], F32, W + 20480)
    w_lo = at("win_lo", [128, 2, KT, 128], F32R, WIN_RAW_AT)
    rms = at("rms", [128, 2, CH], F32, W + 32768)
    ada_hi = at("ada_hi", [128, 4, KT // 2, 512], F32R, X_AT)
    ada_lo = at("ada_lo", [128, 4, KT // 2, 512], F32R, X_AT + 32768)
    ada_raw = at("ada_raw", [128, 4, KT // 2, 512], F32, X_AT + 32768)
    mrow = at("mrow2", [128, 512], F32, X_AT + 65536)
    gate_row = at("gate_row", [128, D], F32, X_AT + 67584)
    STEPS = 2 * 6
    ADA_REST = 12 - ADA_FIRST
    PIECES = 2 * ADA_REST
    GATE1, SHIFT2, SCALE2, GATE2 = 2, 3, 4, 5

    def is_gate(m):
        return (m + ADA_FIRST) // 2 in (GATE1, GATE2)

    def gates_before(m):
        return sum(is_gate(i) for i in range(m))

    def step_of(piece):
        return (1, 2, 3, 3, 4, 5, 6, 6, 7, 8, 9, 9, 10, 10, 11, 11)[piece]

    def pieces_at(n):
        return [q for q in range(PIECES) if step_of(q) == n]

    def split_at(n):
        return [q + 4 for q in pieces_at(n - 1) if q + 4 < PIECES]

    def chunks_at(n):
        return [q // 2 for q in pieces_at(n) if q % 2]

    w_hi_s, w_ready = sem("win_hi_ready"), sem("win_ready")
    z_summed, bank_free = sem("z_summed"), sem("z_bank_free")
    u_stored = [sem(f"u_stored{s}") for s in range(2)]
    sq_hi_s, sq_lo_s = sem("sq_hi_s"), sem("sq_lo_s")
    ada_in, ada_hi_s, ada_ready = [sem(f"ada_rest_in{i}") for i in range(4)], sem("ada_hi_s"), sem("ada_ready")
    ada_used, mod_row, mod_turned, mod_ready = (sem("rest_" + n) for n in ("used", "row", "turned", "ready"))
    gate_bias_in, gate_picked, gate_ready = sem("gate_bias_in"), sem("gate_picked"), sem("gate_ready")
    ss_summed, rms_ready, rinv_ready, qk_normed = sem("ss_summed"), sem("rms_ready"), sem("rinv_ready"), sem("qk_normed")
    J_U, J_QK, J_V = FT // 2, 3 * FT // 2, 2 * FT

    with nc.Block() as block:
        @block.sync
        def _(sp):
            def load(j, s):
                sp.dma_start(w_raw[:, s], w_in[:, bass.ds((2 * j + s) * 128, 128)].rearrange("(k p) n -> p k n", p=128)
                             ).then_inc(w_in_s[s], 16)

            def load_ada(q):
                j, rows = q // 2 + ADA_FIRST, slice(D // 2 * (q % 2), D // 2 * (q % 2) + D // 2)
                sp.dma_start(ada_raw[:, q % 4], w_ada[rows, 512 * j:512 * j + 512].rearrange("(k p) n -> p k n", p=128)
                             ).then_inc(ada_in[q % 4], 16)

            def load_gate_bias(vector):
                sp.dma_start(gate_row[0:2, :], bass.AP(b_ada.tensor, vector * D, [[0, 2], [1, D]])).then_inc(gate_bias_in, 16)

            def store_gate(n):
                sp.wait_ge(gate_ready, 2 * (n + 1))
                sp.dma_start(gate_rows[n], gate_row[0:2, :]).then_inc(gate_stored, 16)
            load_gate_bias(GATE1)
            for q in range(4):
                load_ada(q)
            for n in range(STEPS):
                if n % 3 == 2:
                    sp.wait_ge(z_summed, n + 1)
                    load(n // 6 + 1, n % 6 // 3)
                for q in pieces_at(n):
                    if q + 4 < PIECES:
                        sp.wait_ge(ada_used, q + 1)
                        load_ada(q + 4)
                if n == step_of(7):
                    store_gate(0)
                if n == step_of(9):
                    sp.wait_ge(gate_stored, 16)
                    load_gate_bias(GATE2)
            store_gate(1)
            with sp.Fori(3, J_V) as j:
                for s in range(2):
                    sp.wait_ge(z_summed, 6 * (j - 1) + 3 * s + 3)
                    load(j, s)

        @block.gpsimd
        def _(pool):
            def store(j):
                for i in range(6):
                    s, c = divmod(i, NCH)
                    pool.wait_ge(bank_free, 6 * j + i + 1)
                    pool.dma_start(u_scratch[bass.ds((2 * j + s) * 128, 128), CH * c:CH * c + CH],
                                   u_stage[:, i % 2]).then_inc(u_stored[i % 2], 16)

            def sq_lows(j):
                for i in range(6):
                    n = 6 * j + i
                    pool.wait_ge(sq_hi_s, n + 1)
                    after(pool, ss_summed, n - 1)
                    pool.tensor_tensor(sq_lo[:, i % 2], sq[:, i % 2], sq_hi[:, i % 2].bitcast(F32), ALU.subtract
                                       ).then_inc(sq_lo_s, 1)
            rounds(pool, 0, J_U, store)
            rounds(pool, 0, J_QK - J_U, sq_lows)
            for s in range(2):
                pool.wait_ge(u_stored[s], 16 * 3 * J_U)

        def split_hi(act, j, s):
            act.wait_ge(w_in_s[s], 16 * j + 16)
            act.activation(w_hi[:, s], w_raw[:, s], ACT.Copy).then_inc(w_hi_s, 1)

        def split_lo(dve, j, s):
            dve.wait_ge(w_hi_s, 2 * j + s + 1)
            dve.tensor_tensor(w_lo[:, s], w_raw[:, s], w_hi[:, s].bitcast(F32), ALU.subtract).then_inc(w_ready, 1)

        def late_split(eng, split, j, i):
            if i == 3:
                split(eng, j + 1, 0)
            if i == 0 and j:
                split(eng, j, 1)

        def before(do, j, i):
            if i:
                if not isinstance(j, int) or J_U <= j < J_QK:
                    do(j, i - 1)
            elif not isinstance(j, int) or J_U < j <= J_QK:
                do(j - 1, 5)

        def z_at(j, s, c):
            return z[:, bass.ds(((2 * (j - J_U) + s) * NCH + c) * CH, CH)]

        @block.scalar
        def _(act):
            def evacuate(j, i, kind):
                s, c = divmod(i, NCH)
                act.wait_ge(z_summed, 6 * j + i + 1)
                if kind == "u":
                    after(act, u_stored[i % 2], 16 * (3 * j + i // 2))
                    act.activation(u_stage[:, i % 2], banks[:, i], ACT.Copy).then_inc(bank_free, 1)
                elif kind == "v":
                    act.activation(z_at(j, s, c), banks[:, i], ACT.Copy).then_inc(bank_free, 1)
                else:
                    n = 6 * (j - J_U) + i
                    act.activation(z_at(j, s, c), banks[:, i], ACT.Copy)
                    after(act, sq_lo_s, n - 1)
                    act.activation(sq[:, i % 2], banks[:, i], ACT.Square).then_inc(bank_free, 1)

            def root(j, i):
                n = 6 * (j - J_U) + i
                act.wait_ge(ss_summed, n + 1)
                after(act, qk_normed, n - 1)
                act.activation(rms[:, i % 2], banks[:, 6 + i % 2], ACT.Sqrt, scale=1.0 / HEAD, bias=eps_t[:]
                               ).then_inc(rms_ready, 1)

            def pair(j, kind, more):
                for i in range(6):
                    if kind == "u":
                        for q in split_at(6 * j + i):
                            ada_split_hi(q)
                    evacuate(j, i, kind)
                    before(root, j, i)
                    if kind == "u":
                        late_split(act, split_hi, j, i)
                    elif i % 3 == 2 and more:
                        split_hi(act, j + 1, i // 3)

            def ada_split_hi(q):
                act.wait_ge(ada_in[q % 4], 16 * (q // 4) + 16)
                act.activation(ada_hi[:, q % 4], ada_raw[:, q % 4], ACT.Copy).then_inc(ada_hi_s, 1)
            split_hi(act, 0, 0)
            split_hi(act, 0, 1)
            for q in range(4):
                ada_split_hi(q)
            pair(0, "u", True)
            pair(1, "u", True)
            split_hi(act, 2, 1)
            rounds(act, J_U, J_QK, lambda j: pair(j, "qk", True))
            for j in range(J_QK, J_V):
                pair(j, "v", j + 1 < J_V)

        @block.vector
        def _(dve):
            def sq_split(j, i):
                n = 6 * (j - J_U) + i
                dve.wait_ge(bank_free, 6 * j + i + 1)
                after(dve, ss_summed, n - 1)
                dve.tensor_copy(sq_hi[:, i % 2], sq[:, i % 2]).then_inc(sq_hi_s, 1)

            def qk_norm(j, i, gain):
                s, c = divmod(i, NCH)
                n = 6 * (j - J_U) + i
                dve.wait_ge(rms_ready, n + 1)
                dve.reciprocal(rms[:, i % 2], rms[:, i % 2]).then_inc(rinv_ready, 1)
                dve.wait_ge(rinv_ready, n + 1)
                zz = z_at(j, s, c)
                dve.scalar_tensor_tensor(zz, zz, gain, rms[:, i % 2], ALU.mult, ALU.mult).then_inc(qk_normed, 1)

            def splits(j, i):
                if i % 3 == 2:
                    split_lo(dve, j + 1, i // 3)
            split_lo(dve, 0, 0)
            split_lo(dve, 0, 1)

            def ada_split_lo(q):
                dve.wait_ge(ada_hi_s, q + 1)
                dve.tensor_tensor(ada_lo[:, q % 4], ada_raw[:, q % 4], ada_hi[:, q % 4].bitcast(F32), ALU.subtract
                                  ).then_inc(ada_ready, 1)

            def mod_rows(m):
                dve.wait_ge(ada_used, 2 * m + 2)
                if m:
                    if is_gate(m - 1):
                        dve.wait_ge(gate_picked, gates_before(m))
                    else:
                        dve.wait_ge(mod_turned, m - gates_before(m))
                dve.tensor_copy(mrow[0:4, :], banks[0:4, 6]).then_inc(mod_row, 1)

            def finish(m):
                if is_gate(m):
                    n = gates_before(m)
                    part = gate_row[0:2, 512 * (n % 2):512 * (n % 2) + 512]
                    dve.wait_ge(gate_bias_in, 16 * (n // 2) + 16)
                    dve.wait_ge(gate_picked, n + 1)
                    dve.tensor_tensor(part, banks[0:2, 7], part, ALU.add).then_inc(gate_ready, 1)
                if m == 2 * SCALE2 + 1 - ADA_FIRST:
                    dve.wait_ge(mod_turned, 4)
                    a, b = SHIFT2 * KT, GATE2 * KT
                    dve.tensor_tensor(mod[:, a:b], banks[:, 7, 0:2 * (b - a)].rearrange("p (j r) -> p j r", r=2),
                                      bass.AP(vec, V_BADA + a, [[96, 128], [1, b - a], [0, 2]]), ALU.add).then_inc(mod_ready, 1)
                    dve.wait_ge(mod_ready, 1)
                    dve.scalar_tensor_tensor(coef[:, 1], mod[:, SCALE2 * KT:GATE2 * KT], 1.0,
                                             bass.AP(vec, V_GFFN, [[96, 128], [1, KT], [0, 2]]), ALU.add, ALU.mult
                                             ).then_inc(mod_ready, 1)
            for q in range(4):
                ada_split_lo(q)
            for n in range(STEPS):
                for q in split_at(n):
                    ada_split_lo(q)
                late_split(dve, split_lo, n // 6, n % 6)
                for m in chunks_at(n - 1):
                    finish(m)
                for m in chunks_at(n):
                    mod_rows(m)
            finish(ADA_REST - 1)
            split_lo(dve, 2, 1)
            k_first = J_U + FT // 2

            def head_norm(j, i, gain):
                sq_split(j, i)
                first_k = isinstance(j, int) and j == k_first and i == 0
                before(lambda jj, ii: qk_norm(jj, ii, gq8[:] if first_k else gain), j, i)
                splits(j, i)

            def q_pair(j):
                for i in range(6):
                    head_norm(j, i, gq8[:])

            def k_pair(j):
                for i in range(6):
                    head_norm(j, i, vec[:, V_GK:V_GK + 1])
            rounds(dve, J_U, k_first, q_pair)
            rounds(dve, k_first, J_QK, k_pair)
            qk_norm(J_QK - 1, 5, vec[:, V_GK:V_GK + 1])
            with dve.Fori(J_QK, J_V - 1) as j:
                for i in range(6):
                    splits(j, i)

        @block.tensor
        def _(pe):
            def tile(j, i):
                s, c = divmod(i, NCH)
                if c == 0:
                    pe.wait_ge(w_ready, 2 * j + s + 1)
                after(pe, bank_free, 6 * (j - 1) + i + 1)
                for k in range(KT):
                    last = mm3(pe, banks[:, i], (w_hi[:, s, k], w_lo[:, s, k]),
                               (h_hi[:, k, CH * c:CH * c + CH], h_lo[:, k, CH * c:CH * c + CH]), k == 0, k == KT - 1)
                last.then_inc(z_summed, 1)

            def head_sums(j, i):
                n = 6 * (j - J_U) + i
                pe.wait_ge(sq_lo_s, n + 1)
                after(pe, rms_ready, n - 1)
                pe.matmul(banks[:, 6 + i % 2], ones_head[:], sq_hi[:, i % 2], start=True, stop=False)
                pe.matmul(banks[:, 6 + i % 2], ones_head[:], sq_lo[:, i % 2], start=False, stop=True
                          ).then_inc(ss_summed, 1)

            def tiles(j, i):
                tile(j, i)
                before(head_sums, j, i)
            def mod_products(q):
                m = q // 2
                pe.wait_ge(ada_ready, q + 1)
                if q % 2 == 0 and m:
                    pe.wait_ge(mod_row, m)
                for i in range(KT // 2):
                    k = KT // 2 * (q % 2) + i
                    pe.matmul(banks[0:4, 6], c_split[:, k], ada_hi[:, q % 4, i], start=k == 0, stop=False)
                    last = pe.matmul(banks[0:4, 6], c_split[:, k], ada_lo[:, q % 4, i], start=False, stop=k == KT - 1)
                last.then_inc(ada_used, 1)

            def turn_mod(m):
                pe.wait_ge(mod_row, m + 1)
                if is_gate(m):
                    n = gates_before(m)
                    if n:
                        pe.wait_ge(gate_ready, n)
                    if n == 2:
                        pe.wait_ge(mod_ready, 1)
                    pe.matmul(banks[0:2, 7], pick[0:4, :], mrow[0:4, :], start=True, stop=True).then_inc(gate_picked, 1)
                else:
                    pe.wait_ge(gate_ready, 2)
                    for i in range(4):
                        a = 2 * (4 * (m + ADA_FIRST) + i - SHIFT2 * KT)
                        last = pe.matmul(banks[:, 7, a:a + 2], mrow[0:4, 128 * i:128 * i + 128], pick[0:4, :],
                                         start=True, stop=True)
                    last.then_inc(mod_turned, 1)

            def plain(j):
                for i in range(6):
                    tiles(j, i)
                    if j < 2:
                        for m in chunks_at(6 * j + i - 1):
                            turn_mod(m)
                        for q in pieces_at(6 * j + i):
                            mod_products(q)

            def normed(j):
                for i in range(6):
                    tiles(j, i)
            plain(0)
            plain(1)
            turn_mod(ADA_REST - 1)
            pe.wait_ge(gate_ready, 4)
            rounds(pe, J_U, J_QK, normed)
            plain(J_QK)
            plain(J_QK + 1)


def attention(nc, at, sem, banks, kept):
    z, rpb_pad, masks, ident = kept.z, kept.rpb_pad, kept.masks, kept.ident
    kept.a_out = a_out = at("a_out", [128, FT * T], F32, H_LO)
    mask = at("mask", [128, NB * MASK_COLS], F32, BASE + 24576)
    v_tok = at("v_tok", [128, NB * NVT, 128], F32, BASE + 40960)
    v_pair = at("v_pair", [128, 2, T // 2], F32, BASE + 53248)
    q_pair = at("q_pair", [128, 2, NB, NCH, 128], F32, BASE + 65536)
    m_ring = at("m_ring", [128, 4, 384], F32, BASE + 77824)
    s_ring = at("s_ring", [128, 4, 384], F32, BASE + 83968)
    pt_ring = at("pt_ring", [128, 3, 384], F32, BASE + 90112)
    stats = at("stats", [128, 3, UNITS], F32, BASE + 94720)
    bias_next = at("bias_next", [128, BIAS_E * 2 * BIAS_X], F32, BASE + 172032)
    bias_pair = at("bias_pair", [128, BIAS_E, 2, BIAS_X], F32, BASE + 196608)
    BLOCK = UNITS // NB

    bias_in, mask_in = sem("bias_in"), [sem(f"mask_in{b}") for b in range(NB)]
    q_zeroed, v_staged, v_turned = sem("q_zeroed"), sem("v_staged"), sem("v_turned")
    q_dve, q_act, v_dve, v_act = sem("q_dve"), sem("q_act"), sem("v_dve"), sem("v_act")
    bias_staged = sem("bias_staged")
    masked_bias, qk_done, scored, exped, recip_done, normed = (
        sem(n) for n in ("masked_bias", "qk_done", "scored", "exped", "recip_done", "normed"))
    p_turned, pt_copied, pv_done, o_copied = (sem(n) for n in ("p_turned", "pt_copied", "pv_done", "o_copied"))

    def unit(u):
        b, c, hh = u // BLOCK, u % BLOCK // 2, u % 2
        return b, c, hh, KEY_ROWS[c], KEY_ROWS[c] * KCOLS

    def since(p, u, back, per=UNITS):
        return per * p + u - back + 1

    def each(p, n, per, do):
        q = p + n // per
        if not isinstance(q, int) or 0 <= q < FT:
            do(q, n % per)

    def staging(p, s, lead, do):
        if (s + lead) % BLOCK == 0:
            each(p, (s + lead) // BLOCK, NB, do)

    def block_free(eng, done, p, b):
        after(eng, done, UNITS * (p - 1) + BLOCK * (b + 1))

    def pairs(eng, body):
        body(0)
        with eng.Fori(1, FT - 1) as p:
            body(p)
        body(FT - 1)

    def steps(p, drain):
        return range(UNITS + (drain if isinstance(p, int) and p == FT - 1 else 0))
    LEAD_COPY, LEAD_TURN, LEAD_READY = 9, 7, 5

    with nc.Block() as block:
        @block.sync
        def _(sp):
            for p in range(FT):
                if p:
                    sp.wait_ge(bias_staged, p)
                for i in range(QROWS):
                    src = bass.AP(rpb_pad.tensor, (p * RP_ROWS + 7 - i) * 2 * RP_COLS,
                                  [[1, QCOLS], [RP_COLS, BIAS_E * 2], [1, BIAS_X]])
                    sp.dma_start(bias_next[QCOLS * i:QCOLS * i + QCOLS, :].rearrange("p (eh x) -> p eh x", x=BIAS_X),
                                 src).then_inc(bias_in, 16)
                if p == 0:
                    for b in range(NB):
                        cols = slice(MASK_COLS * b, MASK_COLS * b + MASK_COLS)
                        sp.dma_start(mask[:, cols], masks[:, cols]).then_inc(mask_in[b], 16)

        @block.gpsimd
        def _(pool):
            def head_pair(p):
                pool.wait_ge(bias_staged, p + 1)
                for u in range(UNITS):
                    b, c, hh, rows, n = unit(u)
                    if isinstance(p, int) and p == 0 and u % BLOCK == 0:
                        pool.wait_ge(mask_in[b], 16)
                    after(pool, scored, since(p, u, 4))
                    e0 = 0 if c == 2 else 4
                    x0 = KEY_COL[b] - QCOLS * b + 16
                    tab = bias_pair[:, e0:e0 + rows, hh, x0:x0 + KCOLS]
                    k0 = b * MASK_COLS + sum(KEY_ROWS[:c]) * KCOLS
                    pool.tensor_tensor(m_ring[:, u % 4, 0:n].rearrange("p (e x) -> p e x", e=rows),
                                       mask[:, k0:k0 + n].rearrange("p (e x) -> p e x", e=rows), tab, ALU.subtract
                                       ).then_inc(masked_bias, 1)
            rounds(pool, 0, FT, head_pair)

        @block.scalar
        def _(act):
            def copy_q(p, b):
                block_free(act, qk_done, p, b)
                src = z[64:128, bass.ds(p * T, T)].rearrange("p (r b w) -> p b r w", b=NB, w=QCOLS)[:, b]
                act.activation(q_pair[64:128, 1, b].rearrange("p c (r w) -> p (c r) w", w=QCOLS)[:, :, ::-1], src, ACT.Copy
                               ).then_inc(q_act, 1)

            def values_ready(p, b):
                act.wait_ge(v_turned, 2 * (NB * p + b) + 1)
                block_free(act, pv_done, p, b)
                act.activation(v_tok[:, NVT * b:NVT * b + 4], banks[:, 6].rearrange("p (t f) -> p t f", f=128), ACT.Copy
                               ).then_inc(v_act, 1)

            def exp(p, u):
                n = unit(u)[4]
                act.wait_ge(scored, since(p, u, 0))
                act.activation(s_ring[:, u % 4, 0:n], s_ring[:, u % 4, 0:n], ACT.Exp, scale=-1.0,
                               bias=stats[:, 0, u:u + 1], accum_out=stats[:, 1, u:u + 1]).then_inc(exped, 1)

            def copy_pt(p, u):
                n = unit(u)[4]
                act.wait_ge(p_turned, since(p, u, 0))
                after(act, pv_done, since(p, u, 3))
                act.activation(pt_ring[:, u % 3, 0:n], banks[:, 2 + u % 2, 0:n], ACT.Copy).then_inc(pt_copied, 1)

            def copy_o(p, v):
                b, c = unit(2 * v)[:2]
                act.wait_ge(pv_done, since(p, 2 * v + 1, 0))
                dst = a_out[:, bass.ds(p * T + c * CH, CH)].rearrange("p (r b w) -> p b r w", b=NB, w=QCOLS)[:, b]
                act.activation(dst, banks[:, 4 + v % 2, 0:128].rearrange("p (r w) -> p r w", w=QCOLS)[:, :, ::-1], ACT.Copy
                               ).then_inc(o_copied, 1)

            def head_pair(p):
                for s in steps(p, 5):
                    if s < UNITS:
                        exp(p, s)
                    each(p, s - 3, UNITS, copy_pt)
                    if s % 2 == 0:
                        each(p, (s - 6) // 2, UNITS // 2, copy_o)
                    staging(p, s, LEAD_COPY, copy_q)
                    staging(p, s, LEAD_READY, values_ready)
            act.wait_ge(q_zeroed, 2)
            copy_q(0, 0)
            values_ready(0, 0)
            copy_q(0, 1)
            pairs(act, head_pair)

        @block.vector
        def _(dve):
            def copy_qv(p, b):
                m = NB * p + b
                after(dve, v_turned, 2 * m - 2)
                src = z[:, bass.ds((2 * FT + p) * T, T)].rearrange("p (r w) -> p r w", w=GRID_W)[
                    :, :, KEY_COL[b]:KEY_COL[b] + KCOLS]
                dve.tensor_copy(v_pair[:, b % 2].rearrange("p (r w) -> p r w", w=KCOLS), src).then_inc(v_staged, 1)
                block_free(dve, qk_done, p, b)
                src = z[0:64, bass.ds(p * T, T)].rearrange("p (r b w) -> p b r w", b=NB, w=QCOLS)[:, b]
                dve.tensor_copy(q_pair[0:64, 0, b].rearrange("p c (r w) -> p (c r) w", w=QCOLS)[:, :, ::-1], src
                                ).then_inc(q_dve, 1)

            def values_ready(p, b):
                dve.wait_ge(v_turned, 2 * (NB * p + b) + 2)
                block_free(dve, pv_done, p, b)
                dve.tensor_copy(v_tok[:, NVT * b + 4:NVT * b + 6], banks[:, 7, 0:256].rearrange("p (t f) -> p t f", f=128)
                                ).then_inc(v_dve, 1)

            def copy_bias(p):
                after(dve, masked_bias, UNITS * p)
                dve.wait_ge(bias_in, 16 * QROWS * (p + 1))
                dve.tensor_copy(bias_pair[:].rearrange("p e h x -> p (e h x)"), bias_next[:]).then_inc(bias_staged, 1)

            def ready(p, u):
                dve.wait_ge(qk_done, since(p, u, 0))
                dve.wait_ge(masked_bias, since(p, u, 0))
                after(dve, p_turned, since(p, u, 4))

            def score(p, u):
                n = unit(u)[4]
                dve.tensor_tensor_reduce(s_ring[:, u % 4, 0:n], banks[:, u % 2, 0:n], m_ring[:, u % 4, 0:n], 1.0,
                                         3e38, ALU.add, ALU.min, stats[:, 0, u:u + 1]).then_inc(scored, 1)

            def norm(p, u, following):
                n = unit(u)[4]
                dve.wait_ge(exped, since(p, u, 0))
                dve.reciprocal(stats[:, 2, u:u + 1], stats[:, 1, u:u + 1]).then_inc(recip_done, 1)
                dve.wait_ge(recip_done, since(p, u, 0))
                if following:
                    ready(*following)
                dve.tensor_scalar(s_ring[:, u % 4, 0:n], s_ring[:, u % 4, 0:n], stats[:, 2, u:u + 1], None, ALU.mult
                                  ).then_inc(normed, 1)

            def head_pair(p):
                for s in steps(p, 2):
                    following = (p, s) if s < UNITS else None
                    if isinstance(p, int) and p == 0 and s < 2:
                        ready(p, s)
                    each(p, s - 2, UNITS, lambda q, u: norm(q, u, following))
                    if following:
                        score(p, s)
                    staging(p, s, LEAD_COPY, copy_qv)
                    staging(p, s, LEAD_READY, values_ready)
                    if s == UNITS - 2:
                        each(p, 1, 1, lambda q, _: copy_bias(q))
            dve.memset(q_pair[64:128, 0], 0.0).then_inc(q_zeroed, 1)
            dve.memset(q_pair[0:64, 1], 0.0).then_inc(q_zeroed, 1)
            copy_qv(0, 0)
            copy_qv(0, 1)
            copy_bias(0)
            values_ready(0, 0)
            pairs(dve, head_pair)

        @block.tensor
        def _(pe):
            def turn_v(p, b):
                m = NB * p + b
                pe.wait_ge(v_staged, m + 1)
                for t in range(NVT):
                    if t == 0:
                        after(pe, v_act, m)
                    if t == 4:
                        after(pe, v_dve, m)
                    last = pe.transpose(banks[:, 6 + t // 4, 128 * (t % 4):128 * (t % 4) + 128],
                                        v_pair[:, b % 2, 128 * t:128 * t + 128], ident[:])
                    if t in (3, NVT - 1):
                        last.then_inc(v_turned, 1)

            def scores(p, u):
                b, c, hh, rows, n = unit(u)
                if u % BLOCK == 0:
                    pe.wait_ge(q_dve, NB * p + b + 1)
                    pe.wait_ge(q_act, NB * p + b + 1)
                after(pe, scored, since(p, u, 2))
                keys = z[:, bass.ds((FT + p) * T + KEY_TOKEN0[c], rows * GRID_W)].rearrange(
                    "p (r w) -> p r w", w=GRID_W)[:, :, KEY_COL[b]:KEY_COL[b] + KCOLS]
                pe.matmul(banks[:, u % 2, 0:n], q_pair[:, hh, b, c], keys, start=True, stop=True).then_inc(qk_done, 1)

            def turn(p, u):
                rows = unit(u)[3]
                pe.wait_ge(normed, since(p, u, 0))
                after(pe, pt_copied, since(p, u, 2))
                for j in range(rows // 4):
                    last = pe.transpose(banks[:, 2 + u % 2, 128 * j:128 * j + 128],
                                        s_ring[:, u % 4, 128 * j:128 * j + 128], ident[:])
                last.then_inc(p_turned, 1)

            def values(p, u):
                b, c, hh, rows, n = unit(u)
                v = u // 2
                if u % BLOCK == 0:
                    pe.wait_ge(v_act, NB * p + b + 1)
                    pe.wait_ge(v_dve, NB * p + b + 1)
                pe.wait_ge(pt_copied, since(p, u, 0))
                after(pe, o_copied, since(p, v, 2, UNITS // 2))
                for j in range(rows // 4):
                    last = pe.matmul(banks[64 * hh:64 * hh + 64, 4 + v % 2, 0:128],
                                     v_tok[:, b * NVT + V_TILE0[c] + j, 64 * hh:64 * hh + 64],
                                     pt_ring[:, u % 3, 128 * j:128 * j + 128], start=(j == 0), stop=(j == rows // 4 - 1))
                last.then_inc(pv_done, 1)

            def head_pair(p):
                for s in steps(p, 4):
                    each(p, s + 1, UNITS, scores)
                    each(p, s - 3, UNITS, turn)
                    each(p, s - 4, UNITS, values)
                    staging(p, s, LEAD_TURN, turn_v)
            turn_v(0, 0)
            turn_v(0, 1)
            scores(0, 0)
            pairs(pe, head_pair)


def fourier(nc, at, sem, banks, kept):
    u_scratch, w_fmix, dft_c, dft_t1, dft_t0 = kept.u_scratch, kept.w_fmix, kept.dft_c, kept.dft_t1, kept.dft_t0
    a_out, vec, ones_all, h_hi, h_lo, w_o = kept.a_out, kept.vec, kept.ones_all, kept.h_hi, kept.h_lo, kept.w_o
    wo_hi, wo_lo, wo_raw = (at(f"wo_{n}0", [128, KT, NO], dt, WO_AT[0][n != "hi"])
                            for n, dt in (("hi", F32R), ("lo", F32R), ("raw", F32)))
    kept.wo_hi0, kept.wo_lo0, kept.wo_raw0 = wo_hi, wo_lo, wo_raw
    f_out = at("f_out", [128, FT, T], F32, H_LO + 24576)
    u = at("u", [128, FT, T], F32, H_HI + 24576)
    pq = at("pq", [128, TT // 2, 2, FT, 128], F32, BASE + 98304)
    uo = at("uo", [128, FT, T // 2], F32, BASE + 122880)
    tab1 = at("tab1", [128, 2, T_SAMPLE // 256, T_SAMPLE // 2], F32, BASE + 135168)
    tab0 = at("tab0", [128, 2, T_PROMPT // 256, T_PROMPT // 2], F32, BASE + 151552)
    maps = at("maps", [128, 2, FT, 128], F32, BASE + 172032)
    f_sq = at("f_sq", [128, T_SAMPLE], F32, BASE + 172032)
    b_ring = at("b_ring", [128, 2, CH], F32, BASE + 176128)
    wf = at("wf", [128, FT, 128], F32, BASE + 176128)
    cs = at("cs", [128, 256], F32, BASE + 180224)
    signs = at("signs", [128, CH], F32, BASE + 181248)
    alt = at("alt", [128, 2, FT, 2], F32, BASE + 183296)
    edge = at("edge", [128, FT, 4], F32, BASE + 183360)
    mid = at("mid", [128, FT, 2], F32, BASE + 183424)
    a_sq = at("a_sq", [128, 2, CH], F32, BASE + 192512)
    kept.sq_sum = sq_sum = at("sq_sum", [128, 2, T], F32, SQ_SUM_AT)
    REQS = [(0, T_PROMPT, tab0), (T_PROMPT, T_SAMPLE, tab1)]
    TILES_PQ = TT // 2

    u_in = [sem(f"u_in{c}") for c in range(2)]
    wf_in, cs_in, tab0_in, tab1_in, wo_in = (sem(n) for n in ("wf_in", "cs_in", "tab0_in", "tab1_in", "wo_first_in"))
    wo_hi_s, wo_split = sem("wo_first_hi"), sem("wo_first_split")
    maps_summed, maps_ready, alt_sums, edge_ready, signs_ready = (
        sem(n) for n in ("maps_summed", "maps_ready", "alt_sums", "edge_ready", "signs_ready"))
    fold_odd, fold_even = sem("fold_odd"), sem("fold_even")
    pq_summed, p_ready, q_ready, edge_summed, half_ready = (
        sem(n) for n in ("pq_summed", "p_ready", "q_ready", "edge_summed", "half_ready"))
    ab_summed, a_ready, b_ready, f_upper, f_ready = (
        sem(n) for n in ("ab_summed", "a_ready", "b_ready", "f_upper", "f_ready"))
    a_squared, a_sq_added, a_sq_summed, a_hi_s, a_split = (
        sem(n) for n in ("a_squared", "a_sq_added", "a_sq_summed", "a_hi_s", "a_split"))
    f_squared, f_sq_added, f_hi_s, f_split = (sem(n) for n in ("f_squared", "f_sq_added", "f_hi_s", "f_split"))

    def a_part(n):
        i, c = divmod(n, NCH)
        return i, slice(CH * c, CH * c + CH), a_out[:, T * i + CH * c:T * i + CH * c + CH]

    def a_with(n):
        return range(TILES_PQ + n, TILES_PQ + n + 2) if n % 2 == 0 and n < TT - TILES_PQ else ()

    def group(n):
        return 1 - n % 2, n // 2

    with nc.Block() as block:
        @block.sync
        def _(sp):
            for r, (t0, t, _) in enumerate(REQS):
                cols = slice(t0, t0 + t)
                if r:
                    sp.dma_start(cs[:], dft_c).then_inc(cs_in, 16)
                    sp.dma_start(wf[:], w_fmix.rearrange("g c d -> c g d")).then_inc(wf_in, 16)
                sp.dma_start(u[:, :, cols], u_scratch[:, cols].rearrange("(g p) t -> p g t", p=128)).then_inc(u_in[r], 16)
            for half in range(2):
                sp.dma_start(tab0[:, half], dft_t0[half].rearrange("(t p) k -> p t k", p=128)).then_inc(tab0_in, 16)
            for half in range(2):
                sp.dma_start(tab1[:, half], dft_t1[half].rearrange("(t p) k -> p t k", p=128)).then_inc(tab1_in, 16)
            sp.dma_start(wo_raw[:], w_o[:, 0:NO].rearrange("(k p) n -> p k n", p=128)).then_inc(wo_in, 16)

        @block.scalar
        def _(act):
            def split_a(n):
                i, cols, part = a_part(n)
                if n >= NCH + 2:
                    act.wait_ge(a_sq_added, n - NCH - 1)
                act.activation(sq_sum[:, 0, cols] if i == 0 else a_sq[:, n % 2], part, ACT.Square).then_inc(a_squared, 1)
                act.activation(h_hi[:, i, cols], part, ACT.Copy, scale=vec[:, V_GA + i:V_GA + i + 1]).then_inc(a_hi_s, 1)

            def split_f(n):
                r, c = group(n)
                t0, t, _ = REQS[r]
                if n == 0:
                    act.wait_ge(half_ready, 2)
                act.wait_ge(f_ready, n + 1)
                act.activation(h_hi[:, FT + c, t0:t0 + t], f_out[:, c, t0:t0 + t], ACT.Copy,
                               scale=vec[:, V_GF + c:V_GF + c + 1]).then_inc(f_hi_s, 1)
                if n >= 3:
                    act.wait_ge(f_sq_added, n - 2)
                act.activation(sq_sum[:, 1, t0:t0 + t] if c == 0 else f_sq[:, 0:t], f_out[:, c, t0:t0 + t], ACT.Square
                               ).then_inc(f_squared, 1)
            act.wait_ge(maps_summed, 1)
            for half in range(2):
                act.activation(maps[:, half], banks[:, half].rearrange("p (g n) -> p g n", g=FT), ACT.Copy
                               ).then_inc(maps_ready, 1)
            for t in range(TILES_PQ):
                act.wait_ge(pq_summed, t + 1)
                act.activation(pq[:, t, 0], banks[:, 2 * (t % 2)].rearrange("p (g n) -> p g n", g=FT), ACT.Copy
                               ).then_inc(p_ready, 1)
                split_a(t)
            for n in range(2 * FT):
                r, c = group(n)
                k = REQS[r][1] // 2
                act.wait_ge(ab_summed, n + 1)
                if n >= 2:
                    act.wait_ge(f_ready, n - 1)
                act.activation(b_ring[:, n % 2, 0:k], banks[:, 5 + 2 * (n % 2), 0:k], ACT.Copy).then_inc(b_ready, 1)
                if n == 0:
                    act.wait_ge(edge_summed, 1)
                else:
                    split_f(n - 1)
                for i in a_with(n):
                    split_a(i)
                if n == FT - 1:
                    act.wait_ge(wo_in, 16)
                    act.activation(wo_hi[:], wo_raw[:], ACT.Copy).then_inc(wo_hi_s, 1)
            split_f(2 * FT - 1)

        @block.gpsimd
        def _(pool):
            def add_a(n):
                cols = a_part(n)[1]
                pool.wait_ge(a_squared, n + 1)
                if n >= 2 * NCH:
                    pool.wait_ge(a_sq_added, n - 2 * NCH + 1)
                pool.tensor_tensor(sq_sum[:, 0, cols], sq_sum[:, 0, cols], a_sq[:, n % 2], ALU.add).then_inc(a_sq_added, 1)

            def add_f(n):
                r, c = group(n)
                t0, t, _ = REQS[r]
                pool.wait_ge(f_squared, n + 1)
                if n >= 3:
                    pool.wait_ge(f_sq_added, n - 2)
                pool.tensor_tensor(sq_sum[:, 1, t0:t0 + t], sq_sum[:, 1, t0:t0 + t], f_sq[:, 0:t], ALU.add
                                   ).then_inc(f_sq_added, 1)
            for n in range(NCH, TILES_PQ):
                add_a(n)
            for n in range(2 * FT + 1):
                if n >= 3:
                    add_f(n - 1)
                for i in a_with(n):
                    add_a(i)

        @block.vector
        def _(dve):
            def fold(r):
                t0, t, _ = REQS[r]
                h = t // 2
                dve.wait_ge(u_in[r], 16)
                dve.tensor_copy(uo[:, :, t0 // 2:t0 // 2 + 1], u[:, :, t0:t0 + 1])
                dve.tensor_tensor(uo[:, :, t0 // 2 + 1:t0 // 2 + h], u[:, :, t0 + 1:t0 + h],
                                  u[:, :, t0 + h + 1:t0 + t][:, :, ::-1], ALU.subtract).then_inc(fold_odd, 1)
                dve.wait_ge(fold_odd, r + 1)
                dve.tensor_tensor(u[:, :, t0 + 1:t0 + h], u[:, :, t0 + 1:t0 + h],
                                  u[:, :, t0 + h + 1:t0 + t][:, :, ::-1], ALU.add).then_inc(fold_even, 1)

            def lo_a(n):
                i, cols, part = a_part(n)
                dve.wait_ge(a_squared, n + 1)
                dve.wait_ge(a_hi_s, n + 1)
                dve.scalar_tensor_tensor(h_lo[:, i, cols], part, vec[:, V_GA + i:V_GA + i + 1],
                                         h_hi[:, i, cols].bitcast(F32), ALU.mult, ALU.subtract).then_inc(a_split, 1)

            def copy_q(t):
                dve.wait_ge(pq_summed, t + 1)
                dve.tensor_copy(pq[:, t, 1], banks[:, 2 * (t % 2) + 1].rearrange("p (g n) -> p g n", g=FT)
                                ).then_inc(q_ready, 1)

            def lo_f(n):
                r, c = group(n)
                t0, t, _ = REQS[r]
                dve.wait_ge(f_hi_s, n + 1)
                dve.wait_ge(f_squared, n + 1)
                dve.scalar_tensor_tensor(h_lo[:, FT + c, t0:t0 + t], f_out[:, c, t0:t0 + t], vec[:, V_GF + c:V_GF + c + 1],
                                         h_hi[:, FT + c, t0:t0 + t].bitcast(F32), ALU.mult, ALU.subtract).then_inc(f_split, 1)
            dve.memset(signs[:].rearrange("p (k two) -> p k two", two=2)[:, :, 0], 1.0)
            dve.memset(signs[:].rearrange("p (k two) -> p k two", two=2)[:, :, 1], -1.0).then_inc(signs_ready, 1)
            fold(0)
            fold(1)
            for t in range(TILES_PQ):
                copy_q(t)
                lo_a(t)
                if t == 0:
                    dve.wait_ge(fold_even, 2)
                    for r, (t0, t_, _) in enumerate(REQS):
                        parts = u[:, :, t0:t0 + t_ // 2].rearrange("p g (t two) -> p g two t", two=2)
                        for odd in range(2):
                            dve.tensor_reduce(alt[:, odd, :, r:r + 1], parts[:, :, odd:odd + 1], AX.X, ALU.add
                                              ).then_inc(alt_sums, 1)
                        dve.tensor_copy(edge[:, :, 2 + r:3 + r], u[:, :, t0 + t_ // 2:t0 + t_ // 2 + 1]).then_inc(alt_sums, 1)
                    dve.wait_ge(alt_sums, 6)
                    dve.tensor_tensor(edge[:, :, 0:2], alt[:, 0], alt[:, 1], ALU.subtract).then_inc(alt_sums, 1)
                    dve.wait_ge(alt_sums, 7)
                    dve.tensor_tensor(edge[:, :, 0:2], edge[:, :, 0:2], edge[:, :, 2:4], ALU.add).then_inc(edge_ready, 1)
            dve.wait_ge(edge_summed, 1)
            for r, (t0, t, _) in enumerate(REQS):
                sums = banks[:, 0, 0:4 * FT].rearrange("p (g e) -> p g e", e=4)
                dve.tensor_scalar(f_out[:, :, t0 + t // 2:t0 + t // 2 + 1], sums[:, :, r:r + 1],
                                  t ** -0.5, None, ALU.mult)
                dve.tensor_scalar(mid[:, :, r:r + 1], sums[:, :, 2 + r:3 + r], t ** -0.5, None, ALU.mult).then_inc(half_ready, 1)
            dve.wait_ge(half_ready, 2)
            dve.wait_ge(signs_ready, 1)
            for n in range(2 * FT):
                r, c = group(n)
                t0, t, _ = REQS[r]
                k = t // 2
                part = f_out[:, c, t0:t0 + k]
                dve.wait_ge(ab_summed, n + 1)
                dve.scalar_tensor_tensor(part, signs[:, 0:k], mid[:, c, r:r + 1], banks[:, 4 + 2 * (n % 2), 0:k],
                                         ALU.mult, ALU.add).then_inc(a_ready, 1)
                dve.wait_ge(a_ready, n + 1)
                dve.wait_ge(b_ready, n + 1)
                dve.tensor_tensor(f_out[:, c, t0 + k + 1:t0 + t][:, ::-1], f_out[:, c, t0 + 1:t0 + k],
                                  b_ring[:, n % 2, 1:k], ALU.add).then_inc(f_upper, 1)
                dve.wait_ge(f_upper, n + 1)
                dve.tensor_tensor(part, part, b_ring[:, n % 2, 0:k], ALU.subtract).then_inc(f_ready, 1)
                if n:
                    lo_f(n - 1)
                for i in a_with(n):
                    lo_a(i)
                if n == FT - 1:
                    dve.wait_ge(wo_hi_s, 1)
                    dve.tensor_tensor(wo_lo[:], wo_raw[:], wo_hi[:].bitcast(F32), ALU.subtract).then_inc(wo_split, 1)
            lo_f(2 * FT - 1)

        @block.tensor
        def _(pe):
            pe.wait_ge(cs_in, 16)
            pe.wait_ge(wf_in, 16)
            for half in range(2):
                for c in range(FT):
                    last = pe.matmul(banks[:, half, 128 * c:128 * c + 128], cs[:, 128 * half:128 * half + 128], wf[:, c],
                                     start=True, stop=True)
            last.then_inc(maps_summed, 1)
            pe.wait_ge(maps_ready, 2)
            for t in range(TILES_PQ):
                r = 0 if t < T_PROMPT // 256 else 1
                pe.wait_ge(fold_even, r + 1)
                if t >= 2:
                    pe.wait_ge(p_ready, t - 1)
                    pe.wait_ge(q_ready, t - 1)
                n0 = 128 * t
                for half in range(2):
                    for c in range(FT):
                        tok = uo[:, c, n0:n0 + 128] if half else u[:, c, n0 + r * T_PROMPT // 2:n0 + r * T_PROMPT // 2 + 128]
                        last = pe.matmul(banks[:, 2 * (t % 2) + half, 128 * c:128 * c + 128], tok, maps[:, half, c],
                                         start=True, stop=True)
                last.then_inc(pq_summed, 1)
            pe.wait_ge(edge_ready, 1)
            pe.wait_ge(p_ready, TILES_PQ - 1)
            for c in range(FT):
                last = pe.matmul(banks[:, 0, 4 * c:4 * c + 4], maps[:, 0, c], edge[:, c], start=True, stop=True)
            last.then_inc(edge_summed, 1)
            pe.wait_ge(p_ready, TILES_PQ)
            pe.wait_ge(q_ready, TILES_PQ)
            for n in range(2 * FT):
                r, c = group(n)
                t0, t, tab = REQS[r]
                if c == 0:
                    pe.wait_ge((tab0_in, tab1_in)[r], 32)
                if n >= 2:
                    pe.wait_ge(b_ready, n - 1)
                    pe.wait_ge(a_ready, n - 1)
                for half in range(2):
                    for i in range(t // 256):
                        last = pe.matmul(banks[:, 4 + 2 * (n % 2) + half, 0:t // 2], pq[:, t0 // 256 + i, half, c],
                                         tab[:, half, i], start=(i == 0), stop=(i == t // 256 - 1))
                last.then_inc(ab_summed, 1)
                if n == 2 * FT - 1:
                    pe.wait_ge(a_sq_added, TT - NCH)
                    for t in range(TT):
                        last = pe.matmul(banks[:, 1, 2 * t:2 * t + 2], sq_sum[:, 0, 128 * t:128 * t + 128],
                                         ones_all[:, 0:2].bitcast(F32), start=True, stop=True)
                    last.then_inc(a_sq_summed, 1)


def second_half(nc, at, sem, banks, kept):
    x_prompt, x_sample, w_o, w_gate, w_up, w_down = kept.x_prompt, kept.x_sample, kept.w_o, kept.w_gate, kept.w_up, kept.w_down
    y_prompt, y_sample, mod, coef, ident, ones_all = kept.y_prompt, kept.y_sample, kept.mod, kept.coef, kept.ident, kept.ones_all
    eps_t, h_hi, h_lo = kept.eps_t, kept.h_hi, kept.h_lo
    sq_sum, gate_rows, gate_stored, stat = kept.sq_sum, kept.gate_rows, kept.gate_stored, kept.stat
    x1 = at("x1", [128, TT, D], F32, X_AT)
    gate2 = at("gate2", [128, 2, D], F32, GATE2_AT)
    wo_hi = [kept.wo_hi0, at("wo_hi1", [128, KT, NO], F32R, WO_AT[1][0])]
    wo_lo = [kept.wo_lo0, at("wo_lo1", [128, KT, NO], F32R, WO_AT[1][1])]
    wo_raw = [kept.wo_raw0, at("wo_raw1", [128, KT, NO], F32, WO_AT[1][1])]
    w_hi = at("wff_hi", [128, 3, D], F32R, REST + 24576)
    w_lo = at("wff_lo", [128, 3, D], F32R, REST + 36864)
    w_raw = at("wff_raw", [128, 3, D], F32, REST + 36864)
    xn = at("xn", [128, 4, D], F32, REST)
    gate1 = at("gate1", [128, OS, 2, NO], F32, REST + 16384)
    t_ring = at("t_second", [128, 2, CH], F32, REST + 16384)
    mix_ring = at("mix_ring", [128, 4, NO], F32, REST + 49152)
    ff_hi = at("ff_hi", [128, 2, T], F32R, REST)
    ff_lo = at("ff_lo", [128, 2, T], F32R, REST + 12288)
    ff_raw = at("ff_raw", [128, 2, T], F32, REST + 12288)
    scratch = at("ff_scratch", [128, 3, CH], F32, REST + 49152)
    mix_rstd = at("mix_rstd", [128, 2, 2 * TT], F32, KEEP + 1536)

    x_in, wo_in = [sem(f"x1_in{c}") for c in range(NCH)], [sem(f"wo_in{s}") for s in range(2)]
    wo_hi_s, wo_ready = sem("wo_hi_s"), sem("wo_ready")
    sq_summed, mix_rooted, mix_rstd_ready = sem("sq_summed"), sem("mix_rooted"), sem("mix_rstd_ready")
    gate1_in, gate2_in = sem("gate1_in"), sem("gate2_in")
    o_summed, f_scaled, a_scaled, gated, x1_added = (
        sem(n) for n in ("o_summed", "f_scaled", "a_scaled", "o_gated", "x1_added"))
    squared, rooted, rstd, xn_dve, xn_act, turned, t_ready, hi_ready, split_dve, split_pool = (
        sem("h2_" + n) for n in ("squared", "rooted", "rstd", "xn_dve", "xn_act", "turned", "t_ready", "hi_ready",
                                 "split_dve", "split_pool"))
    PAIRS = FF // 2
    GATE, UP, DOWN = 0, 1, 2
    TILES = [(GATE, 0), (UP, 0), (GATE, 1), (UP, 1), (DOWN, 0), (DOWN, 1)]
    w_in = [sem(f"wff_in{s}") for s in range(3)]
    w_split_hi, w_ready = sem("wff_split_hi"), sem("wff_ready")
    g_summed, u_summed, silu_ready, product, ff_hi_s, ff_ready = (
        sem("ff_" + n) for n in ("g_summed", "u_summed", "silu_ready", "product", "hi_s", "ready"))
    d_summed, d_gated, d_added, d_added_dve = (sem(n) for n in ("d_summed", "d_gated", "d_added", "d_added_dve"))
    y_stored = sem("y_stored")
    DG = 2 * TT
    NG, TB = 4, 4

    DV, DP = DG // 4, DG - DG // 4

    def on_dve(n):
        return n % 4 == 3

    def waits_added(eng, j, n):
        if n < 0:
            j, n = j - 1, n + DG
        if not (isinstance(j, int) and j < 0):
            if on_dve(n):
                eng.wait_ge(d_added_dve, DV * j + n // 4 + 1)
            else:
                eng.wait_ge(d_added, DP * j + n + 1 - (n + 1) // 4)

    def on_pool(n):
        return n < KT and n % 2 == 1

    def waits_split(eng, n):
        if on_pool(n):
            eng.wait_ge(split_pool, n // 2 + 1)
        else:
            eng.wait_ge(split_dve, n + 1 - min((n + 1) // 2, KT // 2))

    with nc.Block() as block:
        @block.sync
        def _(sp):
            def load_o(n):
                sp.dma_start(wo_raw[n % 2][:], w_o[:, NO * n:NO * n + NO].rearrange("(k p) n -> p k n", p=128)
                             ).then_inc(wo_in[n % 2], 16)

            def load(j, i):
                kind, f = TILES[i]
                if kind == DOWN:
                    src, dst = w_down[bass.ds((2 * j + f) * 128, 128), :], w_raw[:, i % 3]
                else:
                    src = (w_gate, w_up)[kind][:, bass.ds((2 * j + f) * 128, 128)].rearrange("(k p) n -> p k n", p=128)
                    dst = w_raw[:, i % 3].rearrange("p (k n) -> p k n", n=128)
                sp.dma_start(dst, src).then_inc(w_in[i % 3], 16)

            def used(j, i):
                kind, f = TILES[i]
                if kind == DOWN:
                    sp.wait_ge(d_summed, DG * j + DG)
                else:
                    sp.wait_ge((g_summed, u_summed)[kind], 6 * j + 3 * f + 3)

            def later(j):
                for i in range(6):
                    used(j, i)
                    load(j + (i + 3) // 6, (i + 3) % 6)
            def load_x(c):
                src = x_prompt if c == 0 else x_sample[CH * (c - 1):CH * c]
                sp.dma_start(x1[:, 4 * c:4 * c + 4], src.rearrange("(t p) n -> p t n", p=128)).then_inc(x_in[c], 16)
            sp.wait_ge(gate_stored, 32)
            for r in range(2):
                row = bass.AP(gate_rows.tensor, r * D, [[0, 128], [NO, OS], [1, NO]])
                sp.dma_start(gate1[:, :, r], row).then_inc(gate1_in, 16)
            load_x(0)
            sp.wait_ge(sq_summed, 1)
            load_x(1)
            load_x(2)
            load_o(1)
            sp.dma_start(gate2[:].rearrange("p r n -> p (r n)"), bass.AP(gate_rows.tensor, 2 * D, [[0, 128], [1, 2 * D]])
                         ).then_inc(gate2_in, 16)
            for n in range(2, OS):
                sp.wait_ge(o_summed, TT * (n - 1))
                load_o(n)
            load(0, 0)
            sp.wait_ge(o_summed, TT * OS)
            load(0, 1)
            sp.wait_ge(gated, TT * OS)
            load(0, 2)
            later(0)
            with sp.Fori(1, PAIRS - 1) as j:
                later(j)
            for i in range(3):
                used(PAIRS - 1, i)
                load(PAIRS - 1, i + 3)
            for t in range(TT):
                waits_added(sp, PAIRS - 1, 2 * t)
                waits_added(sp, PAIRS - 1, 2 * t + 1)
                dst = y_prompt[0, 128 * t:128 * t + 128] if t < 4 else y_sample[0, 128 * (t - 4):128 * (t - 3)]
                sp.dma_start(dst, x1[:, t]).then_inc(y_stored, 16)
            sp.wait_ge(y_stored, 16 * TT)

        def split_hi(act, j, i):
            act.wait_ge(w_in[i % 3], 16 * (2 * j + i // 3) + 16)
            act.activation(w_hi[:, i % 3], w_raw[:, i % 3], ACT.Copy).then_inc(w_split_hi, 1)

        def split_lo(dve, j, i):
            dve.wait_ge(w_split_hi, 6 * j + i + 1)
            dve.tensor_tensor(w_lo[:, i % 3], w_raw[:, i % 3], w_hi[:, i % 3].bitcast(F32), ALU.subtract
                              ).then_inc(w_ready, 1)

        def silu(act, j, n):
            c = n % NCH
            act.wait_ge(g_summed, 6 * j + n + 1)
            if n == 0:
                if isinstance(j, int) and j == 0:
                    act.wait_ge(x1_added, TT * OS)
                waits_added(act, j, -2)
                waits_added(act, j, -1)
            if n >= 3:
                act.wait_ge(product, 6 * j + n - 2)
            act.activation(scratch[:, c], banks[:, c], ACT.Silu).then_inc(silu_ready, 1)

        def pair_act(act, j, last):
            first = isinstance(j, int) and j == 0
            for i, (kind, f) in enumerate(TILES):
                if not (last and i >= 4) and not (first and i == 0):
                    split_hi(act, j + (i + 2) // 6, (i + 2) % 6)
                for c in range(NCH):
                    n = 3 * f + c
                    if kind == GATE and not (first and n < 2):
                        silu(act, j, n)
                    if kind == UP:
                        act.wait_ge(product, 6 * j + n + 1)
                        act.activation(ff_hi[:, f, CH * c:CH * c + CH], ff_raw[:, f, CH * c:CH * c + CH], ACT.Copy
                                       ).then_inc(ff_hi_s, 1)

        @block.scalar
        def _(act):
            def split_o(n):
                act.wait_ge(wo_in[n % 2], 16 * ((n + 1) // 2))
                act.activation(wo_hi[n % 2][:], wo_raw[n % 2][:], ACT.Copy).then_inc(wo_hi_s, 1)

            def scale_f(m):
                act.wait_ge(o_summed, m + 1)
                if m >= 4:
                    act.wait_ge(x1_added, m - 3)
                act.activation(mix_ring[:, m % 4], banks[:, m % NG, NO:2 * NO], ACT.Copy,
                               scale=mix_rstd[:, 1, TT + m % TT:TT + m % TT + 1]).then_inc(f_scaled, 1)

            def square(t):
                act.wait_ge(x1_added, TT * (OS - 1) + t + 1)
                if t:
                    act.wait_ge(squared, t)
                act.activation(banks[:, 6:8], x1[:, t].rearrange("p (b n) -> p b n", b=2), ACT.Square,
                               accum_out=stat[:, 0, t:t + 1]).then_inc(squared, 1)

            def squares_at(m):
                return {TT * OS - 8: (0, 1), TT * OS - 7: (2, 3), TT * OS - 6: (4,), TT * OS - 5: (5,),
                        TT * OS - 4: (6, 7)}.get(m, ())

            def root(c):
                act.wait_ge(squared, 4 * c + 4)
                act.activation(stat[:, 0, 4 * c:4 * c + 4], stat[:, 0, 4 * c:4 * c + 4], ACT.Sqrt,
                               scale=1.0 / D, bias=eps_t[:]).then_inc(rooted, 1)

            def norm(c):
                act.wait_ge(rstd, c + 1)
                if c:
                    act.wait_ge(turned, KT * c)
                t = 4 * c + 3
                act.activation(xn[:, 3], x1[:, t], ACT.Copy, scale=stat[:, 1, t:t + 1]).then_inc(xn_act, 1)

            def modulate(n):
                c, k = divmod(n, KT)
                r = REQ[c]
                act.wait_ge(turned, n + 1)
                if n >= 2:
                    waits_split(act, n - 2)
                act.activation(t_ring[:, n % 2], banks[:, TB + n % 2], ACT.Identity, scale=coef[:, 1, k, r:r + 1],
                               bias=mod[:, 3 * KT + k, r:r + 1]).then_inc(t_ready, 1)
            act.wait_ge(sq_summed, 1)
            act.activation(mix_rstd[:, 0, 0:TT], banks[:, 1, 0:2 * TT:2], ACT.Sqrt, scale=1.0 / D_FOURIER, bias=eps_t[:])
            act.activation(mix_rstd[:, 0, TT:2 * TT], banks[:, TB, 0:2 * TT:2], ACT.Sqrt, scale=1.0 / D_FOURIER, bias=eps_t[:]
                           ).then_inc(mix_rooted, 1)
            act.wait_ge(mix_rstd_ready, 1)
            for m in range(TT * OS - 4):
                scale_f(m)
                if m == 7:
                    split_o(1)
                if m % TT == 0 and m and m // TT + 1 < OS:
                    split_o(m // TT + 1)
                for t in squares_at(m):
                    square(t)
                if m == TT * OS - 7:
                    root(0)
            norm(0)
            for i in range(4):
                scale_f(TT * OS - 4 + i)
                if i == 1:
                    split_hi(act, 0, 0)
                modulate(2 * i)
                modulate(2 * i + 1)
                for t in squares_at(TT * OS - 4 + i):
                    square(t)
                if i == 0:
                    root(1)
            norm(1)
            square(8)
            square(9)
            for k in range(KT):
                modulate(KT + k)
                if k in (1, 3):
                    square(10 + k // 2)
                if k == 3:
                    root(2)
            norm(2)
            split_hi(act, 0, 1)
            for c in range(NCH):
                if c < 2:
                    silu(act, 0, c)
                if c == 0:
                    for k in range(KT):
                        modulate(2 * KT + k)
                    split_hi(act, 0, 2)
            pair_act(act, 0, False)
            with act.Fori(1, PAIRS - 1) as j:
                pair_act(act, j, False)
            pair_act(act, PAIRS - 1, True)

        def pair_dve(dve, j, last):
            first = isinstance(j, int) and j == 0
            for i, (kind, f) in enumerate(TILES):
                if i < 5 and not (last and i == 4) and not (first and i == 0):
                    split_lo(dve, j + (i + 2) // 6, (i + 2) % 6)
                if kind == UP:
                    for c in range(NCH):
                        n = 3 * f + c
                        part = ff_raw[:, f, CH * c:CH * c + CH]
                        dve.wait_ge(u_summed, 6 * j + n + 1)
                        dve.wait_ge(silu_ready, 6 * j + n + 1)
                        dve.tensor_tensor(part, banks[:, 3 + c], scratch[:, c], ALU.mult).then_inc(product, 1)
                        dve.wait_ge(ff_hi_s, 6 * j + n + 1)
                        dve.tensor_tensor(ff_lo[:, f, CH * c:CH * c + CH], part,
                                          ff_hi[:, f, CH * c:CH * c + CH].bitcast(F32), ALU.subtract
                                          ).then_inc(ff_ready, 1)
                if i == 5:
                    if first:
                        dve.wait_ge(gate2_in, 16)
                    for n in range(DG):
                        t, half = divmod(n, 2)
                        dve.wait_ge(d_summed, DG * j + n + 1)
                        if n >= 3:
                            waits_added(dve, j, n - 3)
                        dve.tensor_tensor(scratch[:, n % 3], banks[:, (6 + n) % 8],
                                          gate2[:, REQ[t // 4], 512 * half:512 * half + 512], ALU.mult
                                          ).then_inc(d_gated, 1)
                        if on_dve(n):
                            part = x1[:, t, 512 * half:512 * half + 512]
                            dve.wait_ge(d_gated, DG * j + n + 1)
                            dve.tensor_tensor(part, part, scratch[:, n % 3], ALU.add).then_inc(d_added_dve, 1)
                    if not last:
                        split_lo(dve, j + 1, 1)

        @block.vector
        def _(dve):
            def split_o(n):
                dve.wait_ge(wo_hi_s, n)
                dve.tensor_tensor(wo_lo[n % 2][:], wo_raw[n % 2][:], wo_hi[n % 2][:].bitcast(F32), ALU.subtract
                                  ).then_inc(wo_ready, 1)

            def gate_mix(m):
                n, t = divmod(m, TT)
                part = mix_ring[:, m % 4]
                dve.wait_ge(f_scaled, m + 1)
                dve.scalar_tensor_tensor(part, banks[:, m % NG, 0:NO], mix_rstd[:, 1, t:t + 1], part, ALU.mult, ALU.add
                                         ).then_inc(a_scaled, 1)
                dve.wait_ge(a_scaled, m + 1)
                dve.tensor_tensor(part, part, gate1[:, n, REQ[t // 4]], ALU.mult).then_inc(gated, 1)

            def norm(c):
                dve.wait_ge(rooted, c + 1)
                dve.reciprocal(stat[:, 1, 4 * c:4 * c + 4], stat[:, 0, 4 * c:4 * c + 4]).then_inc(rstd, 1)
                dve.wait_ge(rstd, c + 1)
                if c:
                    dve.wait_ge(turned, KT * c)
                for i in range(3):
                    dve.tensor_scalar(xn[:, i], x1[:, 4 * c + i], stat[:, 1, 4 * c + i:4 * c + i + 1], None, ALU.mult
                                      ).then_inc(xn_dve, 1)

            def split(n):
                c, k = divmod(n, KT)
                dve.wait_ge(t_ready, n + 1)
                hi, lo = (h[:, k, CH * c:CH * c + CH] for h in (h_hi, h_lo))
                dve.tensor_copy(hi, t_ring[:, n % 2]).then_inc(hi_ready, 1)
                if not on_pool(n):
                    dve.wait_ge(hi_ready, n + 1)
                    dve.tensor_tensor(lo, t_ring[:, n % 2], hi.bitcast(F32), ALU.subtract).then_inc(split_dve, 1)
            dve.wait_ge(mix_rooted, 1)
            dve.reciprocal(mix_rstd[:, 1], mix_rstd[:, 0]).then_inc(mix_rstd_ready, 1)
            dve.wait_ge(mix_rstd_ready, 1)
            dve.wait_ge(gate1_in, 32)
            for m in range(TT * OS - 4):
                gate_mix(m)
                if m == 7:
                    split_o(1)
                if m % TT == 1 and m > TT and m // TT + 1 < OS:
                    split_o(m // TT + 1)
            norm(0)
            for i in range(4):
                gate_mix(TT * OS - 4 + i)
                if i == 2:
                    split_lo(dve, 0, 0)
                split(2 * i)
                split(2 * i + 1)
            norm(1)
            for k in range(KT):
                split(KT + k)
            norm(2)
            split_lo(dve, 0, 1)
            for k in range(KT):
                split(2 * KT + k)
            split_lo(dve, 0, 2)
            pair_dve(dve, 0, False)
            with dve.Fori(1, PAIRS - 1) as j:
                pair_dve(dve, j, False)
            pair_dve(dve, PAIRS - 1, True)

        @block.gpsimd
        def _(pool):
            def add_mix(m):
                n, t = divmod(m, TT)
                if n == 0 and t % 4 == 0:
                    pool.wait_ge(x_in[t // 4], 16)
                pool.wait_ge(gated, m + 1)
                part = x1[:, t, NO * n:NO * n + NO]
                pool.tensor_tensor(part, part, mix_ring[:, m % 4], ALU.add).then_inc(x1_added, 1)

            def split(n):
                c, k = divmod(n, KT)
                hi, lo = (h[:, k, CH * c:CH * c + CH] for h in (h_hi, h_lo))
                pool.wait_ge(hi_ready, n + 1)
                pool.tensor_tensor(lo, t_ring[:, n % 2], hi.bitcast(F32), ALU.subtract).then_inc(split_pool, 1)
            for m in range(TT * OS - 4):
                add_mix(m)
            for i in range(4):
                add_mix(TT * OS - 4 + i)
                split(2 * i + 1)
            with pool.Fori(0, PAIRS) as j:
                for n in range(DG):
                    if on_dve(n):
                        continue
                    t, half = divmod(n, 2)
                    pool.wait_ge(d_gated, DG * j + n + 1)
                    part = x1[:, t, 512 * half:512 * half + 512]
                    pool.tensor_tensor(part, part, scratch[:, n % 3], ALU.add).then_inc(d_added, 1)

        @block.tensor
        def _(pe):
            for t in range(TT):
                last = pe.matmul(banks[:, TB, 2 * t:2 * t + 2], sq_sum[:, 1, 128 * t:128 * t + 128],
                                 ones_all[:, 0:2].bitcast(F32), start=True, stop=True)
            last.then_inc(sq_summed, 1)

            def mix_out(m):
                n, t = divmod(m, TT)
                if t == 0 and n:
                    pe.wait_ge(wo_ready, n)
                if m >= NG:
                    pe.wait_ge(gated, m - NG + 1)
                elif m == 1:
                    pe.wait_ge(mix_rooted, 1)
                for half in range(2):
                    for i in range(FT):
                        k, row = FT * half + i, FT * (1 - half) + i
                        last = mm3(pe, banks[:, m % NG, NO * half:NO * half + NO],
                                   (h_hi[:, k, 128 * t:128 * t + 128], h_lo[:, k, 128 * t:128 * t + 128]),
                                   (wo_hi[n % 2][:, row], wo_lo[n % 2][:, row]), i == 0, i == FT - 1)
                last.then_inc(o_summed, 1)

            def turn(n):
                c, k = divmod(n, KT)
                pe.wait_ge(xn_dve, 3 * c + 3)
                pe.wait_ge(xn_act, c + 1)
                if n >= 2:
                    pe.wait_ge(t_ready, n - 1)
                elif n == 0:
                    pe.wait_ge(mix_rooted, 1)
                for i in range(4):
                    last = pe.transpose(banks[:, TB + n % 2, 128 * i:128 * i + 128], xn[:, i, 128 * k:128 * k + 128], ident[:])
                last.then_inc(turned, 1)

            def gate_step(k, c):
                if k == 0:
                    pe.wait_ge(w_ready, 1)
                    waits_split(pe, KT * c + KT - 2)
                    waits_split(pe, KT * c + KT - 1)
                    pe.wait_ge(gated, TT * OS)
                w = [part[:, 0].rearrange("p (k n) -> p k n", n=128) for part in (w_hi, w_lo)]
                last = mm3(pe, banks[:, c], (w[0][:, k], w[1][:, k]),
                           (h_hi[:, k, CH * c:CH * c + CH], h_lo[:, k, CH * c:CH * c + CH]), k == 0, k == KT - 1)
                if k == KT - 1:
                    last.then_inc(g_summed, 1)
            for m in range(TT * OS - 4):
                mix_out(m)
            for i in range(4):
                mix_out(TT * OS - 4 + i)
                turn(2 * i)
                turn(2 * i + 1)
            for c in range(1, NCH):
                for k in range(KT):
                    gate_step(k, c - 1)
                    turn(KT * c + k)
            waits_split(pe, KT * NCH - 1)

            def pair(j):
                first = isinstance(j, int) and j == 0
                for i, (kind, f) in enumerate(TILES[:4]):
                    w = [part[:, i % 3].rearrange("p (k n) -> p k n", n=128) for part in (w_hi, w_lo)]
                    pe.wait_ge(w_ready, 6 * j + i + 1)
                    for c in range(2 if first and i == 0 else 0, NCH):
                        if f == 0 and first:
                            if kind == UP:
                                pe.wait_ge(t_ready, NCH * KT)
                        elif f == 0:
                            pe.wait_ge(d_gated, DG * j - 5 + 3 * kind + c)
                        elif kind == GATE:
                            pe.wait_ge(silu_ready, 6 * j + c + 1)
                        else:
                            pe.wait_ge(product, 6 * j + c + 1)
                        for k in range(KT):
                            last = mm3(pe, banks[:, 3 * kind + c], (w[0][:, k], w[1][:, k]),
                                       (h_hi[:, k, CH * c:CH * c + CH], h_lo[:, k, CH * c:CH * c + CH]), k == 0, k == KT - 1)
                        last.then_inc((g_summed, u_summed)[kind], 1)
                pe.wait_ge(w_ready, 6 * j + 6)
                for n in range(DG):
                    t, half = divmod(n, 2)
                    if t % 4 == 0 and half == 0:
                        pe.wait_ge(ff_ready, 6 * j + 3 + t // 4 + 1)
                    if n >= 8:
                        pe.wait_ge(d_gated, DG * j + n - 7)
                    elif n >= 5:
                        pe.wait_ge(product, 6 * j + 6)
                    elif n >= 2:
                        pe.wait_ge(silu_ready, 6 * j + 6)
                    elif first:
                        pe.wait_ge(squared, TT)
                    for f in range(2):
                        last = mm3(pe, banks[:, (6 + n) % 8],
                                   (ff_hi[:, f, 128 * t:128 * t + 128], ff_lo[:, f, 128 * t:128 * t + 128]),
                                   [part[:, 1 + f, 512 * half:512 * half + 512] for part in (w_hi, w_lo)], f == 0, f == 1)
                    last.then_inc(d_summed, 1)
            pair(0)
            with pe.Fori(1, PAIRS) as j:
                pair(j)


def _inputs(inputs):
    f = lambda n: np.ascontiguousarray(inputs[n])
    g_q, g_k = f("g_q")[0], f("g_k")[0]
    c = np.concatenate([f("c_prompt"), f("c_sample")]).reshape(16, 128)
    rows = [c, f("g_attn").reshape(8, 128), f("g_ffn").reshape(8, 128), f("g_fout").reshape(4, 128),
            f("g_aout").reshape(4, 128), np.concatenate([g_q, g_q])[None], np.concatenate([g_k, g_k])[None],
            f("b_ada").reshape(48, 128)]
    rp = f("rpb")[0]
    pad = np.zeros((N_HEADS // 2, RP_ROWS, 2, RP_COLS), np.float32)
    pad[:, 4:4 + 2 * WIN_ROWS - 1, :, 16:16 + 2 * WIN_COLS - 1] = rp.reshape(
        N_HEADS // 2, 2, 2 * WIN_ROWS - 1, 2 * WIN_COLS - 1).transpose(0, 2, 1, 3)
    return {
        "x_prompt": f("x_prompt")[0], "x_sample": f("x_sample")[0], "b_ada": f("b_ada")[0], "w_ada": f("w_ada")[0],
        "vec_rows": np.concatenate(rows), "w_in": f("w_in")[0], "w_fmix": f("w_fmix")[0], "rpb_pad": pad.reshape(-1),
        "masks": _masks(), "dft_c": _dft_channels(), "dft_t1": _dft_tokens(T_SAMPLE), "dft_t0": _dft_tokens(T_PROMPT),
        "w_o": f("w_o")[0], "w_gate": f("w_gate")[0], "w_up": f("w_up")[0], "w_down": f("w_down")[0],
    }


def _masks():
    out = np.full((128, NB, MASK_COLS), MASKED, np.float32)
    for b in range(NB):
        at = 0
        for c in range(NCH):
            rows = 8 if c == 0 else 16
            for qi in range(QROWS):
                i = qi + (QROWS if c == 2 else 0)
                r0 = min(max(i - WIN_ROWS // 2, 0), rows - WIN_ROWS)
                for qc in range(QCOLS):
                    col = QCOLS * b + qc
                    c0 = min(max(col - WIN_COLS // 2, 0), GRID_W - WIN_COLS)
                    for r in range(r0, r0 + WIN_ROWS):
                        k = at + (r - KEY_ROW0[c]) * KCOLS + c0 - KEY_COL[b]
                        out[qi * QCOLS + QCOLS - 1 - qc, b, k:k + WIN_COLS] = 0.0
            at += KEY_ROWS[c] * KCOLS
    return out.reshape(128, NB * MASK_COLS)


def _dft_channels():
    n = np.arange(128)
    a = 2 * np.pi * ((n[:, None] * n) % 128) / 128
    return np.concatenate([np.cos(a), np.sin(a)], 1).astype(np.float32) / np.float32(128 ** 0.5)


def _dft_tokens(t):
    n = np.arange(t // 2)
    a = 2 * np.pi * ((n[:, None] * n) % t) / t
    return (np.stack([np.cos(a), np.sin(a)]) / t ** 0.5).astype(np.float32)


def kernel(**inputs):
    import concourse.bacc as bacc
    from concourse.bass_utils import run_bass_kernel_spmd

    nc = bacc.Bacc("TRN2", target_bir_lowering=False, num_devices=1)
    arrays, args = {}, {}
    for name, a in _inputs(inputs).items():
        arrays[f"in_{name}"] = a
        args[name] = nc.dram_tensor(f"in_{name}", a.shape, mybir.dt.from_np(a.dtype), kind="ExternalInput").ap()
    args["u_scratch"] = nc.dram_tensor("u_scratch", (D_FOURIER, T), F32).ap()
    args["gate_rows"] = nc.dram_tensor("gate_rows", (2, 2, D), F32).ap()
    for name, t in (("y_prompt", T_PROMPT), ("y_sample", T_SAMPLE)):
        args[name] = nc.dram_tensor(name, (1, t, D), F32, kind="ExternalOutput").ap()
    layer(nc, **args)
    r = run_bass_kernel_spmd(nc, [arrays], core_ids=[0])
    return r.results[0]["y_prompt"], r.results[0]["y_sample"]
```
